# Optimizing a Trainium2 kernel written in Bass

```python
import math
import jax, jax.numpy as jnp
from jax import lax
import numpy as np

D_MODEL = 1024
BATCH = 1
SEQ = 256
DEPTH = 2
DEC_BATCH = 8
DEC_SEQ = 1
PAST_LEN = 1024
PAGE_SIZE = 128

GM_GROUPS = 4
GM_GROUP_DIM = D_MODEL // 16
W_A = GM_GROUPS * GM_GROUP_DIM
GM_CHUNK = 128
MLA_HEADS = 4
MLA_NOPE = 64
MLA_ROPE = 32
MLA_V = 64
MLA_Q_RANK = D_MODEL // 4
MLA_KV_RANK = D_MODEL // 8
W_B = MLA_HEADS * MLA_V
MLA_SCALE = (MLA_NOPE + MLA_ROPE) ** -0.5
ROPE_THETA = 10000.0
Q_BLOCK = 128
GDN_HEADS = 4
GDN_DK = 64
GDN_DV = 64
W_C = GDN_HEADS * GDN_DV
QKV_DIM = GDN_HEADS * (2 * GDN_DK + GDN_DV)
CONV_W = 4
GDN_CHUNK = 64
MEM_TOKENS = 256
MEM_HEADS = 4
MEM_DIM = 64
W_M = MEM_HEADS * MEM_DIM
N_BRANCH = 4
BR_WIDTH = 256
N_GROUPS = 4
EXPERTS_PER_GROUP = 8
N_EXPERTS = N_GROUPS * EXPERTS_PER_GROUP
TOP_K = 2
D_EXPERT = D_MODEL // 4
EPS = 1e-6

IN_SPLITS = (2 * W_A, MLA_Q_RANK, MLA_KV_RANK, MLA_ROPE, QKV_DIM, W_C, GDN_HEADS, GDN_HEADS, W_M, N_BRANCH * D_MODEL)
IN_DIM = sum(IN_SPLITS)
IN_OFFSETS = tuple(int(o) for o in np.cumsum(IN_SPLITS)[:-1])

kernel_name = 'hybrid_gmlp_mla_gdn_mem_hiermoe_step'

def rmsnorm(x, g):
    xf = x.astype(jnp.float32)
    y = xf * lax.rsqrt(jnp.mean(xf * xf, axis=-1, keepdims=True) + EPS)
    return (y * g.astype(jnp.float32)).astype(x.dtype)

def l2norm(x):
    xf = x.astype(jnp.float32)
    return xf * lax.rsqrt(jnp.sum(xf * xf, axis=-1, keepdims=True) + EPS)

def rope(x, pos):
    half = x.shape[-1] // 2
    inv = ROPE_THETA ** (-jnp.arange(half, dtype=jnp.float32) / half)
    ang = pos.astype(jnp.float32)[:, None] * inv[None, :]
    shape = (1, pos.shape[0]) + (1,) * (x.ndim - 3) + (half,)
    cos = jnp.cos(ang).reshape(shape)
    sin = jnp.sin(ang).reshape(shape)
    xf = x.astype(jnp.float32)
    x1, x2 = xf[..., :half], xf[..., half:]
    return jnp.concatenate([x1 * cos - x2 * sin, x1 * sin + x2 * cos], axis=-1).astype(x.dtype)

def causal_conv(x, buf, w):
    xp = jnp.concatenate([buf.astype(x.dtype), x], axis=1)
    y = lax.conv_general_dilated(xp, w[:, None, :].astype(x.dtype), window_strides=(1,), padding='VALID',
                                 dimension_numbers=('NWC', 'WIO', 'NWC'), feature_group_count=x.shape[-1])
    return y, xp[:, -(CONV_W - 1):]

def gmlp_spatial(v, ws, b):
    n, t, _ = v.shape
    nc = -(-t // GM_CHUNK)
    pad = nc * GM_CHUNK - t
    vp = jnp.pad(v, ((0, 0), (0, pad), (0, 0))).reshape(n, nc, GM_CHUNK, GM_GROUPS, GM_GROUP_DIM)
    w = jnp.where(jnp.tril(jnp.ones((GM_CHUNK, GM_CHUNK), bool)), ws, 0)
    s = jnp.einsum('gij,ncjgd->ncigd', w, vp) + b.T[None, None, :, :, None]
    return s.reshape(n, nc * GM_CHUNK, W_A)[:, :t]

def mla_attention(qn, qr, kn, kr, ckv, w_uv, q_pos, k_pos):
    n, tq, h, _ = qn.shape
    qb = min(Q_BLOCK, tq)
    nb = -(-tq // qb)
    pad = nb * qb - tq
    qn = jnp.pad(qn, ((0, 0), (0, pad), (0, 0), (0, 0)))
    qr = jnp.pad(qr, ((0, 0), (0, pad), (0, 0), (0, 0)))
    q_pos = jnp.pad(q_pos, (0, pad), mode='edge')

    def to_blocks(a):
        return jnp.moveaxis(a.reshape((n, nb, qb) + a.shape[2:]), 1, 0)

    def one_block(args):
        qn_b, qr_b, pos_b = args
        s = jnp.einsum('nthe,nshe->nhts', qn_b, kn) + jnp.einsum('nthe,nse->nhts', qr_b, kr)
        s = s.astype(jnp.float32) * MLA_SCALE
        s = jnp.where((k_pos[None, :] <= pos_b[:, None])[None, None], s, -jnp.inf)
        p = jax.nn.softmax(s, axis=-1).astype(ckv.dtype)
        return jnp.einsum('nhts,nsr->nthr', p, ckv)

    lat = lax.map(one_block, (to_blocks(qn), to_blocks(qr), q_pos.reshape(nb, qb)))
    lat = jnp.moveaxis(lat, 0, 1).reshape(n, nb * qb, h, ckv.shape[-1])[:, :tq]
    return jnp.einsum('nthr,rhe->nthe', lat, w_uv)

def mem_attention(q, k, v):
    s = jnp.einsum('nthe,nshe->nhts', q, k).astype(jnp.float32) * MEM_DIM ** -0.5
    p = jax.nn.softmax(s, axis=-1).astype(v.dtype)
    return jnp.einsum('nhts,nshe->nthe', p, v)

def gdn_chunked(q, k, v, beta, g, s0):
    n, t, h, _ = q.shape
    c = min(GDN_CHUNK, t)
    nc = -(-t // c)
    pad = nc * c - t

    def blk4(a):
        a = jnp.pad(a, ((0, 0), (0, pad), (0, 0), (0, 0)))
        return a.reshape(n, nc, c, a.shape[2], a.shape[3]).transpose(1, 0, 3, 2, 4)

    def blk3(a):
        a = jnp.pad(a, ((0, 0), (0, pad), (0, 0)))
        return a.reshape(n, nc, c, a.shape[2]).transpose(1, 0, 3, 2)

    incl = jnp.tril(jnp.ones((c, c), bool))
    strict = jnp.tril(jnp.ones((c, c), bool), k=-1)
    eye = jnp.eye(c, dtype=jnp.float32)

    def step(s, xs):
        qc, kc, vc, bc, gc = xs
        gcum = jnp.cumsum(gc, axis=-1)
        decay = jnp.exp(jnp.where(incl, gcum[..., :, None] - gcum[..., None, :], -jnp.inf))
        a = jnp.where(strict, bc[..., :, None] * jnp.einsum('nhtd,nhsd->nhts', kc, kc) * decay, 0.0)
        lmat = a + eye
        u_v = lax.linalg.triangular_solve(lmat, bc[..., None] * vc, left_side=True, lower=True, unit_diagonal=True)
        w_k = lax.linalg.triangular_solve(lmat, (bc * jnp.exp(gcum))[..., None] * kc,
                                          left_side=True, lower=True, unit_diagonal=True)
        u = u_v - jnp.einsum('nhck,nhvk->nhcv', w_k, s)
        qk = jnp.einsum('nhtd,nhsd->nhts', qc, kc) * decay
        o = jnp.exp(gcum)[..., None] * jnp.einsum('nhtk,nhvk->nhtv', qc, s) + jnp.einsum('nhts,nhsv->nhtv', qk, u)
        g_last = gcum[..., -1:]
        s_new = jnp.exp(g_last)[..., None] * s + jnp.einsum('nhs,nhsv,nhsk->nhvk', jnp.exp(g_last - gcum), u, kc)
        return s_new, o

    s_fin, o = lax.scan(step, s0, (blk4(q), blk4(k), blk4(v), blk3(beta), blk3(g)))
    o = o.transpose(1, 0, 3, 2, 4).reshape(n, nc * c, h, v.shape[-1])[:, :t]
    return o, s_fin

def hier_moe(x, lp):
    n, t, d = x.shape
    m = n * t
    xf = x.reshape(m, d)
    pg = jax.nn.softmax((xf @ lp['moe_wg']).astype(jnp.float32) + lp['moe_bg'].astype(jnp.float32), axis=-1)
    g_w, g_idx = lax.top_k(pg, 1)
    le = ((xf @ lp['moe_we']).astype(jnp.float32) + lp['moe_be'].astype(jnp.float32)).reshape(m, N_GROUPS, EXPERTS_PER_GROUP)
    le_sel = jnp.take_along_axis(le, jnp.broadcast_to(g_idx[:, :, None], (m, 1, EXPERTS_PER_GROUP)), axis=1)[:, 0]
    e_w, e_idx = lax.top_k(jax.nn.softmax(le_sel, axis=-1), TOP_K)
    e_w = e_w / jnp.sum(e_w, axis=-1, keepdims=True) * g_w
    e_glob = g_idx * EXPERTS_PER_GROUP + e_idx
    comb = jnp.einsum('mk,mke->me', e_w, jax.nn.one_hot(e_glob, N_EXPERTS, dtype=jnp.float32)).astype(x.dtype)
    act = jax.nn.silu(jnp.einsum('md,edf->mef', xf, lp['moe_w_gate'])) * jnp.einsum('md,edf->mef', xf, lp['moe_w_up'])
    y = jnp.einsum('mef,efd->md', act * comb[:, :, None], lp['moe_w_down'])
    return y.reshape(n, t, d)

def mem_kv(mem, lp):
    n, m, _ = mem.shape
    kv = rmsnorm(mem, lp['mem_norm_g']) @ lp['mem_w_kv']
    k, v = jnp.split(kv, 2, axis=-1)
    k = rmsnorm(k.reshape(n, m, MEM_HEADS, MEM_DIM), lp['mem_kn_g'])
    return k, v.reshape(n, m, MEM_HEADS, MEM_DIM)

def block(x, pos, lp, mla_past, gdn_s0, conv0, mem_k, mem_v):
    n, t, _ = x.shape
    h = rmsnorm(x, lp['norm1_g'])
    z = h @ lp['w_in']
    (a_raw, cq_raw, ckv_raw, kr_raw, qkv_raw, z_gate, b_raw, alpha_raw, mq_raw, gate_raw) = jnp.split(z, IN_OFFSETS, axis=-1)

    u, v = jnp.split(jax.nn.gelu(a_raw, approximate=False), 2, axis=-1)
    v = rmsnorm(v, lp['gm_norm_g'])
    a_out = u * gmlp_spatial(v, lp['gm_ws'], lp['gm_b'])

    cq = rmsnorm(cq_raw, lp['mla_cq_g'])
    q = jnp.einsum('ntr,rhe->nthe', cq, lp['mla_w_uq'])
    qn = rmsnorm(q[..., :MLA_NOPE], lp['mla_qn_g'])
    qr = rope(rmsnorm(q[..., MLA_NOPE:], lp['mla_qr_g']), pos)
    ckv = rmsnorm(ckv_raw, lp['mla_ckv_g'])
    kr = rope(rmsnorm(kr_raw, lp['mla_kr_g']), pos)
    if mla_past is None:
        ckv_all, kr_all, k_pos = ckv, kr, pos
    else:
        ckv_all = jnp.concatenate([mla_past[0].astype(ckv.dtype), ckv], axis=1)
        kr_all = jnp.concatenate([mla_past[1].astype(kr.dtype), kr], axis=1)
        k_pos = jnp.arange(ckv_all.shape[1], dtype=jnp.int32)
    kn = rmsnorm(jnp.einsum('nsr,rhe->nshe', ckv_all, lp['mla_w_uk']), lp['mla_kn_g'])
    b_out = mla_attention(qn, qr, kn, kr_all, ckv_all, lp['mla_w_uv'], pos, k_pos).reshape(n, t, W_B)

    qkv, conv_new = causal_conv(qkv_raw, conv0, lp['gdn_conv_w'])
    qkv = jax.nn.silu(qkv).astype(jnp.float32)
    gq, gk, gv = jnp.split(qkv, [GDN_HEADS * GDN_DK, 2 * GDN_HEADS * GDN_DK], axis=-1)
    gq = l2norm(gq.reshape(n, t, GDN_HEADS, GDN_DK)) * GDN_DK ** -0.5
    gk = l2norm(gk.reshape(n, t, GDN_HEADS, GDN_DK))
    gv = gv.reshape(n, t, GDN_HEADS, GDN_DV)
    beta = jax.nn.sigmoid(b_raw.astype(jnp.float32))
    gdec = -jnp.exp(lp['gdn_a_log'].astype(jnp.float32)) * jax.nn.softplus(
        alpha_raw.astype(jnp.float32) + lp['gdn_dt_bias'].astype(jnp.float32))
    o, s_new = gdn_chunked(gq, gk, gv, beta, gdec, gdn_s0.astype(jnp.float32))
    o = rmsnorm(o.astype(x.dtype), lp['gdn_out_g']) * jax.nn.silu(z_gate.reshape(n, t, GDN_HEADS, GDN_DV))
    c_out = o.reshape(n, t, W_C)

    mq = rmsnorm(mq_raw.reshape(n, t, MEM_HEADS, MEM_DIM), lp['mem_qn_g'])
    m_out = mem_attention(mq, mem_k.astype(mq.dtype), mem_v.astype(mq.dtype)).reshape(n, t, W_M)

    branches = jnp.stack([a_out, b_out, c_out, m_out], axis=2)
    proj = jnp.einsum('ntbw,bwd->ntbd', branches, lp['w_branch'])
    gates = jax.nn.sigmoid(gate_raw.reshape(n, t, N_BRANCH, D_MODEL))
    x = x + jnp.einsum('ntbd,ntbd->ntd', gates, proj) @ lp['w_out']

    x = x + hier_moe(rmsnorm(x, lp['norm2_g']), lp)
    return x, ckv, kr, s_new.astype(x.dtype), conv_new, v

def setup_inputs(seed: int = 0) -> dict:
    key = jax.random.key(seed)
    ks = iter(jax.random.split(key, 64))

    def nrm(shape, scale=1.0):
        return jax.random.normal(next(ks), shape, jnp.float32) * scale

    def gain(shape):
        return 1.0 + nrm(shape, 0.02)

    n_pages = PAST_LEN // PAGE_SIZE
    n_used = DEC_BATCH * n_pages
    n_pool = n_used + n_used // 4
    page_table = jax.random.permutation(next(ks), n_pool)[:n_used].reshape(DEC_BATCH, n_pages).astype(jnp.int32)
    dt = jnp.exp(jax.random.uniform(next(ks), (DEPTH, GDN_HEADS), jnp.float32, math.log(1e-3), math.log(1e-1)))
    gm_row_scale = (jnp.arange(1, GM_CHUNK + 1, dtype=jnp.float32) ** -0.5)[:, None]
    return {
        'x_prompt': nrm((BATCH, SEQ, D_MODEL)),
        'mem_prompt': nrm((BATCH, MEM_TOKENS, D_MODEL)),
        'x_sample': nrm((DEC_BATCH, DEC_SEQ, D_MODEL)),
        'cache_mla_ckv': nrm((DEPTH, n_pool, PAGE_SIZE, MLA_KV_RANK)),
        'cache_mla_kr': nrm((DEPTH, n_pool, PAGE_SIZE, MLA_ROPE)),
        'cache_mem_k': nrm((DEPTH, DEC_BATCH, MEM_TOKENS, MEM_HEADS, MEM_DIM)),
        'cache_mem_v': nrm((DEPTH, DEC_BATCH, MEM_TOKENS, MEM_HEADS, MEM_DIM)),
        'state_gdn': nrm((DEPTH, DEC_BATCH, GDN_HEADS, GDN_DV, GDN_DK), 0.1),
        'state_conv': nrm((DEPTH, DEC_BATCH, CONV_W - 1, QKV_DIM)),
        'page_table': page_table,
        'norm1_g': gain((DEPTH, D_MODEL)),
        'w_in': nrm((DEPTH, D_MODEL, IN_DIM), D_MODEL ** -0.5),
        'gm_norm_g': gain((DEPTH, W_A)),
        'gm_ws': nrm((DEPTH, GM_GROUPS, GM_CHUNK, GM_CHUNK)) * gm_row_scale,
        'gm_b': nrm((DEPTH, GM_GROUPS, GM_CHUNK), 0.02),
        'mla_cq_g': gain((DEPTH, MLA_Q_RANK)),
        'mla_w_uq': nrm((DEPTH, MLA_Q_RANK, MLA_HEADS, MLA_NOPE + MLA_ROPE), MLA_Q_RANK ** -0.5),
        'mla_qn_g': gain((DEPTH, MLA_NOPE)),
        'mla_qr_g': gain((DEPTH, MLA_ROPE)),
        'mla_ckv_g': gain((DEPTH, MLA_KV_RANK)),
        'mla_kr_g': gain((DEPTH, MLA_ROPE)),
        'mla_w_uk': nrm((DEPTH, MLA_KV_RANK, MLA_HEADS, MLA_NOPE), MLA_KV_RANK ** -0.5),
        'mla_kn_g': gain((DEPTH, MLA_NOPE)),
        'mla_w_uv': nrm((DEPTH, MLA_KV_RANK, MLA_HEADS, MLA_V), MLA_KV_RANK ** -0.5),
        'gdn_conv_w': nrm((DEPTH, CONV_W, QKV_DIM), CONV_W ** -0.5),
        'gdn_a_log': jnp.log(jax.random.uniform(next(ks), (DEPTH, GDN_HEADS), jnp.float32, 1.0, 16.0)),
        'gdn_dt_bias': dt + jnp.log(-jnp.expm1(-dt)),
        'gdn_out_g': gain((DEPTH, GDN_DV)),
        'mem_norm_g': gain((DEPTH, D_MODEL)),
        'mem_w_kv': nrm((DEPTH, D_MODEL, 2 * W_M), D_MODEL ** -0.5),
        'mem_qn_g': gain((DEPTH, MEM_DIM)),
        'mem_kn_g': gain((DEPTH, MEM_DIM)),
        'w_branch': nrm((DEPTH, N_BRANCH, BR_WIDTH, D_MODEL), BR_WIDTH ** -0.5),
        'w_out': nrm((DEPTH, D_MODEL, D_MODEL), D_MODEL ** -0.5),
        'norm2_g': gain((DEPTH, D_MODEL)),
        'moe_wg': nrm((DEPTH, D_MODEL, N_GROUPS), D_MODEL ** -0.5),
        'moe_bg': nrm((DEPTH, N_GROUPS), 0.01),
        'moe_we': nrm((DEPTH, D_MODEL, N_EXPERTS), D_MODEL ** -0.5),
        'moe_be': nrm((DEPTH, N_EXPERTS), 0.01),
        'moe_w_gate': nrm((DEPTH, N_EXPERTS, D_MODEL, D_EXPERT), D_MODEL ** -0.5),
        'moe_w_up': nrm((DEPTH, N_EXPERTS, D_MODEL, D_EXPERT), D_MODEL ** -0.5),
        'moe_w_down': nrm((DEPTH, N_EXPERTS, D_EXPERT, D_MODEL), D_EXPERT ** -0.5),
    }

def reference(x_prompt, mem_prompt, x_sample, cache_mla_ckv, cache_mla_kr, cache_mem_k, cache_mem_v,
              state_gdn, state_conv, page_table, norm1_g, w_in, gm_norm_g, gm_ws, gm_b, mla_cq_g, mla_w_uq,
              mla_qn_g, mla_qr_g, mla_ckv_g, mla_kr_g, mla_w_uk, mla_kn_g, mla_w_uv, gdn_conv_w, gdn_a_log,
              gdn_dt_bias, gdn_out_g, mem_norm_g, mem_w_kv, mem_qn_g, mem_kn_g, w_branch, w_out, norm2_g,
              moe_wg, moe_bg, moe_we, moe_be, moe_w_gate, moe_w_up, moe_w_down):
    bp, tp, _ = x_prompt.shape
    bs, ts, _ = x_sample.shape
    n_pages = page_table.shape[1]
    past_len = n_pages * cache_mla_ckv.shape[2]
    pos_p = jnp.arange(tp, dtype=jnp.int32)
    pos_s = past_len + jnp.arange(ts, dtype=jnp.int32)
    xp, xs = x_prompt, x_sample
    rows_p, rows_s = [], []
    for l in range(DEPTH):
        lp = {
            'norm1_g': norm1_g[l], 'w_in': w_in[l], 'gm_norm_g': gm_norm_g[l], 'gm_ws': gm_ws[l], 'gm_b': gm_b[l],
            'mla_cq_g': mla_cq_g[l], 'mla_w_uq': mla_w_uq[l], 'mla_qn_g': mla_qn_g[l], 'mla_qr_g': mla_qr_g[l],
            'mla_ckv_g': mla_ckv_g[l], 'mla_kr_g': mla_kr_g[l], 'mla_w_uk': mla_w_uk[l], 'mla_kn_g': mla_kn_g[l],
            'mla_w_uv': mla_w_uv[l], 'gdn_conv_w': gdn_conv_w[l], 'gdn_a_log': gdn_a_log[l],
            'gdn_dt_bias': gdn_dt_bias[l], 'gdn_out_g': gdn_out_g[l], 'mem_norm_g': mem_norm_g[l],
            'mem_w_kv': mem_w_kv[l], 'mem_qn_g': mem_qn_g[l], 'mem_kn_g': mem_kn_g[l], 'w_branch': w_branch[l],
            'w_out': w_out[l], 'norm2_g': norm2_g[l], 'moe_wg': moe_wg[l], 'moe_bg': moe_bg[l], 'moe_we': moe_we[l],
            'moe_be': moe_be[l], 'moe_w_gate': moe_w_gate[l], 'moe_w_up': moe_w_up[l], 'moe_w_down': moe_w_down[l],
        }
        mk_p, mv_p = mem_kv(mem_prompt, lp)
        zero_s = jnp.zeros((bp, GDN_HEADS, GDN_DV, GDN_DK), jnp.float32)
        zero_c = jnp.zeros((bp, CONV_W - 1, QKV_DIM), xp.dtype)
        xp, ckv_p, kr_p, s_p, c_p, _ = block(xp, pos_p, lp, None, zero_s, zero_c, mk_p, mv_p)
        rows_p.append((ckv_p, kr_p, s_p, c_p, mk_p, mv_p))
        ckv_past = cache_mla_ckv[l][page_table].reshape(bs, past_len, MLA_KV_RANK)
        kr_past = cache_mla_kr[l][page_table].reshape(bs, past_len, MLA_ROPE)
        xs, ckv_s, kr_s, s_s, c_s, v_s = block(xs, pos_s, lp, (ckv_past, kr_past), state_gdn[l], state_conv[l],
                                               cache_mem_k[l], cache_mem_v[l])
        rows_s.append((ckv_s, kr_s, s_s, c_s, v_s))
    p_ckv, p_kr, p_gdn, p_conv, p_mk, p_mv = [jnp.stack(a) for a in zip(*rows_p)]
    s_ckv, s_kr, s_gdn, s_conv, s_v = [jnp.stack(a) for a in zip(*rows_s)]
    return (xp, xs, p_ckv, p_kr, p_gdn, p_conv, p_mk, p_mv, s_ckv, s_kr, s_gdn, s_conv, s_v)


_drawn_inputs = setup_inputs


def setup_inputs(seed=0):
    import zlib

    import numpy as np

    out = dict(_drawn_inputs(seed))
    spreads = {}
    factors = {'mla_cq_g': 3.298,
     'mla_qn_g': 8.0,
     'mla_qr_g': 8.0,
     'mla_ckv_g': 2.733,
     'mla_kr_g': 3.525,
     'mla_kn_g': 3.665,
     'gdn_out_g': 3.065,
     'mem_norm_g': 2.687,
     'mem_qn_g': 4.955,
     'mem_kn_g': 2.782,
     'gm_b': 3.889,
     'moe_be': 5.327,
     'gm_norm_g': 2.697}
    for name, (base, spread) in spreads.items():
        noise = np.random.default_rng([zlib.crc32(name.encode()), seed]).standard_normal(out[name].shape)
        drawn = base * np.exp(spread * noise) if base else spread * noise
        out[name] = __import__('jax').numpy.asarray(drawn.astype(out[name].dtype))
    for name, factor in factors.items():
        out[name] = (out[name] * factor).astype(out[name].dtype)
    return out
```

```python
from contextlib import ExitStack

import numpy as np

import concourse.bass as bass
from concourse import mybir

F32 = mybir.dt.float32
I32 = mybir.dt.int32
ALU = mybir.AluOpType
ACT = mybir.ActivationFunctionType
AX = mybir.AxisListType

P = 128
D_MODEL = 1024
KT = D_MODEL // P
DEPTH = 2
NP_TOK = 256
NS_TOK = 8
T = NP_TOK + NS_TOK
CHUNKS = ((0, P), (P, P), (NP_TOK, NS_TOK))
H = 4
HD = 64
ROPE = 32
QK = HD + ROPE
RANK = 128
PAGES = 8
NPG = NS_TOK * PAGES
POOL = 80
MEM = 256
EPS = 1e-6
FIRST_SEM = 110
NEG = -1e30
MLA_SCALE = QK ** -0.5
MEM_SCALE = HD ** -0.5

TM_V, TM_CKV, TM_KR, TM_BETA, TM_ALPHA, TM_W = 0, 256, 384, 416, 420, 424
FM_U, FM_CQ, FM_QKV, FM_ZG, FM_MQ, FM_N = 0, 2, 4, 10, 12, 14
GATE_TILES = 4 * KT

CONST_COLS = dict(ident=128, tri=128, blk=128, lev=7 * 128, causal=128, rope=96, m832=256, sel832=32,
                  selrow=8, qr=64, hsel=4, selg=512, mv=4, m16=16, seln=8, rev=8, mq=512)
CONST_AT, _at = {}, 0
for _name, _n in CONST_COLS.items():
    CONST_AT[_name] = _at
    _at += _n
CONST_W = _at

VEC_COLS = dict(g1=8, cq_g=2, conv=24, gdn_g=1, mq_g=1, memn_g=8, g2=8, ws0=2, b0=2, kn_g=1)
VEC_AT, _at = {}, 0
for _name, _n in VEC_COLS.items():
    VEC_AT[_name] = _at
    _at += _n
VEC_W = _at

ROW_COLS = dict(gm_g=256, ckv_g=128, kr_g=32, qn_g=64, qr_g=32, kn_g=64, memk_g=64, a_log=4, dt=4,
                moe_b=36)
ROW_AT, _at = {}, 0
for _name, _n in ROW_COLS.items():
    ROW_AT[_name] = _at
    _at += _n
ROW_W = _at


def constants():
    c = np.zeros((P, CONST_W), np.float32)
    p = np.arange(P)

    def put(name, a):
        a = np.asarray(a, np.float32).reshape(-1, CONST_COLS[name])
        c[:a.shape[0], CONST_AT[name]:CONST_AT[name] + CONST_COLS[name]] = a

    put("ident", np.eye(P))
    put("tri", p[:, None] <= p[None, :])
    put("blk", p[:, None] // HD == p[None, :] // HD)
    lev = [(p[:, None] // (2 << k) == p[None, :] // (2 << k)) & (p[:, None] // (1 << k) % 2 == 0)
           & (p[None, :] // (1 << k) % 2 == 1) for k in range(7)]
    put("lev", np.stack(lev, 1))
    put("causal", np.where(p[None, :] <= p[:, None], 0.0, NEG))
    half = ROPE // 2
    inv = np.float32(10000.0) ** (-np.arange(half, dtype=np.float32) / np.float32(half))
    pos = np.stack([p, p + P, np.full(P, PAGES * P)], 1).astype(np.float32)
    ang = pos[:, :, None] * inv
    put("rope", np.stack([np.cos(ang), np.sin(ang)], 2))
    n = np.arange(NS_TOK)
    nh_n, nh_h = np.arange(32) // H, np.arange(32) % H
    put("m832", np.broadcast_to(n[:, None] == nh_n[None, :], (P, NS_TOK, 32)))
    put("sel832", n[:, None] == nh_n[None, :])
    put("selrow", nh_n[:, None] == n[None, :])
    put("qr", (4 * np.arange(2)[None, :, None] + (p // ROPE)[:, None, None]) == nh_n[None, None, :])
    put("hsel", nh_h[:, None] == np.arange(H)[None, :])
    gn, gh, gv = p // 16, p // 4 % 4, p % 4
    put("selg", (n[:, None, None] == gn) & (np.arange(H)[None, :, None] == gh))
    put("mv", gv[:, None] == np.arange(4))
    put("m16", (gh[:, None, None] == np.arange(H)[None, :, None]) & (gv[:, None, None] == np.arange(4)))
    put("seln", gn[:, None] == n)
    put("rev", np.broadcast_to(np.arange(8, 0, -1), (P, 8)))
    t = np.arange(2)
    put("mq", (n[None, :, None, None] == nh_n) & (2 * t[None, None, :, None] + (p // HD)[:, None, None, None]
                                                  == nh_h))
    return c


def build(nc, A):
    with ExitStack() as top:
        def alloc(ctx, name, shape, dt=F32):
            return ctx.enter_context(nc.sbuf_tensor(name, shape, dt))

        xT = alloc(top, "xT", [P, KT, T])
        hT = alloc(top, "hT", [P, KT, T])
        zT = alloc(top, "zT", [P, FM_N, T])
        tm = alloc(top, "tm", [P, 3, TM_W])
        brT = alloc(top, "brT", [P, 8, T])
        cst = alloc(top, "cst", [P, CONST_W])
        ones = alloc(top, "ones", [P, P])
        epsc = alloc(top, "epsc", [P, 1])
        vec = alloc(top, "vec", [P, VEC_W])
        row = alloc(top, "row", [P, ROW_W])
        bank = [top.enter_context(nc.psum_tensor(f"bank{i}", [P, 512], F32)) for i in range(8)]

        def C(name, *dims):
            a = cst[:, CONST_AT[name]:CONST_AT[name] + CONST_COLS[name]]
            if len(dims) == 2:
                return a.rearrange("p (a b) -> p a b", a=dims[0])
            if len(dims) == 3:
                return a.rearrange("p (a b c) -> p a b c", a=dims[0], b=dims[1])
            return a

        def V(name, i=0, n=1):
            return vec[:, VEC_AT[name] + i:VEC_AT[name] + i + n]

        def R(name):
            return row[:, ROW_AT[name]:ROW_AT[name] + ROW_COLS[name]]

        class Phase:

            def __init__(self, name):
                self.name, self.ctx, self.sems, self.count = name, ExitStack(), {}, {}

            def sb(self, name, shape, dt=F32):
                return alloc(self.ctx, f"{self.name}_{name}", shape, dt)

            def sem(self, name):
                if name not in self.sems:
                    self.sems[name] = self.ctx.enter_context(
                        nc.semaphore(f"{self.name}_{name}", num=FIRST_SEM + len(self.sems)))
                return self.sems[name]

            def __enter__(self):
                self.block = nc.Block(no_gpsimd_drain=True)
                self.b = self.block.__enter__()
                return self

            def __exit__(self, *e):
                self.block.__exit__(*e)
                if e[0] is None:
                    nc.all_engine_barrier(sems_to_clear=range(FIRST_SEM, FIRST_SEM + len(self.sems)))
                self.ctx.close()

        def stepper(ph, eng, default):
            count = {}

            def step(ins, name=default, wait=True):
                count[name] = count.get(name, 0) + 1
                ins.then_inc(ph.sem(name), 1)
                if wait:
                    eng.wait_ge(ph.sem(name), count[name])

            return step

        env = dict(locals())
        env.pop("nc"), env.pop("A")
        start(nc, A, env)
        with nc.Fori(0, DEPTH) as l:
            for phase in PHASES:
                phase(nc, A, env, l)
        finish(nc, A, env)


def start(nc, A, E):
    with E["Phase"]("start") as ph:
        @ph.b.sync
        def _(sp):
            sp.dma_start(E["xT"][:], A["xT"]).then_inc(ph.sem("loaded"), 16)
            sp.dma_start(E["cst"][:], A["cst"]).then_inc(ph.sem("loaded"), 16)
            sp.wait_ge(ph.sem("loaded"), 32)

        @ph.b.vector
        def _(dve):
            nc.vector.memset(E["tm"][:], 0.0)
            nc.vector.memset(E["ones"][:], 1.0)
            nc.vector.memset(E["epsc"][:], EPS).then_inc(ph.sem("set"), 1)
            dve.wait_ge(ph.sem("set"), 1)


def finish(nc, A, E):
    with E["Phase"]("finish") as ph:
        @ph.b.sync
        def _(sp):
            sp.dma_start(A["o_x"], E["xT"][:]).then_inc(ph.sem("stored"), 16)
            sp.wait_ge(ph.sem("stored"), 16)


def project(nc, A, E, l):
    xT, hT, zT, tm, ones, bank, V = (E[k] for k in ("xT", "hT", "zT", "tm", "ones", "bank", "V"))
    with E["Phase"]("proj") as ph:
        S = ph.sem
        sq = ph.sb("sq", [P, KT, T])
        rstd = ph.sb("rstd", [P, T])
        wtm = ph.sb("wtm", [P, KT, TM_W])
        wfm = [ph.sb(f"wfm{i}", [P, KT, P]) for i in range(2)]

        @ph.b.sync
        def _(sp):
            sp.dma_start(E["vec"][:], A["vec"][l]).then_inc(S("vec_loaded"), 16)
            sp.dma_start(E["row"][:], A["row"][l].partition_broadcast(P)).then_inc(S("row_loaded"), 16)
            sp.dma_start(wtm[:], A["w_tm"][l]).then_inc(S("wtm_loaded"), 16)
            for i in range(2):
                sp.dma_start(wfm[i][:], A["w_fm"][l, i]).then_inc(S(f"wfm{i}_loaded"), 16)
            with sp.Fori(1, FM_N // 2) as t:
                for i in range(2):
                    tile = A["w_fm"][l, 2 * t + i]
                    sp.wait_ge(S(f"fm{i}_done"), t)
                    sp.dma_start(wfm[i][:], tile).then_inc(S(f"wfm{i}_loaded"), 16)
            sp.wait_ge(S("row_loaded"), 16)

        @ph.b.vector
        def _(dve):
            nc.vector.tensor_tensor(sq[:], xT[:], xT[:], ALU.mult).then_inc(S("sq_ready"), 1)
            dve.wait_ge(S("root_ready"), 1)
            nc.vector.reciprocal(rstd[:], rstd[:]).then_inc(S("rstd_ready"), 1)
            dve.wait_ge(S("rstd_ready"), 1)
            dve.wait_ge(S("vec_loaded"), 16)
            for k in range(KT):
                nc.vector.scalar_tensor_tensor(hT[:, k, :], xT[:, k, :], V("g1", k), rstd[:], ALU.mult,
                                               ALU.mult).then_inc(S("h_ready"), 1)

        @ph.b.tensor
        def _(pe):
            pe.wait_ge(S("sq_ready"), 1)
            for k in range(KT):
                mm = pe.matmul(bank[0][:, 0:T], ones[:], sq[:, k, :], start=k == 0, stop=k == KT - 1)
            mm.then_inc(S("ss_done"), 1)
            pe.wait_ge(S("wtm_loaded"), 16)
            for c, (t0, n) in enumerate(CHUNKS):
                for k in range(KT):
                    if c == 0:
                        pe.wait_ge(S("h_ready"), k + 1)
                    mm = pe.matmul(bank[1 + c][0:n, 0:TM_W], hT[:, k, t0:t0 + n], wtm[:, k, :],
                                   start=k == 0, stop=k == KT - 1)
                mm.then_inc(S("tm_done"), 1)

            def tile(i):
                for k in range(KT):
                    mm = pe.matmul(bank[4 + i][:, 0:T], wfm[i][:, k, :], hT[:, k, :], start=k == 0,
                                   stop=k == KT - 1)
                mm.then_inc(S(f"fm{i}_done"), 1)

            for i in range(2):
                pe.wait_ge(S(f"wfm{i}_loaded"), 16)
                tile(i)
            with pe.Fori(1, FM_N // 2) as t:
                for i in range(2):
                    pe.wait_ge(S(f"wfm{i}_loaded"), 16 * t + 16)
                    pe.wait_ge(S(f"fm{i}_copied"), t)
                    tile(i)

        @ph.b.scalar
        def _(act):
            act.wait_ge(S("ss_done"), 1)
            nc.scalar.activation(rstd[:], bank[0][:, 0:T], ACT.Sqrt, bias=E["epsc"][:],
                                 scale=1.0 / D_MODEL).then_inc(S("root_ready"), 1)
            for c, (t0, n) in enumerate(CHUNKS):
                act.wait_ge(S("tm_done"), c + 1)
                nc.scalar.copy(tm[0:n, c, :], bank[1 + c][0:n, 0:TM_W])
            with act.Fori(0, FM_N // 2) as t:
                for i in range(2):
                    act.wait_ge(S(f"fm{i}_done"), t + 1)
                    nc.scalar.copy(zT[:, 2 * t + i, :], bank[4 + i][:, 0:T]).then_inc(S(f"fm{i}_copied"), 1)


def gmlp(nc, A, E, l):
    zT, tm, brT, bank, C, V, R = (E[k] for k in ("zT", "tm", "brT", "bank", "C", "V", "R"))
    with E["Phase"]("gmlp") as ph:
        S = ph.sem
        uT = ph.sb("uT", [P, 2, T])
        gv = ph.sb("gv", [P, 3, 256])
        sq = ph.sb("sq", [P, 3, 256])
        ss = ph.sb("ss", [P, 3])
        ws = ph.sb("ws", [P, H, P])
        bias = ph.sb("bias", [P, 2, P])
        mixed = ph.sb("mixed", [P, 2, T])

        @ph.b.sync
        def _(sp):
            sp.dma_start(ws[:], A["gm_ws"][l]).then_inc(S("ws_loaded"), 16)
            for g in range(2):
                sp.dma_start(bias[HD * g:HD * g + HD], A["gm_b"][l, g].partition_broadcast(HD))\
                    .then_inc(S("bias_loaded"), 16)
            sp.wait_ge(S("v_ready"), 2)
            sp.dma_start(A["o_gv"][l], gv[0:NS_TOK, 2, :]).then_inc(S("v_stored"), 16)
            sp.wait_ge(S("v_stored"), 16)

        @ph.b.scalar
        def _(act):
            nc.scalar.activation(gv[:], tm[:, :, TM_V:TM_V + 256], ACT.Gelu).then_inc(S("gelu_done"), 1)
            nc.scalar.activation(uT[:], zT[:, FM_U:FM_U + 2, :], ACT.Gelu).then_inc(S("u_ready"), 1)
            act.wait_ge(S("ss_ready"), 1)
            nc.scalar.activation(ss[:], ss[:], ACT.Sqrt, bias=E["epsc"][:], scale=1.0 / 256)\
                .then_inc(S("root_ready"), 1)

        @ph.b.vector
        def _(dve):
            step = E["stepper"](ph, dve, "dve_step")
            dve.wait_ge(S("gelu_done"), 1)
            step(nc.vector.tensor_tensor(sq[:], gv[:], gv[:], ALU.mult))
            step(nc.vector.tensor_reduce(ss[:], sq[:], AX.X, ALU.add), "ss_ready", wait=False)
            dve.wait_ge(S("ws_loaded"), 16)
            nc.vector.tensor_tensor(ws[:], ws[:], C("tri").unsqueeze(1).to_broadcast([P, H, P]), ALU.mult)\
                .then_inc(S("ws_ready"), 1)
            dve.wait_ge(S("root_ready"), 1)
            step(nc.vector.reciprocal(ss[:], ss[:]))
            step(nc.vector.tensor_tensor(gv[:], gv[:], ss[:].unsqueeze(2).to_broadcast([P, 3, 256]), ALU.mult),
                 "v_ready")
            step(nc.vector.tensor_tensor(gv[:], gv[:], R("gm_g").unsqueeze(1).to_broadcast([P, 3, 256]),
                                         ALU.mult), "v_ready", wait=False)
            dve.wait_ge(S("bias_loaded"), 32)
            for c in range(2):
                dve.wait_ge(S("mix_done"), c + 1)
                step(nc.vector.tensor_tensor(mixed[:, :, c * P:c * P + P],
                                             bank[c][:, 0:256].rearrange("p (a i) -> p a i", a=2), bias[:],
                                             ALU.add))
            dve.wait_ge(S("vT_done"), 1)
            for a in range(2):
                step(nc.vector.tensor_scalar(mixed[:, a, NP_TOK:T], bank[2][:, NS_TOK * a:NS_TOK * a + NS_TOK],
                                             V("ws0", a), V("b0", a), ALU.mult, ALU.add))
            dve.wait_ge(S("u_ready"), 1)
            step(nc.vector.tensor_tensor(brT[:, 0:2, :], mixed[:], uT[:], ALU.mult))

        @ph.b.tensor
        def _(pe):
            pe.wait_ge(S("v_ready"), 2)
            pe.wait_ge(S("ws_ready"), 1)
            for c in range(2):
                for g in range(H):
                    o = HD * (g % 2)
                    mm = pe.matmul(bank[c][o:o + HD, P * (g // 2):P * (g // 2) + P],
                                   gv[:, c, HD * g:HD * g + HD], ws[:, g, :], start=True, stop=True)
                mm.then_inc(S("mix_done"), 1)
            for a in range(2):
                mm = pe.transpose(bank[2][:, NS_TOK * a:NS_TOK * a + NS_TOK], gv[0:NS_TOK, 2, P * a:P * a + P],
                                  C("ident")[0:NS_TOK, 0:NS_TOK])
            mm.then_inc(S("vT_done"), 1)


def memory(nc, A, E, l):
    zT, brT, bank, C, V, R, ones = (E[k] for k in ("zT", "brT", "bank", "C", "V", "R", "ones"))
    with E["Phase"]("mem") as ph:
        S = ph.sem
        memT = ph.sb("memT", [P, KT, MEM])
        sq = ph.sb("sq", [P, KT, MEM])
        rstd = ph.sb("rstd", [P, MEM])
        wkv = ph.sb("wkv", [P, KT, 512])
        kv = ph.sb("kv", [P, 2, 512])
        ksq = ph.sb("ksq", [P, 2, 256])
        kss = ph.sb("kss", [P, 2, H])
        kT = ph.sb("kT", [P, 2, MEM])
        qT = ph.sb("qT", [P, 2, T])
        qsq = ph.sb("qsq", [P, 2, T])
        qblk = ph.sb("qblk", [P, 16, 32])
        sc = ph.sb("sc", [P, 2, H, MEM])
        scs = ph.sb("scs", [32, MEM])
        mx = ph.sb("mx", [P, 2, H])
        mxs = ph.sb("mxs", [32, 1])
        sm = ph.sb("sm", [P, 2, H])
        sms = ph.sb("sms", [32, 1])
        pT = ph.sb("pT", [P, 2, H, NP_TOK])
        psT = ph.sb("psT", [P, 2, 32])
        pblk = ph.sb("pblk", [P, 2, NS_TOK, 32])
        outs = ph.sb("outs", [32, H, HD])
        ckT = ph.sb("ckT", [P, NS_TOK, 2, MEM])
        cv = ph.sb("cv", [P, NS_TOK, 2, 256])

        @ph.b.sync
        def _(sp):
            sp.dma_start(memT[:], A["memT"]).then_inc(S("mem_loaded"), 16)
            sp.dma_start(wkv[:], A["w_kv"][l]).then_inc(S("wkv_loaded"), 16)
            sp.dma_start(ckT[:], A["memkT"][l]).then_inc(S("ck_loaded"), 16)
            sp.dma_start(cv[:], A["memv"][l]).then_inc(S("cv_loaded"), 16)
            sp.wait_ge(S("kv_ready"), 1)
            for i in range(2):
                sp.dma_start(A["o_mem"][l, :, i], kv[:, :, 256 * i:256 * i + 256]).then_inc(S("kv_stored"), 16)
            sp.wait_ge(S("kv_stored"), 32)

        @ph.b.tensor
        def _(pe):
            pe.wait_ge(S("memsq_ready"), 1)
            for k in range(KT):
                mm = pe.matmul(bank[0][:, 0:MEM], ones[:], sq[:, k, :], start=k == 0, stop=k == KT - 1)
            mm.then_inc(S("memss_done"), 1)
            pe.wait_ge(S("qsq_ready"), 1)
            for t in range(2):
                mm = pe.matmul(bank[1 + t][:, 0:T], C("blk"), qsq[:, t, :], start=True, stop=True)
            mm.then_inc(S("qss_done"), 1)
            pe.wait_ge(S("memh_ready"), KT)
            pe.wait_ge(S("wkv_loaded"), 16)
            for c in range(2):
                for k in range(KT):
                    mm = pe.matmul(bank[3 + c][:], memT[:, k, P * c:P * c + P], wkv[:, k, :], start=k == 0,
                                   stop=k == KT - 1)
                mm.then_inc(S("kv_done"), 1)
            pe.wait_ge(S("qblk_ready"), 16)
            pe.wait_ge(S("ck_loaded"), 16)
            for i in range(16):
                mm = pe.matmul(bank[5][0:32, 0:MEM], qblk[:, i, :], ckT[:, i // 2, i % 2, :], start=i == 0,
                               stop=i == 15)
            mm.then_inc(S("scs_done"), 1)
            pe.wait_ge(S("kv_ready"), 1)
            for c in range(2):
                for t in range(2):
                    at = P * (2 * t + c)
                    mm = pe.transpose(bank[6][:, at:at + P], kv[:, c, P * t:P * t + P], C("ident"))
            mm.then_inc(S("kT_done"), 1)
            pe.wait_ge(S("kT_ready"), 1)
            pe.wait_ge(S("q_ready"), 3)
            pe.wait_ge(S("kv_copied"), 2)
            for c in range(2):
                for h in range(H):
                    o = HD * (h % 2)
                    mm = pe.matmul(bank[2 * c + h % 2][:, MEM * (h // 2):MEM * (h // 2) + MEM],
                                   qT[o:o + HD, h // 2, P * c:P * c + P], kT[o:o + HD, h // 2, :],
                                   start=True, stop=True)
                    mm.then_inc(S("sc_done"), 1)
            pe.wait_ge(S("ps_ready"), 1)
            for half in range(2):
                mm = pe.transpose(bank[7][:, 32 * half:32 * half + 32], scs[:, P * half:P * half + P],
                                  C("ident")[0:32, 0:32])
            mm.then_inc(S("psT_done"), 1)
            pe.wait_ge(S("p_ready"), 1)
            pe.wait_ge(S("sc_copied"), 4)
            for c in range(2):
                for half in range(2):
                    for h in range(H):
                        mm = pe.transpose(bank[2 * c + half][:, P * h:P * h + P],
                                          sc[:, c, h, P * half:P * half + P], C("ident"))
                    mm.then_inc(S("pT_done"), 1)
            pe.wait_ge(S("pblk_ready"), 1)
            pe.wait_ge(S("cv_loaded"), 16)
            for i in range(16):
                mm = pe.matmul(bank[5][0:32, 0:256], pblk[:, i % 2, i // 2, :], cv[:, i // 2, i % 2, :],
                               start=i == 0, stop=i == 15)
            mm.then_inc(S("outs_done"), 1)
            pe.wait_ge(S("pT_copied"), 4)
            for h in range(H):
                o = HD * (h % 2)
                for half in range(2):
                    mm = pe.matmul(bank[6 + h // 2][o:o + HD, 0:NP_TOK],
                                   kv[:, half, 256 + HD * h:256 + HD * h + HD], pT[:, half, h, :],
                                   start=half == 0, stop=half == 1)
            mm.then_inc(S("out_done"), 1)
            pe.wait_ge(S("outs_ready"), 1)
            pe.wait_ge(S("pT_copied"), 4)
            for t in range(2):
                mm = pe.matmul(bank[t][:, 0:NS_TOK], outs[:, 2 * t:2 * t + 2, :].rearrange("p a b -> p (a b)"),
                               C("selrow")[0:32, :], start=True, stop=True)
            mm.then_inc(S("outsT_done"), 1)

        @ph.b.scalar
        def _(act):
            act.wait_ge(S("memss_done"), 1)
            nc.scalar.activation(rstd[:], bank[0][:, 0:MEM], ACT.Sqrt, bias=E["epsc"][:], scale=1.0 / D_MODEL)\
                .then_inc(S("root_ready"), 1)
            act.wait_ge(S("qss_done"), 1)
            for t in range(2):
                nc.scalar.activation(qsq[:, t, :], bank[1 + t][:, 0:T], ACT.Sqrt, bias=E["epsc"][:],
                                     scale=1.0 / HD).then_inc(S("qroot_ready"), 1)
            act.wait_ge(S("kss_ready"), 1)
            nc.scalar.activation(kss[:], kss[:], ACT.Sqrt, bias=E["epsc"][:], scale=1.0 / HD)\
                .then_inc(S("kroot_ready"), 1)
            act.wait_ge(S("shift_s"), 1)
            nc.scalar.activation(scs[:], scs[:], ACT.Exp, scale=MEM_SCALE).then_inc(S("exps_done"), 1)
            act.wait_ge(S("sc_copied"), 4)
            nc.scalar.activation(sc[:], sc[:], ACT.Exp, scale=MEM_SCALE).then_inc(S("exp_done"), 1)
            for i in range(4):
                c, half = i // 2, i % 2
                act.wait_ge(S("pT_done"), i + 1)
                nc.scalar.copy(pT[:, half, :, P * c:P * c + P], bank[i][:].rearrange("p (h t) -> p h t", h=H))\
                    .then_inc(S("pT_copied"), 1)

        @ph.b.vector
        def _(dve):
            step = E["stepper"](ph, dve, "dve_step")
            dve.wait_ge(S("mem_loaded"), 16)
            step(nc.vector.tensor_tensor(sq[:], memT[:], memT[:], ALU.mult), "memsq_ready", wait=False)
            mq = zT[:, FM_MQ:FM_MQ + 2, :]
            step(nc.vector.tensor_tensor(qsq[:], mq, mq, ALU.mult), "qsq_ready")
            dve.wait_ge(S("root_ready"), 1)
            step(nc.vector.reciprocal(rstd[:], rstd[:]))
            for k in range(KT):
                step(nc.vector.scalar_tensor_tensor(memT[:, k, :], memT[:, k, :], V("memn_g", k), rstd[:],
                                                    ALU.mult, ALU.mult), "memh_ready", wait=False)
            dve.wait_ge(S("qroot_ready"), 2)
            step(nc.vector.reciprocal(qsq[:], qsq[:]), "q_ready")
            step(nc.vector.tensor_tensor(qT[:], mq, qsq[:], ALU.mult), "q_ready")
            step(nc.vector.tensor_scalar(qT[:], qT[:], V("mq_g"), None, ALU.mult), "q_ready")
            for i in range(16):
                n, t = i // 2, i % 2
                last = nc.vector.tensor_scalar(qblk[:, i, :], C("mq", 16, 32)[:, i, :],
                                               qT[:, t, NP_TOK + n:NP_TOK + n + 1], None, ALU.mult)
                step(last, "qblk_ready", wait=False)
            for c in range(2):
                dve.wait_ge(S("kv_done"), c + 1)
                step(nc.vector.tensor_copy(kv[:, c, :], bank[3 + c][:]), "kv_copied")
            k4 = kv[:, :, 0:256].rearrange("p c (h e) -> p c h e", h=H)
            step(nc.vector.tensor_tensor(ksq[:], kv[:, :, 0:256], kv[:, :, 0:256], ALU.mult))
            step(nc.vector.tensor_reduce(kss[:], ksq[:].rearrange("p c (h e) -> p c h e", h=H), AX.X, ALU.add),
                 "kss_ready", wait=False)
            dve.wait_ge(S("kroot_ready"), 1)
            step(nc.vector.reciprocal(kss[:], kss[:]))
            for c in range(2):
                step(nc.vector.tensor_tensor(k4[:, c], k4[:, c], kss[:, c].unsqueeze(2).to_broadcast([P, H, HD]),
                                             ALU.mult))
                last = nc.vector.tensor_tensor(k4[:, c], k4[:, c],
                                               R("memk_g").unsqueeze(1).to_broadcast([P, H, HD]), ALU.mult)
                step(last, *(["kv_ready"] if c else []))
            dve.wait_ge(S("scs_done"), 1)
            step(nc.vector.tensor_reduce(mxs[:], bank[5][0:32, 0:MEM], AX.X, ALU.max))
            step(nc.vector.tensor_scalar(scs[:], bank[5][0:32, 0:MEM], mxs[:], None, ALU.subtract), "shift_s",
                 wait=False)
            dve.wait_ge(S("kT_done"), 1)
            step(nc.vector.tensor_copy(kT[:].rearrange("p t s -> p (t s)"), bank[6][:]), "kT_ready", wait=False)
            dve.wait_ge(S("exps_done"), 1)
            step(nc.vector.tensor_reduce(sms[:], scs[:], AX.X, ALU.add))
            step(nc.vector.reciprocal(sms[:], sms[:]))
            step(nc.vector.tensor_scalar(scs[:], scs[:], sms[:], None, ALU.mult), "ps_ready", wait=False)
            for i in range(4):
                c, a = i // 2, i % 2
                dve.wait_ge(S("sc_done"), 4 * c + 3 + a)
                two = bank[i][:].rearrange("p (h s) -> p h s", h=2)
                mxa = mx[:, c].rearrange("p (b a) -> p a b", a=2)[:, a]
                step(nc.vector.tensor_reduce(mxa, two, AX.X, ALU.max))
                step(nc.vector.tensor_tensor(sc[:, c].rearrange("p (b a) s -> p a b s", a=2)[:, a], two,
                                             mxa.unsqueeze(2).to_broadcast([P, 2, MEM]), ALU.subtract),
                     "sc_copied")
            dve.wait_ge(S("exp_done"), 1)
            step(nc.vector.tensor_reduce(sm[:], sc[:], AX.X, ALU.add))
            step(nc.vector.reciprocal(sm[:], sm[:]))
            flat = sc[:].rearrange("p c h s -> p (c h) s")
            step(nc.vector.tensor_tensor(flat, flat, sm[:].rearrange("p c h -> p (c h)").unsqueeze(2)
                                         .to_broadcast([P, 2 * H, MEM]), ALU.mult), "p_ready", wait=False)
            dve.wait_ge(S("psT_done"), 1)
            step(nc.vector.tensor_copy(psT[:].rearrange("p a b -> p (a b)"), bank[7][:, 0:64]))
            for half in range(2):
                last = nc.vector.tensor_tensor(pblk[:, half], C("m832", NS_TOK, 32),
                                               psT[:, half].unsqueeze(1).to_broadcast([P, NS_TOK, 32]), ALU.mult)
                step(last, *(["pblk_ready"] if half else []))
            dve.wait_ge(S("outs_done"), 1)
            step(nc.vector.tensor_tensor(outs[:], bank[5][0:32, 0:256].rearrange("p (h e) -> p h e", h=H),
                                         C("hsel")[0:32, :].unsqueeze(2).to_broadcast([32, H, HD]), ALU.mult),
                 "outs_ready", wait=False)
            dve.wait_ge(S("out_done"), 1)
            for t in range(2):
                step(nc.vector.tensor_copy(brT[:, 6 + t, 0:NP_TOK], bank[6 + t][:, 0:NP_TOK]))
            dve.wait_ge(S("outsT_done"), 1)
            for t in range(2):
                step(nc.vector.tensor_copy(brT[:, 6 + t, NP_TOK:T], bank[t][:, 0:NS_TOK]))


def mla(nc, A, E, l):
    with ExitStack() as both:
        sb = lambda name, shape, dt=F32: E["alloc"](both, f"mla_{name}", shape, dt)
        B = dict(
            q=sb("q", [P, 3, H * QK]),
            kc=sb("kc", [P, 3, H * QK]),
            ckvn=sb("ckvn", [P, 3, RANK]),
            latT=sb("latT", [P, H, T]),
            wuk=sb("wuk", [P, H * HD]),
            ids=sb("ids", [1, NPG], I32),
            ck=sb("ck", [P, NPG, RANK]),
            ckT=sb("ckT", [P, NPG, P]),
            krT=sb("krT", [P, 2, PAGES, P]))
        mla_prompt(nc, A, E, l, B)
        mla_decode(nc, A, E, l, B)


def rotate(step, nc, x, cos, sin, tmp, name="dve_step"):
    half = ROPE // 2
    x1, x2 = x[..., 0:half], x[..., half:ROPE]
    for i, (a, b) in enumerate(((x1, cos), (x2, sin), (x1, sin), (x2, cos))):
        step(nc.vector.tensor_tensor(tmp[i], a, b, ALU.mult))
    step(nc.vector.tensor_tensor(x1, tmp[0], tmp[1], ALU.subtract))
    step(nc.vector.tensor_tensor(x2, tmp[2], tmp[3], ALU.add), name)


def mla_prompt(nc, A, E, l, B):
    zT, tm, bank, C, V, R, ones = (E[k] for k in ("zT", "tm", "bank", "C", "V", "R", "ones"))
    q, kc, ckvn, latT, wuk = (B[k] for k in ("q", "kc", "ckvn", "latT", "wuk"))
    with E["Phase"]("mlap") as ph:
        S = ph.sem
        cqT = ph.sb("cqT", [P, 2, T])
        cqs = ph.sb("cqs", [P, 2, T])
        wuq = ph.sb("wuq", [P, 2, H * QK])
        sq = ph.sb("sq", [P, 3, H * QK])
        rs = ph.sb("rs", [P, 3, 2 * H])
        krn = ph.sb("krn", [P, 3, ROPE])
        crs = ph.sb("crs", [P, 3, 2])
        krss = ph.sb("krss", [P, 3, H])
        tmp = ph.sb("tmp", [P, 4, 3 * H * 16])
        ckvT = ph.sb("ckvT", [P, T])
        qT = ph.sb("qT", [QK, H, NP_TOK])
        kT = ph.sb("kT", [QK, H, NP_TOK])
        sc0 = ph.sb("sc0", [P, H, P])
        sc1 = ph.sb("sc1", [P, H, NP_TOK])
        mx = ph.sb("mx", [P, 2, H])
        pT0 = ph.sb("pT0", [P, 1, 512])
        pT1 = ph.sb("pT1", [P, 2, 512])
        cos, sin = C("rope", 3, 2, 16)[:, :, 0, :], C("rope", 3, 2, 16)[:, :, 1, :]

        @ph.b.sync
        def _(sp):
            sp.dma_start(wuq[:], A["w_uq"][l]).then_inc(S("wuq_loaded"), 16)
            sp.dma_start(wuk[:], A["w_uk"][l]).then_inc(S("wuk_loaded"), 16)
            sp.dma_start(B["ids"][:], A["pages"]).then_inc(S("ids_loaded"), 16)
            sp.wait_ge(S("ids_loaded"), 16)
            with sp.Fori(0, PAGES) as p:
                for g in range(2):
                    for j in range(4):
                        n = 4 * g + j
                        page = sp.value_load(B["ids"][0:1, bass.ds(p + PAGES * n, 1)], min_val=0, max_val=POOL - 1)
                        sp.dma_start(B["ck"][:, bass.ds(p + PAGES * n, 1), :].squeeze(1), A["ckv"][l, page])\
                            .then_inc(S("pages_loaded"), 16)
                        sp.dma_start(B["ckT"][:, bass.ds(p + PAGES * n, 1), :].squeeze(1), A["ckvT"][l, page])\
                            .then_inc(S("pages_loaded"), 16)
                        sp.dma_start(B["krT"][ROPE * j:ROPE * j + ROPE, g, bass.ds(p, 1), :].squeeze(1),
                                     A["krT"][l, page]).then_inc(S("pages_loaded"), 16)
            sp.wait_ge(S("latent_ready"), 2)
            sp.dma_start(A["o_ckv"][l], ckvn[:]).then_inc(S("latent_stored"), 16)
            sp.dma_start(A["o_kr"][l], krn[:]).then_inc(S("latent_stored"), 16)
            sp.wait_ge(S("latent_stored"), 32)
            sp.wait_ge(S("pages_loaded"), 16 * 3 * NPG)

        @ph.b.tensor
        def _(pe):
            pe.wait_ge(S("cqsq_ready"), 1)
            for t in range(2):
                mm = pe.matmul(bank[0][:, 0:T], ones[:], cqs[:, t, :], start=t == 0, stop=t == 1)
            mm.then_inc(S("cqss_done"), 1)
            pe.wait_ge(S("latent_ready"), 1)
            for c, (t0, n) in enumerate(CHUNKS):
                mm = pe.transpose(bank[4][:, t0:t0 + n], ckvn[0:n, c, :], C("ident")[0:n, 0:n])
            mm.then_inc(S("ckvT_done"), 1)
            pe.wait_ge(S("cq_ready"), 2)
            pe.wait_ge(S("wuq_loaded"), 16)
            for c, (t0, n) in enumerate(CHUNKS):
                for t in range(2):
                    mm = pe.matmul(bank[1 + c][0:n, 0:H * QK], cqT[:, t, t0:t0 + n], wuq[:, t, :], start=t == 0,
                                   stop=t == 1)
                mm.then_inc(S("q_done"), 1)
            pe.wait_ge(S("ckvT_ready"), 1)
            pe.wait_ge(S("wuk_loaded"), 16)
            for c, (t0, n) in enumerate(CHUNKS):
                mm = pe.matmul(bank[5 + c][0:n, 0:H * HD], ckvT[:, t0:t0 + n], wuk[:], start=True, stop=True)
                mm.then_inc(S("k_done"), 1)
            pe.wait_ge(S("qn_ready"), 1)
            for c in range(2):
                for h in range(H):
                    mm = pe.transpose(bank[c][0:QK, P * h:P * h + P], q[:, c, QK * h:QK * h + QK], C("ident"))
                mm.then_inc(S("qT_done"), 1)
            pe.wait_ge(S("kn_ready"), 1)
            for c in range(2):
                for h in range(H):
                    mm = pe.transpose(bank[2 + c][0:QK, P * h:P * h + P], kc[:, c, QK * h:QK * h + QK],
                                      C("ident"))
                mm.then_inc(S("kT_done"), 1)
            pe.wait_ge(S("qkT_ready"), 4)
            for h in range(H):
                mm = pe.matmul(bank[4][:, P * h:P * h + P], qT[:, h, 0:P], kT[:, h, 0:P], start=True, stop=True)
            mm.then_inc(S("sc_done"), 1)
            for h in range(H):
                mm = pe.matmul(bank[5 + h // 2][:, NP_TOK * (h % 2):NP_TOK * (h % 2) + NP_TOK], qT[:, h, P:2 * P],
                               kT[:, h, :], start=True, stop=True)
                if h % 2:
                    mm.then_inc(S("sc_done"), 1)
            pe.wait_ge(S("p0_ready"), 1)
            for h in range(H):
                mm = pe.transpose(bank[7][:, P * h:P * h + P], sc0[:, h, :], C("ident"))
            mm.then_inc(S("pT_done"), 1)
            pe.wait_ge(S("p1_ready"), 1)
            for s in range(2):
                for h in range(H):
                    mm = pe.transpose(bank[s][:, P * h:P * h + P], sc1[:, h, P * s:P * s + P], C("ident"))
                mm.then_inc(S("pT_done"), 1)
            pe.wait_ge(S("pT_ready"), 1)
            pe.matmul(bank[2][:], ckvn[:, 0, :], pT0[:, 0, :], start=True, stop=True).then_inc(S("lat_done"), 1)
            pe.wait_ge(S("pT_ready"), 3)
            for s in range(2):
                mm = pe.matmul(bank[3][:], ckvn[:, s, :], pT1[:, s, :], start=s == 0, stop=s == 1)
            mm.then_inc(S("lat_done"), 1)

        @ph.b.scalar
        def _(act):
            eps = E["epsc"][:]
            act.wait_ge(S("cqss_done"), 1)
            nc.scalar.activation(cqs[:, 0, :], bank[0][:, 0:T], ACT.Sqrt, bias=eps, scale=1.0 / 256)\
                .then_inc(S("cqroot_ready"), 1)
            act.wait_ge(S("ckvss_ready"), 2)
            for i, n in enumerate((RANK, ROPE)):
                nc.scalar.activation(crs[:, :, i], crs[:, :, i], ACT.Sqrt, bias=eps, scale=1.0 / n)\
                    .then_inc(S("ckvroot_ready"), 1)
            act.wait_ge(S("ckvT_done"), 1)
            nc.scalar.copy(ckvT[:], bank[4][:, 0:T]).then_inc(S("ckvT_ready"), 1)
            act.wait_ge(S("zeroed"), 2)
            for c, (t0, n) in enumerate(CHUNKS):
                act.wait_ge(S("q_done"), c + 1)
                nc.scalar.copy(q[0:n, c, :], bank[1 + c][0:n, 0:H * QK]).then_inc(S("q_ready"), 1)
            act.wait_ge(S("qss_ready"), 2)
            for i, n in enumerate((HD, ROPE)):
                nc.scalar.activation(rs[:, :, H * i:H * i + H], rs[:, :, H * i:H * i + H], ACT.Sqrt, bias=eps,
                                     scale=1.0 / n).then_inc(S("qroot_ready"), 1)
            for c, (t0, n) in enumerate(CHUNKS):
                act.wait_ge(S("k_done"), c + 1)
                nc.scalar.copy(kc[0:n, c, :].rearrange("p (h e) -> p h e", h=H)[:, :, 0:HD],
                               bank[5 + c][0:n, 0:H * HD].rearrange("p (h e) -> p h e", h=H))\
                    .then_inc(S("k_ready"), 1)
            act.wait_ge(S("kss_ready"), 1)
            nc.scalar.activation(krss[:], krss[:], ACT.Sqrt, bias=eps, scale=1.0 / HD).then_inc(S("kroot_ready"), 1)
            for c in range(2):
                act.wait_ge(S("qT_done"), c + 1)
                nc.scalar.copy(qT[:, :, P * c:P * c + P], bank[c][0:QK, :].rearrange("p (h t) -> p h t", h=H))\
                    .then_inc(S("qkT_ready"), 1)
            for c in range(2):
                act.wait_ge(S("kT_done"), c + 1)
                nc.scalar.copy(kT[:, :, P * c:P * c + P], bank[2 + c][0:QK, :].rearrange("p (h t) -> p h t", h=H))\
                    .then_inc(S("qkT_ready"), 1)
            act.wait_ge(S("shift0"), 1)
            nc.scalar.activation(sc0[:], sc0[:], ACT.Exp).then_inc(S("exp0_done"), 1)
            act.wait_ge(S("shift1"), 1)
            nc.scalar.activation(sc1[:], sc1[:], ACT.Exp).then_inc(S("exp1_done"), 1)
            act.wait_ge(S("pT_done"), 1)
            nc.scalar.copy(pT0[:, 0, :], bank[7][:]).then_inc(S("pT_ready"), 1)
            for s in range(2):
                act.wait_ge(S("pT_done"), s + 2)
                nc.scalar.copy(pT1[:, s, :], bank[s][:]).then_inc(S("pT_ready"), 1)
            for c in range(2):
                act.wait_ge(S("lat_done"), c + 1)
                nc.scalar.copy(latT[:, :, P * c:P * c + P], bank[2 + c][:].rearrange("p (h t) -> p h t", h=H))

        @ph.b.vector
        def _(dve):
            step = E["stepper"](ph, dve, "dve_step")
            tt, red = nc.vector.tensor_tensor, nc.vector.tensor_reduce
            step(nc.vector.memset(q[:], 0.0), "zeroed", wait=False)
            step(nc.vector.memset(kc[:], 0.0), "zeroed")
            cq = zT[:, FM_CQ:FM_CQ + 2, :]
            step(tt(cqs[:], cq, cq, ALU.mult), "cqsq_ready", wait=False)
            raw, rawr = tm[:, :, TM_CKV:TM_CKV + RANK], tm[:, :, TM_KR:TM_KR + ROPE]
            step(tt(sq[:, :, 0:RANK], raw, raw, ALU.mult), wait=False)
            step(tt(sq[:, :, RANK:RANK + ROPE], rawr, rawr, ALU.mult))
            step(red(crs[:, :, 0], sq[:, :, 0:RANK], AX.X, ALU.add), "ckvss_ready", wait=False)
            step(red(crs[:, :, 1], sq[:, :, RANK:RANK + ROPE], AX.X, ALU.add), "ckvss_ready", wait=False)
            dve.wait_ge(S("cqroot_ready"), 1)
            step(nc.vector.reciprocal(cqs[:, 1, :], cqs[:, 0, :]))
            for t in range(2):
                step(nc.vector.scalar_tensor_tensor(cqT[:, t, :], zT[:, FM_CQ + t, :], V("cq_g", t), cqs[:, 1, :],
                                                    ALU.mult, ALU.mult), "cq_ready", wait=False)
            dve.wait_ge(S("ckvroot_ready"), 2)
            step(nc.vector.reciprocal(crs[:], crs[:]))
            step(tt(ckvn[:], raw, crs[:, :, 0].unsqueeze(2).to_broadcast([P, 3, RANK]), ALU.mult), wait=False)
            step(tt(krn[:], rawr, crs[:, :, 1].unsqueeze(2).to_broadcast([P, 3, ROPE]), ALU.mult))
            step(tt(ckvn[:], ckvn[:], R("ckv_g").unsqueeze(1).to_broadcast([P, 3, RANK]), ALU.mult),
                 "latent_ready", wait=False)
            step(tt(krn[:], krn[:], R("kr_g").unsqueeze(1).to_broadcast([P, 3, ROPE]), ALU.mult))
            rotate(step, nc, krn[:], cos, sin,
                   [tmp[:, i, 0:48].rearrange("p (c e) -> p c e", c=3) for i in range(4)])
            kc4 = kc[:].rearrange("p c (h e) -> p c h e", h=H)
            step(tt(kc4[:, :, :, HD:QK], krn[:].unsqueeze(2).to_broadcast([P, 3, H, ROPE]),
                    krn[:].unsqueeze(2).to_broadcast([P, 3, H, ROPE]), ALU.max), "latent_ready", wait=False)
            dve.wait_ge(S("q_ready"), 3)
            q4, sq4 = (a.rearrange("p c (h e) -> p c h e", h=H) for a in (q[:], sq[:]))
            step(tt(sq[:], q[:], q[:], ALU.mult))
            step(red(rs[:, :, 0:H], sq4[:, :, :, 0:HD], AX.X, ALU.add), "qss_ready", wait=False)
            step(red(rs[:, :, H:2 * H], sq4[:, :, :, HD:QK], AX.X, ALU.add), "qss_ready", wait=False)
            dve.wait_ge(S("qroot_ready"), 2)
            step(nc.vector.reciprocal(rs[:], rs[:]))
            q12 = q[:].rearrange("p c (h e) -> p (c h) e", h=H)
            for part, o, n, g in ((0, 0, HD, "qn_g"), (1, HD, ROPE, "qr_g")):
                dims = [P, 3, H, n]
                step(tt(q4[:, :, :, o:o + n], q4[:, :, :, o:o + n],
                        rs[:, :, H * part:H * part + H].unsqueeze(3).to_broadcast(dims), ALU.mult))
                step(tt(q12[:, :, o:o + n], q12[:, :, o:o + n], R(g).unsqueeze(1).to_broadcast([P, 3 * H, n]),
                        ALU.mult))
            wide = [P, 3, H, 16]
            rotate(step, nc, q4[:, :, :, HD:QK], cos.unsqueeze(2).to_broadcast(wide),
                   sin.unsqueeze(2).to_broadcast(wide),
                   [tmp[:, i].rearrange("p (c h e) -> p c h e", c=3, h=H) for i in range(4)], "qn_ready")
            dve.wait_ge(S("k_ready"), 3)
            kn = kc[:].rearrange("p c (h e) -> p (c h) e", h=H)[:, :, 0:HD]
            step(tt(sq[:, :, 0:256].rearrange("p c (h e) -> p c h e", h=H), kc4[:, :, :, 0:HD],
                    kc4[:, :, :, 0:HD], ALU.mult))
            step(red(krss[:], sq[:, :, 0:256].rearrange("p c (h e) -> p c h e", h=H), AX.X, ALU.add), "kss_ready",
                 wait=False)
            dve.wait_ge(S("kroot_ready"), 1)
            step(nc.vector.reciprocal(krss[:], krss[:]))
            step(tt(kn, kn, krss[:].rearrange("p c h -> p (c h)").unsqueeze(2).to_broadcast([P, 3 * H, HD]),
                    ALU.mult))
            step(tt(kn, kn, R("kn_g").unsqueeze(1).to_broadcast([P, 3 * H, HD]), ALU.mult), "kn_ready")
            dve.wait_ge(S("sc_done"), 1)
            mask = C("causal")

            def rows(sc, m, n):
                step(red(m, sc, AX.X, ALU.max))
                return tt(sc, sc, m.unsqueeze(2).to_broadcast([P, H, n]), ALU.subtract)

            for h in range(H):
                step(nc.vector.scalar_tensor_tensor(sc0[:, h, :], bank[4][:, P * h:P * h + P], MLA_SCALE, mask,
                                                    ALU.mult, ALU.add))
            step(rows(sc0[:], mx[:, 0], P), "shift0", wait=False)
            for h in range(H):
                dve.wait_ge(S("sc_done"), 2 + h // 2)
                src = bank[5 + h // 2][:, NP_TOK * (h % 2):NP_TOK * (h % 2) + NP_TOK]
                step(nc.vector.tensor_scalar(sc1[:, h, 0:P], src[:, 0:P], MLA_SCALE, None, ALU.mult))
                step(nc.vector.scalar_tensor_tensor(sc1[:, h, P:2 * P], src[:, P:2 * P], MLA_SCALE, mask, ALU.mult,
                                                    ALU.add))
            step(rows(sc1[:], mx[:, 1], NP_TOK), "shift1", wait=False)
            for i, (sc, n) in enumerate(((sc0, P), (sc1, NP_TOK))):
                dve.wait_ge(S(f"exp{i}_done"), 1)
                step(red(mx[:, i], sc[:], AX.X, ALU.add))
                step(nc.vector.reciprocal(mx[:, i], mx[:, i]))
                step(tt(sc[:], sc[:], mx[:, i].unsqueeze(2).to_broadcast([P, H, n]), ALU.mult), f"p{i}_ready",
                     wait=False)


def mla_decode(nc, A, E, l, B):
    brT, bank, C, V, ones = (E[k] for k in ("brT", "bank", "C", "V", "ones"))
    q, kc, ckvn, latT, wuk, ck, ckT, krT = (B[k] for k in ("q", "kc", "ckvn", "latT", "wuk", "ck", "ckT", "krT"))
    N = NS_TOK
    RAW = 4
    with E["Phase"]("mlad") as ph:
        S = ph.sem
        wukT = ph.sb("wukT", [HD, H, RANK])
        wuv = ph.sb("wuv", [P, H * HD])
        qsT = ph.sb("qsT", [QK, H, N])
        qa = ph.sb("qa", [P, N, H])
        qblk = ph.sb("qblk", [P, N, 32])
        qrep = ph.sb("qrep", [N, H, 4, ROPE])
        qr = ph.sb("qr", [P, N, H])
        qrblk = ph.sb("qrblk", [P, 2, 32])
        prod = ph.sb("prod", [N, H * QK])
        so = ph.sb("so", [N, H])
        sox = ph.sb("sox", [N, N, H])
        sqr = ph.sb("sqr", [P, RAW, 512])
        ssq = ph.sb("ssq", [P, PAGES, 32])
        rT = ph.sb("rT", [32, PAGES * P])
        sc = ph.sb("sc", [32, PAGES * P + 1])
        mx = ph.sb("mx", [32, 1])
        pT = ph.sb("pT", [P, PAGES, 32])
        pblk = ph.sb("pblk", [P, PAGES, N, 32])
        own = ph.sb("own", [32, RANK])
        lat = ph.sb("lat", [32, RANK])

        @ph.b.sync
        def _(sp):
            sp.dma_start(wukT[:], A["w_ukT"][l]).then_inc(S("wukT_loaded"), 16)
            sp.dma_start(wuv[:], A["w_uv"][l]).then_inc(S("wuv_loaded"), 16)

        @ph.b.tensor
        def _(pe):
            ident = C("ident")
            for h in range(H):
                mm = pe.transpose(bank[0][0:QK, N * h:N * h + N], q[0:N, 2, QK * h:QK * h + QK], ident[0:N, 0:N])
            mm.then_inc(S("qsT_done"), 1)
            pe.wait_ge(S("qrep_ready"), 1)
            for h in range(H):
                mm = pe.matmul(bank[2][:, N * h:N * h + N], qrep[:, h].rearrange("p a b -> p (a b)"),
                               ident[0:N, 0:N], start=True, stop=True)
            mm.then_inc(S("qr_done"), 1)
            pe.wait_ge(S("sox_ready"), 1)
            pe.matmul(bank[3][0:32, 0:1], sox[:].rearrange("p a b -> p (a b)"), ones[0:N, 0:1], start=True,
                      stop=True).then_inc(S("own_done"), 1)
            pe.wait_ge(S("qsT_ready"), 1)
            pe.wait_ge(S("wukT_loaded"), 16)
            for h in range(H):
                mm = pe.matmul(bank[1][:, N * h:N * h + N], wukT[:, h, :], qsT[0:HD, h, :], start=True, stop=True)
            mm.then_inc(S("qa_done"), 1)
            for b in range(NPG // 2):
                if b >= RAW:
                    pe.wait_ge(S("squared"), b - RAW + 1)
                for j in range(2):
                    mm = pe.matmul(bank[4 + b % RAW][:, 256 * j:256 * j + 256], ckT[:, 2 * b + j, :], wuk[:],
                                   start=True, stop=True)
                mm.then_inc(S("raw_done"), 1)
            pe.wait_ge(S("qblk_ready"), 3)
            for half in range(2):
                for n in range(N):
                    at = PAGES * n + 4 * half
                    mm = pe.matmul(bank[half][0:32, :], qblk[:, n, :],
                                   ckT[:, at:at + 4, :].rearrange("p a b -> p (a b)"), start=n == 0, stop=n == N - 1)
                mm.then_inc(S("nope_done"), 1)
            for half in range(2):
                for g in range(2):
                    mm = pe.matmul(bank[2 + half][0:32, :], qrblk[:, g, :],
                                   krT[:, g, 4 * half:4 * half + 4, :].rearrange("p a b -> p (a b)"),
                                   start=g == 0, stop=g == 1)
                mm.then_inc(S("rope_done"), 1)
            pe.wait_ge(S("rinv_ready"), 1)
            for p in range(PAGES):
                mm = pe.transpose(bank[4 + p // 4][0:32, P * (p % 4):P * (p % 4) + P], ssq[:, p, :], ident)
            mm.then_inc(S("rT_done"), 1)
            pe.matmul(bank[6][0:32, 0:RANK], C("sel832")[0:N, :], ckvn[0:N, 2, :], start=True, stop=True)\
                .then_inc(S("rep_done"), 1)
            pe.wait_ge(S("p_ready"), 1)
            for p in range(PAGES):
                mm = pe.transpose(bank[7][:, 32 * p:32 * p + 32], sc[:, P * p:P * p + P], ident[0:32, 0:32])
            mm.then_inc(S("pT_done"), 1)
            pe.wait_ge(S("pblk_ready"), 1)
            for p in range(PAGES):
                for n in range(N):
                    i = N * p + n
                    mm = pe.matmul(bank[5][0:32, 0:RANK], pblk[:, p, n, :], ck[:, PAGES * n + p, :], start=i == 0,
                                   stop=i == NPG - 1)
            mm.then_inc(S("lat_done"), 1)
            pe.wait_ge(S("lat_ready"), 1)
            pe.transpose(bank[4][:, 0:32], lat[:], ident[0:32, 0:32]).then_inc(S("latT_done"), 1)
            pe.wait_ge(S("latT_ready"), 1)
            pe.wait_ge(S("wuv_loaded"), 16)
            for h in range(H):
                o = HD * (h % 2)
                mm = pe.matmul(bank[h // 2][o:o + HD, 0:T], wuv[:, HD * h:HD * h + HD], latT[:, h, :], start=True,
                               stop=True)
            mm.then_inc(S("out_done"), 1)

        @ph.b.scalar
        def _(act):
            for b in range(NPG // 2):
                act.wait_ge(S("raw_done"), b + 1)
                if b >= RAW:
                    act.wait_ge(S("summed"), b - RAW + 1)
                nc.scalar.activation(sqr[:, b % RAW, :], bank[4 + b % RAW][:], ACT.Square)\
                    .then_inc(S("squared"), 1)
            act.wait_ge(S("summed"), NPG // 2)
            nc.scalar.activation(ssq[:], ssq[:], ACT.Sqrt, bias=E["epsc"][:], scale=1.0 / HD)\
                .then_inc(S("root_ready"), 1)
            act.wait_ge(S("shift"), 1)
            nc.scalar.activation(sc[:], sc[:], ACT.Exp, scale=MLA_SCALE).then_inc(S("exp_done"), 1)
            act.wait_ge(S("out_done"), 1)
            for t in range(2):
                nc.scalar.copy(brT[:, 2 + t, :], bank[t][:, 0:T])

        @ph.b.vector
        def _(dve):
            step = E["stepper"](ph, dve, "dve_step")
            tt, red = nc.vector.tensor_tensor, nc.vector.tensor_reduce
            q3 = q[0:N, 2, :].rearrange("p (h e) -> p h e", h=H)
            step(nc.vector.tensor_copy(qrep[:], q3[:, :, HD:QK].unsqueeze(2).to_broadcast([N, H, 4, ROPE])),
                 "qrep_ready", wait=False)
            step(tt(prod[:], q[0:N, 2, :], kc[0:N, 2, :], ALU.mult))
            step(red(so[:], prod[:].rearrange("p (h e) -> p h e", h=H), AX.X, ALU.add))
            step(tt(sox[:], C("sel832")[0:N].rearrange("p (n h) -> p n h", n=N),
                    so[:].unsqueeze(1).to_broadcast([N, N, H]), ALU.mult), "sox_ready", wait=False)
            dve.wait_ge(S("qsT_done"), 1)
            step(nc.vector.tensor_scalar(qsT[0:HD].rearrange("p h n -> p (h n)"), bank[0][0:HD, 0:H * N],
                                         V("kn_g")[0:HD], None, ALU.mult), "qsT_ready", wait=False)
            dve.wait_ge(S("qr_done"), 1)
            step(nc.vector.tensor_copy(qr[:], bank[2][:, 0:H * N].rearrange("p (h n) -> p n h", h=H)))
            step(tt(qrblk[:], C("qr", 2, 32), qr[:].rearrange("p n h -> p (n h)").unsqueeze(1)
                    .to_broadcast([P, 2, 32]), ALU.mult), "qblk_ready", wait=False)
            dve.wait_ge(S("qa_done"), 1)
            step(nc.vector.tensor_copy(qa[:], bank[1][:, 0:H * N].rearrange("p (h n) -> p n h", h=H)))
            step(tt(qblk[:], C("m832", N, 32), qa[:].rearrange("p n h -> p (n h)").unsqueeze(1)
                    .to_broadcast([P, N, 32]), ALU.mult), "qblk_ready", wait=False)
            dve.wait_ge(S("own_done"), 1)
            step(nc.vector.tensor_copy(sc[:, PAGES * P:], bank[3][0:32, 0:1]), "qblk_ready")
            for b in range(NPG // 2):
                n, p = b // 4, 2 * (b % 4)
                dve.wait_ge(S("squared"), b + 1)
                step(red(ssq[:, p:p + 2, H * n:H * n + H],
                         sqr[:, b % RAW, :].rearrange("p (j h e) -> p j h e", j=2, h=H), AX.X, ALU.add), "summed",
                     wait=False)
            dve.wait_ge(S("root_ready"), 1)
            step(nc.vector.reciprocal(ssq[:], ssq[:]), "rinv_ready", wait=False)
            dve.wait_ge(S("rT_done"), 1)
            for half in range(2):
                step(nc.vector.tensor_copy(rT[:, 512 * half:512 * half + 512], bank[4 + half][0:32, :]))
            for half in range(2):
                at = slice(512 * half, 512 * half + 512)
                dve.wait_ge(S("nope_done"), half + 1)
                step(tt(sc[:, at], rT[:, at], bank[half][0:32, :], ALU.mult))
                dve.wait_ge(S("rope_done"), half + 1)
                step(tt(sc[:, at], sc[:, at], bank[2 + half][0:32, :], ALU.add))
            step(red(mx[:], sc[:], AX.X, ALU.max))
            step(nc.vector.tensor_scalar(sc[:], sc[:], mx[:], None, ALU.subtract), "shift", wait=False)
            dve.wait_ge(S("exp_done"), 1)
            step(red(mx[:], sc[:], AX.X, ALU.add))
            step(nc.vector.reciprocal(mx[:], mx[:]))
            step(nc.vector.tensor_scalar(sc[:], sc[:], mx[:], None, ALU.mult), "p_ready")
            dve.wait_ge(S("rep_done"), 1)
            step(nc.vector.tensor_copy(own[:], bank[6][0:32, 0:RANK]))
            dve.wait_ge(S("pT_done"), 1)
            step(nc.vector.tensor_copy(pT[:].rearrange("p a b -> p (a b)"), bank[7][:, 0:PAGES * 32]))
            for p in range(PAGES):
                last = tt(pblk[:, p], C("m832", N, 32), pT[:, p].unsqueeze(1).to_broadcast([P, N, 32]), ALU.mult)
                step(last, *(["pblk_ready"] if p == PAGES - 1 else []))
            dve.wait_ge(S("lat_done"), 1)
            step(nc.vector.scalar_tensor_tensor(lat[:], own[:], sc[:, PAGES * P:], bank[5][0:32, 0:RANK], ALU.mult,
                                                ALU.add), "lat_ready", wait=False)
            dve.wait_ge(S("latT_done"), 1)
            step(nc.vector.tensor_copy(latT[:, :, NP_TOK:T], bank[4][:, 0:32].rearrange("p (n h) -> p h n", h=H)),
                 "latT_ready", wait=False)


def gdn(nc, A, E, l):
    zT, tm, brT, bank, C, V, R, ones = (E[k] for k in ("zT", "tm", "brT", "bank", "C", "V", "R", "ones"))
    N = NS_TOK
    GS = 3 * HD + 2
    with E["Phase"]("gdn") as ph:
        S = ph.sem
        y = ph.sb("y", [P, 6, T])
        sq = ph.sb("sq", [P, 4, T])
        buf = ph.sb("buf", [P, 6, 3, N])
        gb = ph.sb("gb", [P, 2, 3, H])
        e1 = ph.sb("e1", [P, 2, 3, H])
        sp1 = ph.sb("sp1", [P, 3, 3, H])
        alog = ph.sb("alog", [P, H])
        G = ph.sb("G", [P, 2, H])
        wG = ph.sb("wG", [P, 3, 2, H])
        rep = ph.sb("rep", [P, 2, 2, H, P])
        D = ph.sb("D", [P, 2, H, P])
        EG = ph.sb("EG", [P, 2, H, P])
        bB = ph.sb("bB", [P, 2, H, P])
        AT = ph.sb("AT", [P, 2, H, P])
        PT = ph.sb("PT", [P, 2, H, P])
        MT = ph.sb("MT", [P, 2, H, P])
        P1 = ph.sb("P1", [P, 2, H, P])
        X = ph.sb("X", [P, 2, H, P])
        XT = ph.sb("XT", [P, 2, H, P])
        qg = ph.sb("qg", [P, 2, NP_TOK])
        kv = ph.sb("kv", [P, 2, 512])
        ST = ph.sb("ST", [P, 2, HD])
        Rr = ph.sb("Rr", [P, 2, H, HD])
        u = ph.sb("u", [P, 2, H, HD])
        oT = ph.sb("oT", [P, 2, T])
        osq = ph.sb("osq", [P, 2, T])
        zg = ph.sb("zg", [P, 2, T])
        gs = ph.sb("gs", [N, H, GS])
        rs = ph.sb("rs", [P, GS])
        st = ph.sb("st", [P, 16, HD])
        pr = ph.sb("pr", [P, 16, HD])
        v16 = ph.sb("v16", [P, 4, 16])
        sc1 = ph.sb("sc1", [P, 2])
        oX = ph.sb("oX", [P, 16, 16])
        raw = zT[:, FM_QKV:FM_QKV + 6, :]
        ident = C("ident")

        def by_parity(a, par):
            return a.rearrange("p (a b) t -> p b a t", b=2)[:, par]

        @ph.b.sync
        def _(sp):
            sp.dma_start(buf[:], A["sconv"][l]).then_inc(S("buf_loaded"), 16)
            sp.dma_start(st[:], A["sgdn"][l]).then_inc(S("state_loaded"), 16)
            sp.dma_start(A["o_conv"][l], raw[:, :, NP_TOK - 3:NP_TOK]).then_inc(S("stored"), 16)
            sp.dma_start(A["o_convs"][l, :, :, 2, :], raw[:, :, NP_TOK:T]).then_inc(S("stored"), 16)
            sp.wait_ge(S("buf_loaded"), 16)
            for i in range(2):
                sp.dma_start(A["o_convs"][l, :, :, i, :], buf[:, :, i + 1, :]).then_inc(S("stored"), 16)
            sp.wait_ge(S("state_s_ready"), 1)
            sp.dma_start(A["o_gdns"][l], st[:]).then_inc(S("stored"), 16)
            sp.wait_ge(S("state_ready"), 8)
            sp.dma_start(A["o_gdn"][l], ST[:]).then_inc(S("stored"), 16)
            sp.wait_ge(S("stored"), 96)

        @ph.b.tensor
        def _(pe):
            pe.wait_ge(S("sq_ready"), 1)
            for t in range(4):
                mm = pe.matmul(bank[t][:, 0:T], C("blk"), sq[:, t, :], start=True, stop=True)
            mm.then_inc(S("ss_done"), 1)
            pe.wait_ge(S("gb_ready"), 3)
            for j in range(2):
                mm = pe.matmul(bank[4 + j][:, 0:H], C("tri"), gb[:, 1, j, :], start=True, stop=True)
            mm.then_inc(S("G_done"), 1)
            pe.wait_ge(S("rep_ready"), 4)
            pe.wait_ge(S("G_ready"), 2)
            pe.wait_ge(S("roots_taken"), 4)
            pe.wait_ge(S("qk_ready"), 2)
            for j in range(2):
                for h in range(H):
                    pe.matmul(bank[4 * j][:, P * h:P * h + P], rep[:, 1, j, h, :], C("tri"), start=True, stop=True)
                for h in range(H):
                    mm = pe.matmul(bank[4 * j + 1][:, P * h:P * h + P], rep[:, 0, j, h, :], ident, start=True,
                                   stop=True)
                mm.then_inc(S("rows_done"), 1)
                for h in range(H):
                    o, a, c = HD * (h % 2), h // 2, slice(P * j, P * j + P)
                    for i in range(2):
                        mm = pe.matmul(bank[4 * j + 2 + h % 2][:, P * (2 * i + a):P * (2 * i + a) + P],
                                       y[o:o + HD, 2 + a, c], y[o:o + HD, 2 * (1 - i) + a, c], start=True, stop=True)
                    mm.then_inc(S("kq_done"), 1)
            for j in range(2):
                pe.wait_ge(S(f"mt{j}_ready"), 1)
                pe.wait_ge(S("kq_read"), 8)
                for h in range(H):
                    mm = pe.matmul(bank[4 * j][:, P * h:P * h + P], MT[:, j, h, :], ident, start=True, stop=True)
                mm.then_inc(S(f"p1{j}_done"), 1)
            with pe.Fori(1, 7) as k:
                for j in range(2):
                    pe.wait_ge(S(f"mt{j}_ready"), k + 1)
                    pe.wait_ge(S(f"x{j}_ready"), 2 * k)
                    for h in range(H):
                        mm = pe.matmul(bank[4 * j][:, P * h:P * h + P], MT[:, j, h, :], X[:, j, h, :], start=True,
                                       stop=True)
                    mm.then_inc(S(f"p1{j}_done"), 1)
                for j in range(2):
                    pe.wait_ge(S(f"p1{j}_copied"), k)
                    for h in range(H):
                        mm = pe.matmul(bank[4 * j + 1][:, P * h:P * h + P], XT[:, j, h, :], P1[:, j, h, :],
                                       start=True, stop=True)
                    for h in range(H):
                        mm = pe.matmul(bank[4 * j + 2][:, P * h:P * h + P], P1[:, j, h, :], XT[:, j, h, :],
                                       start=True, stop=True)
                    mm.then_inc(S(f"xp{j}_done"), 1)
            pe.wait_ge(S("x0_ready"), 14)
            pe.wait_ge(S("x1_ready"), 14)
            for j in range(2):
                for i in range(4):
                    mm = pe.transpose(bank[j][:, P * i:P * i + P], y[:, 2 + i, P * j:P * j + P], ident)
                mm.then_inc(S("kvT_done"), 1)
            for i in range(6):
                mm = pe.transpose(bank[2 + i // 4][0:N, P * (i % 4):P * (i % 4) + P], y[:, i, NP_TOK:T], ident)
            mm.then_inc(S("sT_done"), 1)
            pe.wait_ge(S("gs_ready"), 4)
            for h in range(H):
                mm = pe.matmul(bank[7][:, 0:GS], C("selg", H, P)[0:N, h, :], gs[:, h, :], start=h == 0,
                               stop=h == H - 1)
            mm.then_inc(S("rs_done"), 1)
            pe.wait_ge(S("kv_ready"), 2)
            pe.wait_ge(S("qg_ready"), 8)
            for j in range(2):
                c = slice(P * j, P * j + P)
                pe.wait_ge(S("state_ready"), 4 * j) if j else pe.wait_ge(S("state_zeroed"), 1)
                for h in range(H):
                    o, a = HD * (h % 2), h // 2
                    mm = pe.matmul(bank[h % 2][:, HD * a:HD * a + HD], y[o:o + HD, 2 + a, c], ST[o:o + HD, a, :],
                                   start=True, stop=True)
                mm.then_inc(S("kS_done"), 1)
                if j:
                    pe.wait_ge(S("o_read"), 2)
                for h in range(H):
                    o, a = HD * (h % 2), h // 2
                    mm = pe.matmul(bank[3 + h % 2][o:o + HD, P * a:P * a + P], ST[o:o + HD, a, :], qg[o:o + HD, a, c],
                                   start=True, stop=True)
                pe.wait_ge(S("R_ready"), j + 1)
                for h in range(H):
                    mm = pe.matmul(bank[2][:, HD * h:HD * h + HD], XT[:, j, h, :], Rr[:, j, h, :], start=True,
                                   stop=True)
                mm.then_inc(S("u_done"), 1)
                pe.wait_ge(S("u_ready"), 2 * j + 1)
                for h in range(H):
                    o, a = HD * (h % 2), h // 2
                    mm = pe.matmul(bank[5][o:o + HD, P * a:P * a + P], u[:, 0, h, :], PT[:, j, h, :], start=True,
                                   stop=True)
                mm.then_inc(S("o_done"), 1)
                pe.wait_ge(S("u_ready"), 2 * j + 2)
                for h in range(H):
                    o, a = HD * (h % 2), h // 2
                    mm = pe.matmul(bank[6][o:o + HD, HD * a:HD * a + HD], kv[:, j, HD * h:HD * h + HD],
                                   u[:, 1, h, :], start=True, stop=True)
                mm.then_inc(S("ku_done"), 1)
            pe.wait_ge(S("oX_ready"), 1)
            for t in range(2):
                mm = pe.matmul(bank[7][:, N * t:N * t + N], oX[:, 8 * t:8 * t + 8, :].rearrange("p a b -> p (a b)"),
                               C("seln"), start=True, stop=True)
            mm.then_inc(S("os_done"), 1)
            pe.wait_ge(S("osq_ready"), 1)
            for t in range(2):
                mm = pe.matmul(bank[t][:, 0:T], C("blk"), osq[:, t, :], start=True, stop=True)
            mm.then_inc(S("oss_done"), 1)

        @ph.b.scalar
        def _(act):
            eps = E["epsc"][:]
            act.wait_ge(S("conv_ready"), 1)
            nc.scalar.activation(y[:], y[:], ACT.Silu).then_inc(S("silu_done"), 1)
            nc.scalar.activation(zg[:], zT[:, FM_ZG:FM_ZG + 2, :], ACT.Silu)
            act.wait_ge(S("ss_done"), 1)
            for t in range(4):
                nc.scalar.activation(sq[:, t, :], bank[t][:, 0:T], ACT.Sqrt, bias=eps).then_inc(S("roots_taken"), 1)
            act.wait_ge(S("neg_ready"), 2)
            nc.scalar.activation(e1[:], e1[:], ACT.Exp, scale=-1.0).then_inc(S("e1_done"), 1)
            nc.scalar.activation(alog[:], R("a_log"), ACT.Exp).then_inc(S("e1_done"), 1)
            act.wait_ge(S("one_plus_ready"), 2)
            nc.scalar.activation(sp1[:, 1], sp1[:, 0], ACT.Ln).then_inc(S("ln_done"), 1)
            for j in range(2):
                act.wait_ge(S("rows_done"), j + 1)
                nc.scalar.activation(EG[:, j].rearrange("p h t -> p (h t)"), bank[4 * j][:], ACT.Exp)\
                    .then_inc(S("EG_done"), 1)
                nc.scalar.copy(bB[:, j].rearrange("p h t -> p (h t)"), bank[4 * j + 1][:]).then_inc(S("bB_done"), 1)
                act.wait_ge(S("D_shifted"), j + 1)
                nc.scalar.activation(D[:, j], D[:, j], ACT.Exp).then_inc(S("D_done"), 1)
            act.wait_ge(S("wG_shifted"), 2)
            nc.scalar.activation(wG[:, 2], wG[:, 2], ACT.Exp).then_inc(S("wG_done"), 1)
            nc.scalar.activation(wG[:, 0], G[:], ACT.Exp).then_inc(S("wG_done"), 1)
            nc.scalar.activation(e1[:, 1], gb[:, 1], ACT.Exp).then_inc(S("wG_done"), 1)
            with act.Fori(1, 7) as k:
                for j in range(2):
                    act.wait_ge(S(f"p1{j}_done"), k + 1)
                    nc.scalar.copy(P1[:, j].rearrange("p h t -> p (h t)"), bank[4 * j][:])\
                        .then_inc(S(f"p1{j}_copied"), 1)
            for j in range(2):
                act.wait_ge(S("kvT_done"), j + 1)
                nc.scalar.copy(kv[:, j], bank[j][:]).then_inc(S("kv_ready"), 1)
            act.wait_ge(S("oss_done"), 1)
            for t in range(2):
                nc.scalar.activation(osq[:, t, :], bank[t][:, 0:T], ACT.Sqrt, bias=eps, scale=1.0 / HD)\
                    .then_inc(S("oroot_ready"), 1)

        @ph.b.vector
        def _(dve):
            step = E["stepper"](ph, dve, "dve_step")
            v = nc.vector
            tt, ts, stt, red = v.tensor_tensor, v.tensor_scalar, v.scalar_tensor_tensor, v.tensor_reduce
            for t in range(6):
                step(ts(y[:, t, :], raw[:, t, :], V("conv", 18 + t), None, ALU.mult), wait=t == 5)
            for i in range(1, 4):
                for t in range(6):
                    step(stt(y[:, t, i:NP_TOK], raw[:, t, 0:NP_TOK - i], V("conv", 6 * (3 - i) + t),
                             y[:, t, i:NP_TOK], ALU.mult, ALU.add), wait=t == 5)
            dve.wait_ge(S("buf_loaded"), 16)
            for i in range(3):
                for t in range(6):
                    last = stt(y[:, t, NP_TOK:T], buf[:, t, i, :], V("conv", 6 * i + t), y[:, t, NP_TOK:T], ALU.mult,
                               ALU.add)
                    if i == 2 and t == 5:
                        step(last, "conv_ready", wait=False)
                    else:
                        step(last, wait=t == 5)
            dve.wait_ge(S("silu_done"), 1)
            step(tt(sq[:], y[:, 0:4, :], y[:, 0:4, :], ALU.mult), "sq_ready", wait=False)
            step(v.tensor_copy(e1[:, 0], tm[:, :, TM_BETA:TM_BETA + H]), "neg_ready")
            step(tt(gb[:, 1], tm[:, :, TM_ALPHA:TM_ALPHA + H], R("dt").unsqueeze(1).to_broadcast([P, 3, H]), ALU.add))
            step(ts(sp1[:, 0], gb[:, 1], -1.0, None, ALU.mult))
            step(tt(e1[:, 1], gb[:, 1], sp1[:, 0], ALU.max), "neg_ready")
            dve.wait_ge(S("e1_done"), 2)
            step(ts(sp1[:, 0], e1[:, 1], 1.0, None, ALU.add), "one_plus_ready")
            step(ts(gb[:, 0], e1[:, 0], 1.0, None, ALU.add), "one_plus_ready")
            step(v.reciprocal(gb[:, 0], gb[:, 0]), "gb_ready")
            step(ts(sp1[:, 2], sp1[:, 0], -1.0, None, ALU.add))
            dve.wait_ge(S("ln_done"), 1)
            step(ts(sp1[:, 0], sp1[:, 2], 1e-30, None, ALU.max))
            step(v.reciprocal(sp1[:, 0], sp1[:, 0]))
            step(tt(sp1[:, 1], sp1[:, 1], sp1[:, 0], ALU.mult))
            step(ts(sp1[:, 2], sp1[:, 2], 0.0, None, ALU.is_equal))
            step(tt(sp1[:, 1], sp1[:, 1], sp1[:, 2], ALU.add))
            step(tt(sp1[:, 1], sp1[:, 1], e1[:, 1], ALU.mult))
            step(stt(gb[:, 1], gb[:, 1], 0.0, sp1[:, 1], ALU.max, ALU.add), "gb_ready")
            step(stt(gb[:, 1], gb[:, 1], -1.0, alog[:].unsqueeze(1).to_broadcast([P, 3, H]), ALU.mult, ALU.mult),
                 "gb_ready")
            for i in range(2):
                for j in range(2):
                    step(v.tensor_copy(rep[:, i, j], gb[:, i, j].unsqueeze(2).to_broadcast([P, H, P])), "rep_ready",
                         wait=False)
            dve.wait_ge(S("roots_taken"), 4)
            step(v.reciprocal(sq[:], sq[:]))
            step(stt(y[:, 0:2, :], y[:, 0:2, :], HD ** -0.5, sq[:, 0:2, :], ALU.mult, ALU.mult), "qk_ready",
                 wait=False)
            step(tt(y[:, 2:4, :], y[:, 2:4, :], sq[:, 2:4, :], ALU.mult), "qk_ready")
            dve.wait_ge(S("G_done"), 1)
            for j in range(2):
                step(v.tensor_copy(G[:, j], bank[4 + j][:, 0:H]), "G_ready")
            for j in range(2):
                dve.wait_ge(S("rows_done"), j + 1)
                g4 = bank[4 * j][:].rearrange("p (h t) -> p h t", h=H)
                dve.wait_ge(S("EG_done"), j + 1)
                step(tt(D[:, j], g4, G[:, j].unsqueeze(2).to_broadcast([P, H, P]), ALU.subtract))
                step(tt(wG[:, 2, j], g4[:, :, P - 1], G[:, j], ALU.subtract), "wG_shifted")
                step(ts(D[:, j], D[:, j], 0.0, None, ALU.min), "D_shifted", wait=False)
                dve.wait_ge(S("D_done"), j + 1)
                step(tt(D[:, j], D[:, j], C("tri").unsqueeze(1).to_broadcast([P, H, P]), ALU.mult))
                dve.wait_ge(S("bB_done"), j + 1)
                dve.wait_ge(S("kq_done"), 4 * j + 4)
                for par in range(2):
                    kq = bank[4 * j + 2 + par][:].rearrange("p (i a t) -> p i a t", i=2, a=2)
                    step(tt(by_parity(AT[:, j], par), kq[:, 0], by_parity(D[:, j], par), ALU.mult), "kq_read")
                    step(tt(by_parity(PT[:, j], par), kq[:, 1], by_parity(D[:, j], par), ALU.mult), "kq_read")
                step(tt(AT[:, j], AT[:, j], bB[:, j], ALU.mult))
                step(tt(MT[:, j], AT[:, j], C("lev", 7, P)[:, 0:1].to_broadcast([P, H, P]), ALU.mult),
                     f"mt{j}_ready")
            eye = ident.unsqueeze(1).to_broadcast([P, H, P])
            for j in range(2):
                step(tt(XT[:, j], eye, MT[:, j], ALU.subtract), f"x{j}_ready", wait=False)
                dve.wait_ge(S(f"p1{j}_done"), 1)
                step(tt(X[:, j], eye, bank[4 * j][:].rearrange("p (h t) -> p h t", h=H), ALU.subtract),
                     f"x{j}_ready", wait=False)
            with dve.Fori(1, 7) as k:
                for j in range(2):
                    dve.wait_ge(S(f"p1{j}_done"), k)
                    dve.wait_ge(S(f"x{j}_ready"), 2 * k)
                    tt(MT[:, j], AT[:, j], C("lev", 7, P)[:, bass.ds(k, 1)].to_broadcast([P, H, P]), ALU.mult)\
                        .then_inc(S(f"mt{j}_ready"), 1)
                for j in range(2):
                    dve.wait_ge(S(f"xp{j}_done"), k)
                    tt(X[:, j].rearrange("p h t -> p (h t)"), X[:, j].rearrange("p h t -> p (h t)"),
                       bank[4 * j + 1][:], ALU.subtract).then_inc(S(f"x{j}_ready"), 1)
                    tt(XT[:, j].rearrange("p h t -> p (h t)"), XT[:, j].rearrange("p h t -> p (h t)"),
                       bank[4 * j + 2][:], ALU.subtract).then_inc(S(f"x{j}_ready"), 1)
            dve.wait_ge(S("wG_done"), 3)
            step(tt(wG[:, 1], wG[:, 0], gb[:, 0, 0:2], ALU.mult))
            for j in range(2):
                for h in range(H):
                    o, a = HD * (h % 2), h // 2
                    c = slice(P * j, P * j + P)
                    step(tt(qg[o:o + HD, a, c], y[o:o + HD, a, c], EG[o:o + HD, j, h, :], ALU.mult), "qg_ready",
                         wait=False)
            step(v.memset(ST[:], 0.0), "state_zeroed")
            dve.wait_ge(S("sT_done"), 1)
            step(v.tensor_copy(gs[:, :, 0:2 * HD].rearrange("p h (s e) -> p h s e", s=2),
                               bank[2][0:N, :].rearrange("p (s h e) -> p h s e", s=2, h=H)), "gs_ready")
            step(v.tensor_copy(gs[:, :, 2 * HD:3 * HD], bank[3][0:N, 0:256].rearrange("p (h e) -> p h e", h=H)),
                 "gs_ready")
            step(v.tensor_copy(gs[:, :, 3 * HD], gb[0:N, 0, 2, :]), "gs_ready")
            step(v.tensor_copy(gs[:, :, 3 * HD + 1], e1[0:N, 1, 2, :]), "gs_ready")
            for j in range(2):
                dve.wait_ge(S("kv_ready"), j + 1)
                step(tt(Rr[:, j], kv[:, j, 256:512].rearrange("p (h e) -> p h e", h=H),
                        gb[:, 0, j].unsqueeze(2).to_broadcast([P, H, HD]), ALU.mult))
                dve.wait_ge(S("kS_done"), j + 1)
                for par in range(2):
                    w = wG[:, 1, j].rearrange("p (a b) -> p b a", b=2)[:, par].unsqueeze(2).to_broadcast([P, 2, HD])
                    step(tt(by_parity(u[:, 1], par), bank[par][:, 0:P].rearrange("p (a e) -> p a e", a=2), w,
                            ALU.mult))
                step(tt(Rr[:, j], Rr[:, j], u[:, 1], ALU.subtract), "R_ready", wait=False)
                dve.wait_ge(S("u_done"), j + 1)
                u4 = bank[2][:, 0:H * HD].rearrange("p (h e) -> p h e", h=H)
                step(v.tensor_copy(u[:, 0], u4), "u_ready", wait=False)
                step(tt(u[:, 1], u4, wG[:, 2, j].unsqueeze(2).to_broadcast([P, H, HD]), ALU.mult), "u_ready",
                     wait=False)
                dve.wait_ge(S("o_done"), j + 1)
                for par in range(2):
                    o = HD * par
                    p4 = bank[3 + par][o:o + HD, 0:256].rearrange("p (a t) -> p a t", a=2)
                    step(v.tensor_copy(oT[o:o + HD, :, P * j:P * j + P], p4))
                    step(tt(oT[o:o + HD, :, P * j:P * j + P], oT[o:o + HD, :, P * j:P * j + P],
                            bank[5][o:o + HD, 0:256].rearrange("p (a t) -> p a t", a=2), ALU.add), "o_read")
                dve.wait_ge(S("ku_done"), j + 1)
                for h in range(H):
                    o, a = HD * (h % 2), h // 2
                    step(stt(ST[o:o + HD, a, :], ST[o:o + HD, a, :], EG[o:o + HD, j, h, P - 1:P],
                             bank[6][o:o + HD, HD * a:HD * a + HD], ALU.mult, ALU.add), "state_ready")
            dve.wait_ge(S("rs_done"), 1)
            step(v.tensor_copy(rs[:], bank[7][:, 0:GS]))
            dve.wait_ge(S("state_loaded"), 16)
            qv, kvec, beta, eg = rs[:, 0:HD], rs[:, HD:2 * HD], rs[:, 3 * HD:3 * HD + 1], rs[:, 3 * HD + 1:GS]
            wide = [P, 16, HD]
            step(tt(v16[:], rs[:, 2 * HD:3 * HD].rearrange("p (a b) -> p a b", a=4),
                    C("mv").unsqueeze(2).to_broadcast([P, 4, 16]), ALU.mult))
            step(red(oX[:, 0, :], v16[:].rearrange("p a b -> p b a"), AX.X, ALU.add))
            step(tt(pr[:], st[:], kvec.unsqueeze(1).to_broadcast(wide), ALU.mult))
            step(red(v16[:, 0, :], pr[:], AX.X, ALU.add))
            step(tt(pr[:], st[:], qv.unsqueeze(1).to_broadcast(wide), ALU.mult))
            step(red(v16[:, 1, :], pr[:], AX.X, ALU.add))
            step(ts(v16[:, 0, :], v16[:, 0, :], eg, beta, ALU.mult, ALU.mult))
            step(stt(v16[:, 2, :], oX[:, 0, :], beta, v16[:, 0, :], ALU.mult, ALU.subtract))
            step(tt(pr[:, 0, :], qv, kvec, ALU.mult))
            step(red(sc1[:, 0:1], pr[:, 0, :], AX.X, ALU.add))
            step(ts(v16[:, 1, :], v16[:, 1, :], eg, None, ALU.mult))
            step(stt(v16[:, 3, :], v16[:, 2, :], sc1[:, 0:1], v16[:, 1, :], ALU.mult, ALU.add))
            step(tt(pr[:], v16[:, 2, :].unsqueeze(2).to_broadcast(wide), kvec.unsqueeze(1).to_broadcast(wide),
                    ALU.mult))
            step(stt(st[:].rearrange("p a b -> p (a b)"), st[:].rearrange("p a b -> p (a b)"), eg,
                     pr[:].rearrange("p a b -> p (a b)"), ALU.mult, ALU.add), "state_s_ready", wait=False)
            step(tt(oX[:], C("m16").unsqueeze(2).to_broadcast([P, 16, 16]),
                    v16[:, 3, :].unsqueeze(1).to_broadcast([P, 16, 16]), ALU.mult), "oX_ready")
            dve.wait_ge(S("os_done"), 1)
            step(v.tensor_copy(oT[:, :, NP_TOK:T], bank[7][:, 0:2 * N].rearrange("p (t n) -> p t n", t=2)))
            step(tt(osq[:], oT[:], oT[:], ALU.mult), "osq_ready", wait=False)
            dve.wait_ge(S("oroot_ready"), 2)
            step(v.reciprocal(osq[:], osq[:]))
            step(tt(oT[:], oT[:], osq[:], ALU.mult))
            step(stt(brT[:, 4:6, :], oT[:], V("gdn_g"), zg[:], ALU.mult, ALU.mult))


def mix(nc, A, E, l):
    xT, hT, brT, bank = (E[k] for k in ("xT", "hT", "brT", "bank"))
    with E["Phase"]("mix") as ph:
        S = ph.sem
        w = [ph.sb(f"w{b}", [P, KT + 2, P]) for b in range(4)]
        wo = [ph.sb(f"wo{i}", [P, KT, P]) for i in range(4)]
        gate = ph.sb("gate", [P, 4, T])
        mixT = ph.sb("mixT", [P, KT, T])

        @ph.b.sync
        def _(sp):
            for b in range(4):
                sp.dma_start(w[b][:], A["w_gb"][l, 0, b]).then_inc(S(f"w{b}_loaded"), 16)
            for i in range(4):
                sp.dma_start(wo[i][:], A["w_out"][l, i]).then_inc(S(f"wo{i}_loaded"), 16)
            with sp.Fori(1, KT) as dt:
                for b in range(4):
                    src = A["w_gb"][l, dt, b]
                    sp.wait_ge(S(f"p{b}_done"), dt)
                    sp.dma_start(w[b][:], src).then_inc(S(f"w{b}_loaded"), 16)
            for i in range(4):
                sp.wait_ge(S("o_done"), i + 1)
                sp.dma_start(wo[i][:], A["w_out"][l, 4 + i]).then_inc(S(f"wo{i}_loaded"), 16)

        @ph.b.tensor
        def _(pe):
            def tile(dt):
                for b in range(4):
                    pe.wait_ge(S(f"w{b}_loaded"), 16 * dt + 16)
                    if not isinstance(dt, int):
                        pe.wait_ge(S(f"g{b}_read"), dt)
                    for k in range(KT):
                        mm = pe.matmul(bank[b][:, 0:T], w[b][:, k, :], hT[:, k, :], start=k == 0, stop=k == KT - 1)
                    mm.then_inc(S(f"g{b}_done"), 1)
                    if not isinstance(dt, int):
                        pe.wait_ge(S(f"p{b}_read"), dt)
                    for k in range(2):
                        mm = pe.matmul(bank[4 + b][:, 0:T], w[b][:, KT + k, :], brT[:, 2 * b + k, :], start=k == 0,
                                       stop=k == 1)
                    mm.then_inc(S(f"p{b}_done"), 1)

            tile(0)
            with pe.Fori(1, KT) as dt:
                tile(dt)
            pe.wait_ge(S("mix_ready"), KT)
            for dt in range(KT):
                i = dt % 4
                pe.wait_ge(S(f"wo{i}_loaded"), 16 * (dt // 4) + 16)
                if dt >= 4:
                    pe.wait_ge(S("x_ready"), dt - 3)
                for k in range(KT):
                    mm = pe.matmul(bank[i][:, 0:T], wo[i][:, k, :], mixT[:, k, :], start=k == 0, stop=k == KT - 1)
                mm.then_inc(S("o_done"), 1)

        @ph.b.scalar
        def _(act):
            def tile(dt):
                for b in range(4):
                    act.wait_ge(S(f"g{b}_done"), dt + 1)
                    if not isinstance(dt, int):
                        act.wait_ge(S(f"p{b}_read"), dt)
                    nc.scalar.activation(gate[:, b, :], bank[b][:, 0:T], ACT.Sigmoid).then_inc(S(f"g{b}_read"), 1)

            tile(0)
            with act.Fori(1, KT) as dt:
                tile(dt)

        @ph.b.vector
        def _(dve):
            with dve.Fori(0, KT) as dt:
                for b in range(4):
                    dve.wait_ge(S(f"g{b}_read"), dt + 1)
                    dve.wait_ge(S(f"p{b}_done"), dt + 1)
                    nc.vector.tensor_tensor(gate[:, b, :], gate[:, b, :], bank[4 + b][:, 0:T], ALU.mult)\
                        .then_inc(S(f"m{b}_done"), 1)
                    if b == 1:
                        dve.wait_ge(S("m0_done"), dt + 1)
                        dve.wait_ge(S("m1_done"), dt + 1)
                        nc.vector.tensor_tensor(mixT[:, bass.ds(dt, 1), :].squeeze(1), gate[:, 0, :], gate[:, 1, :],
                                                ALU.add).then_inc(S("a1_done"), 1)
                    if b >= 2:
                        dve.wait_ge(S(f"m{b}_done"), dt + 1)
                        dve.wait_ge(S(f"a{b - 1}_done"), dt + 1)
                        nc.vector.tensor_tensor(mixT[:, bass.ds(dt, 1), :].squeeze(1),
                                                mixT[:, bass.ds(dt, 1), :].squeeze(1), gate[:, b, :], ALU.add)\
                            .then_inc(S(f"a{b}_done" if b < 3 else "mix_ready"), 1)
                dve.wait_ge(S("mix_ready"), dt + 1)
                for b in range(4):
                    dve.sem_inc(S(f"p{b}_read"), 1)
            for dt in range(KT):
                dve.wait_ge(S("o_done"), dt + 1)
                nc.vector.tensor_tensor(xT[:, dt, :], xT[:, dt, :], bank[dt % 4][:, 0:T], ALU.add)\
                    .then_inc(S("x_ready"), 1)


def route(nc, A, E, l):
    xT, hT, ones, bank, C, V, R = (E[k] for k in ("xT", "hT", "ones", "bank", "C", "V", "R"))
    with E["Phase"]("route") as ph:
        S = ph.sem
        sq = ph.sb("sq", [P, KT, T])
        rstd = ph.sb("rstd", [P, T])
        wrt = ph.sb("wrt", [P, KT, 36])
        lg = ph.sb("lg", [P, 3, 36])
        m = ph.sb("m", [P, 8, 3])
        eg = ph.sb("eg", [P, 3, 4])
        ohg = ph.sb("ohg", [P, 3, 4])
        sel = ph.sb("sel", [P, 3, 4, 8])
        le = ph.sb("le", [P, 3, 8])
        oh = [ph.sb(f"oh{i}", [P, 3, 8]) for i in range(2)]
        comb = ph.sb("comb", [P, 3, 4, 8])
        combT = ph.sb("combT", [32, T])

        @ph.b.sync
        def _(sp):
            sp.dma_start(wrt[:], A["w_rt"][l]).then_inc(S("wrt_loaded"), 16)
            sp.wait_ge(S("combT_ready"), 1)
            sp.dma_start(A["combT"], combT[:]).then_inc(S("combT_stored"), 16)
            sp.wait_ge(S("combT_stored"), 16)

        @ph.b.tensor
        def _(pe):
            pe.wait_ge(S("sq_ready"), 1)
            for k in range(KT):
                mm = pe.matmul(bank[0][:, 0:T], ones[:], sq[:, k, :], start=k == 0, stop=k == KT - 1)
            mm.then_inc(S("ss_done"), 1)
            pe.wait_ge(S("wrt_loaded"), 16)
            pe.wait_ge(S("h_ready"), KT)
            for c, (t0, n) in enumerate(CHUNKS):
                for k in range(KT):
                    mm = pe.matmul(bank[1 + c][0:n, 0:36], hT[:, k, t0:t0 + n], wrt[:, k, :], start=k == 0,
                                   stop=k == KT - 1)
                mm.then_inc(S("lg_done"), 1)
            pe.wait_ge(S("comb_ready"), 1)
            for c, (t0, n) in enumerate(CHUNKS):
                mm = pe.transpose(bank[4][0:32, t0:t0 + n], comb[0:n, c].rearrange("p g e -> p (g e)"),
                                  C("ident")[0:n, 0:n])
            mm.then_inc(S("combT_done"), 1)

        @ph.b.scalar
        def _(act):
            act.wait_ge(S("ss_done"), 1)
            nc.scalar.activation(rstd[:], bank[0][:, 0:T], ACT.Sqrt, bias=E["epsc"][:], scale=1.0 / D_MODEL)\
                .then_inc(S("root_ready"), 1)
            act.wait_ge(S("eg_shifted"), 1)
            nc.scalar.activation(eg[:], eg[:], ACT.Exp).then_inc(S("exp_done"), 1)
            act.wait_ge(S("p2_shifted"), 1)
            nc.scalar.activation(m[:, 5], m[:, 5], ACT.Exp).then_inc(S("exp_done"), 1)

        @ph.b.vector
        def _(dve):
            step = E["stepper"](ph, dve, "dve_step")
            v = nc.vector
            tt, ts, stt, red = v.tensor_tensor, v.tensor_scalar, v.scalar_tensor_tensor, v.tensor_reduce
            step(tt(sq[:], xT[:], xT[:], ALU.mult), "sq_ready", wait=False)
            step(v.memset(lg[:], 0.0))
            dve.wait_ge(S("root_ready"), 1)
            step(v.reciprocal(rstd[:], rstd[:]))
            for k in range(KT):
                step(stt(hT[:, k, :], xT[:, k, :], V("g2", k), rstd[:], ALU.mult, ALU.mult), "h_ready", wait=False)
            for c, (t0, n) in enumerate(CHUNKS):
                dve.wait_ge(S("lg_done"), c + 1)
                step(tt(lg[0:n, c, :], bank[1 + c][0:n, 0:36], R("moe_b")[0:n], ALU.add))

            def first_max(onehot, x, top, at, n):
                wide = [P, 3, n]
                step(red(top, x, AX.X, ALU.max))
                step(tt(onehot, x, top.unsqueeze(2).to_broadcast(wide), ALU.is_equal))
                step(tt(onehot, onehot, C("rev")[:, 0:n].unsqueeze(1).to_broadcast(wide), ALU.mult))
                step(red(at, onehot, AX.X, ALU.max))
                step(tt(onehot, onehot, at.unsqueeze(2).to_broadcast(wide), ALU.is_equal))

            lgg = lg[:, :, 0:4]
            first_max(ohg[:], lgg, m[:, 0], m[:, 1], 4)
            step(tt(eg[:], lgg, m[:, 0].unsqueeze(2).to_broadcast([P, 3, 4]), ALU.subtract), "eg_shifted",
                 wait=False)
            step(tt(sel[:], lg[:, :, 4:36].rearrange("p c (g e) -> p c g e", g=4),
                    ohg[:].unsqueeze(3).to_broadcast([P, 3, 4, 8]), ALU.mult))
            step(red(le[:], sel[:].rearrange("p c g e -> p c e g"), AX.X, ALU.add))
            first_max(oh[0][:], le[:], m[:, 2], m[:, 1], 8)
            step(stt(le[:], oh[0][:], NEG, le[:], ALU.mult, ALU.add))
            first_max(oh[1][:], le[:], m[:, 3], m[:, 1], 8)
            step(tt(m[:, 5], m[:, 3], m[:, 2], ALU.subtract), "p2_shifted", wait=False)
            dve.wait_ge(S("exp_done"), 2)
            step(red(m[:, 4], eg[:], AX.X, ALU.add))
            step(ts(m[:, 6], m[:, 5], 1.0, None, ALU.add))
            step(tt(m[:, 6], m[:, 6], m[:, 4], ALU.mult))
            step(v.reciprocal(m[:, 6], m[:, 6]))
            step(tt(m[:, 7], m[:, 6], m[:, 5], ALU.mult))
            for i in range(2):
                step(tt(oh[i][:], oh[i][:], m[:, 6 + i].unsqueeze(2).to_broadcast([P, 3, 8]), ALU.mult))
            step(tt(le[:], oh[0][:], oh[1][:], ALU.add))
            for c in range(3):
                step(tt(comb[:, c], ohg[:, c].unsqueeze(2).to_broadcast([P, 4, 8]),
                        le[:, c].unsqueeze(1).to_broadcast([P, 4, 8]), ALU.mult),
                     *(["comb_ready"] if c == 2 else []))
            dve.wait_ge(S("combT_done"), 1)
            step(v.tensor_copy(combT[:], bank[4][0:32, 0:T]), "combT_ready", wait=False)


def experts(nc, A, E, l):
    xT, hT, bank = (E[k] for k in ("xT", "hT", "bank"))
    NE, FT = 32, 2
    with E["Phase"]("moe") as ph:
        S = ph.sem
        wg = [ph.sb(f"wg{s}", [P, KT, FT * P]) for s in range(2)]
        wu = [ph.sb(f"wu{s}", [P, KT, FT * P]) for s in range(2)]
        wd = [ph.sb(f"wd{s}", [P, FT, D_MODEL]) for s in range(2)]
        cb = [ph.sb(f"cb{s}", [P, T]) for s in range(2)]
        sg = [ph.sb(f"sg{s}", [P, FT, T]) for s in range(2)]
        up = [ph.sb(f"up{s}", [P, FT, T]) for s in range(2)]
        zero = ph.sb("zero", [P, 1])

        @ph.b.sync
        def _(sp):
            def load(e, s):
                sp.dma_start(wg[s][:], A["w_g"][l, e]).then_inc(S(f"gu{s}_loaded"), 16)
                sp.dma_start(wu[s][:], A["w_u"][l, e]).then_inc(S(f"gu{s}_loaded"), 16)

            for s in range(2):
                load(s, s)
            with sp.Fori(1, NE // 2) as i:
                for s in range(2):
                    g, u = A["w_g"][l, 2 * i + s], A["w_u"][l, 2 * i + s]
                    sp.wait_ge(S("u_done"), 4 * i + 2 * s - 2)
                    sp.dma_start(wg[s][:], g).then_inc(S(f"gu{s}_loaded"), 16)
                    sp.dma_start(wu[s][:], u).then_inc(S(f"gu{s}_loaded"), 16)

        @ph.b.tensor
        def _(pe):
            def gate_up(i, s, first=False):
                e = 2 * i + s
                pe.wait_ge(S(f"gu{s}_loaded"), 32 * i + 32)
                for f in range(FT):
                    if not first:
                        pe.wait_ge(S("up_read"), 2 * e + f - 1)
                    for j, w in enumerate((wg[s], wu[s])):
                        for k in range(KT):
                            mm = pe.matmul(bank[2 * f + j][:, 0:T], w[:, k, P * f:P * f + P], hT[:, k, :],
                                           start=k == 0, stop=k == KT - 1)
                        mm.then_inc(S(("g_done", "u_done")[j]), 1)

            def down(i, s):
                e = 2 * i + s
                pe.wait_ge(S(f"d{s}_loaded"), 16 * i + 16)
                pe.wait_ge(S("act_ready"), 2 * e + 2)
                for dt in range(KT):
                    pe.wait_ge(S("y_bank_free"), 8 * e + dt + 1)
                    for f in range(FT):
                        mm = pe.matmul(bank[4 + dt % 4][:, 0:T], wd[s][:, f, P * dt:P * dt + P], sg[s][:, f, :],
                                       start=f == 0, stop=f == FT - 1)
                    mm.then_inc(S("y_done"), 1)

            gate_up(0, 0, first=True)
            with pe.Fori(0, NE // 2 - 1) as i:
                gate_up(i, 1)
                down(i, 0)
                gate_up(i + 1, 0)
                down(i, 1)
            gate_up(NE // 2 - 1, 1)
            down(NE // 2 - 1, 0)
            down(NE // 2 - 1, 1)

        @ph.b.scalar
        def _(act):
            def silu(i, s, first=False):
                e = 2 * i + s
                c, d = A["combT"][e].partition_broadcast(P), A["w_d"][l, e]
                if not first:
                    act.wait_ge(S("act_ready"), 2 * e - 2)
                act.dma_start(cb[s][:], c).then_inc(S(f"cb{s}_loaded"), 16)
                if not first:
                    act.wait_ge(S("y_done"), 8 * e - 8)
                act.dma_start(wd[s][:], d).then_inc(S(f"d{s}_loaded"), 16)
                for f in range(FT):
                    act.wait_ge(S("g_done"), 2 * e + f + 1)
                    if not first:
                        act.wait_ge(S("y_done"), 8 * e - 8)
                    nc.scalar.activation(sg[s][:, f, :], bank[2 * f][:, 0:T], ACT.Silu).then_inc(S("silu_done"), 1)

            for s in range(2):
                silu(0, s, first=True)
            with act.Fori(1, NE // 2) as i:
                for s in range(2):
                    silu(i, s)

        @ph.b.vector
        def _(dve):
            nc.vector.memset(zero[:], 0.0).then_inc(S("y_bank_free"), 4)

            def gated(i, s):
                e = 2 * i + s
                dve.wait_ge(S(f"cb{s}_loaded"), 16 * i + 16)
                for f in range(FT):
                    dve.wait_ge(S("u_done"), 2 * e + f + 1)
                    dve.wait_ge(S("silu_done"), 2 * e + f + 1)
                    nc.vector.tensor_tensor(up[s][:, f, :], bank[2 * f + 1][:, 0:T], cb[s][:], ALU.mult)\
                        .then_inc(S("up_read"), 1)
                for f in range(FT):
                    dve.wait_ge(S("up_read"), 2 * e + f + 1)
                    last = nc.vector.tensor_tensor(sg[s][:, f, :], sg[s][:, f, :], up[s][:, f, :], ALU.mult)
                    last.then_inc(S("act_ready"), 1)

            def add(i, s):
                e = 2 * i + s
                for dt in range(KT):
                    dve.wait_ge(S("y_done"), 8 * e + dt + 1)
                    nc.vector.tensor_tensor(xT[:, dt, :], xT[:, dt, :], bank[4 + dt % 4][:, 0:T], ALU.add)\
                        .then_inc(S("y_bank_free"), 1)

            gated(0, 0)
            with dve.Fori(0, NE // 2 - 1) as i:
                gated(i, 1)
                add(i, 0)
                gated(i + 1, 0)
                add(i, 1)
            gated(NE // 2 - 1, 1)
            add(NE // 2 - 1, 0)
            add(NE // 2 - 1, 1)


PHASES = [project, gmlp, gdn, mla, memory, mix, route, experts]

OUTS = dict(
    o_x=(P, KT, T), o_ckv=(DEPTH, P, 3, RANK), o_kr=(DEPTH, P, 3, ROPE), o_gdn=(DEPTH, P, 2, HD),
    o_conv=(DEPTH, P, 6, 3), o_mem=(DEPTH, P, 2, 2, MEM), o_gdns=(DEPTH, P, 16, HD),
    o_convs=(DEPTH, P, 6, 3, NS_TOK), o_gv=(DEPTH, NS_TOK, 256))


def arrange(I):
    f = np.ascontiguousarray
    L = DEPTH
    w_in = I["w_in"].reshape(L, KT, P, -1).transpose(0, 2, 1, 3)
    off = dict(u=0, v=256, cq=512, ckv=768, kr=896, qkv=928, zg=1696, b=1952, alpha=1956, mq=1960, gate=2216)

    def cols(name, n):
        return w_in[..., off[name]:off[name] + n]

    fm = np.concatenate([cols("u", 256), cols("cq", 256), cols("qkv", 768), cols("zg", 256), cols("mq", 256)], -1)
    gate = cols("gate", 4096).reshape(L, P, KT, 4, KT, P)
    part = lambda a, n: a.reshape(L, n, P).transpose(0, 2, 1)
    twice = lambda a: np.concatenate([a, a], -1)[..., None]
    rep = lambda a: np.repeat(a.reshape(L, 2, 2), HD, 2).transpose(0, 2, 1)
    return {
        "xT": f(np.concatenate([I["x_prompt"][0], I["x_sample"][:, 0]]).reshape(T, KT, P).transpose(2, 1, 0)),
        "memT": f(I["mem_prompt"][0].reshape(MEM, KT, P).transpose(2, 1, 0)),
        "cst": constants(),
        "vec": f(np.concatenate([
            part(I["norm1_g"], 8), part(I["mla_cq_g"], 2),
            I["gdn_conv_w"].reshape(L, 4, 6, P).transpose(0, 3, 1, 2).reshape(L, P, 24),
            twice(I["gdn_out_g"]), twice(I["mem_qn_g"]), part(I["mem_norm_g"], 8), part(I["norm2_g"], 8),
            rep(I["gm_ws"][:, :, 0, 0]), rep(I["gm_b"][:, :, 0]), twice(I["mla_kn_g"])], -1)),
        "row": f(np.concatenate([
            I["gm_norm_g"], I["mla_ckv_g"], I["mla_kr_g"], I["mla_qn_g"], I["mla_qr_g"], I["mla_kn_g"],
            I["mem_kn_g"], I["gdn_a_log"], I["gdn_dt_bias"], I["moe_bg"], I["moe_be"]], -1)),
        "w_tm": f(np.concatenate([cols("v", 256), cols("ckv", 128), cols("kr", 32), cols("b", 4),
                                  cols("alpha", 4)], -1)),
        "w_fm": f(fm.reshape(L, P, KT, FM_N, P).transpose(0, 3, 1, 2, 4)),
        "w_gb": f(np.concatenate([gate.transpose(0, 4, 3, 1, 2, 5),
                                  I["w_branch"].reshape(L, 4, 2, P, KT, P).transpose(0, 4, 1, 3, 2, 5)], 4)),
        "gm_ws": f(I["gm_ws"].transpose(0, 3, 1, 2)),
        "gm_b": f(I["gm_b"].reshape(L, 2, 2, P).transpose(0, 2, 1, 3)),
        "w_uq": f(I["mla_w_uq"].reshape(L, 2, P, H * QK).transpose(0, 2, 1, 3)),
        "w_uk": f(I["mla_w_uk"].reshape(L, P, H * HD)),
        "w_ukT": f(I["mla_w_uk"].transpose(0, 3, 2, 1)),
        "w_uv": f(I["mla_w_uv"].reshape(L, P, H * HD)),
        "ckv": f(I["cache_mla_ckv"]),
        "ckvT": f(I["cache_mla_ckv"].transpose(0, 1, 3, 2)),
        "krT": f(I["cache_mla_kr"].transpose(0, 1, 3, 2)),
        "pages": f(I["page_table"].reshape(1, NPG)),
        "sgdn": f(I["state_gdn"].reshape(L, P, 16, HD)),
        "sconv": f(I["state_conv"].reshape(L, NS_TOK, 3, 6, P).transpose(0, 4, 3, 2, 1)),
        "w_kv": f(I["mem_w_kv"].reshape(L, KT, P, 512).transpose(0, 2, 1, 3)),
        "memkT": f(I["cache_mem_k"].reshape(L, NS_TOK, MEM, 2, P).transpose(0, 4, 1, 3, 2)),
        "memv": f(I["cache_mem_v"].reshape(L, NS_TOK, 2, P, 256).transpose(0, 3, 1, 2, 4)),
        "w_out": f(I["w_out"].reshape(L, KT, P, KT, P).transpose(0, 3, 2, 1, 4)),
        "w_rt": f(np.concatenate([I["moe_wg"], I["moe_we"]], -1).reshape(L, KT, P, 36).transpose(0, 2, 1, 3)),
        "w_g": f(I["moe_w_gate"].reshape(L, 32, KT, P, 256).transpose(0, 1, 3, 2, 4)),
        "w_u": f(I["moe_w_up"].reshape(L, 32, KT, P, 256).transpose(0, 1, 3, 2, 4)),
        "w_d": f(I["moe_w_down"].reshape(L, 32, 2, P, D_MODEL).transpose(0, 1, 3, 2, 4)),
    }


def restore(r):
    L = DEPTH
    x = r["o_x"].transpose(2, 1, 0).reshape(T, D_MODEL)
    prompt = lambda a: a[:, :, 0:2].transpose(0, 2, 1, 3).reshape(L, 1, NP_TOK, -1)
    mem = r["o_mem"].transpose(2, 0, 3, 1, 4).reshape(2, L, 1, MEM, H, HD)
    gdn = r["o_gdn"].reshape(L, 2, HD, 2, HD).transpose(0, 3, 1, 4, 2).reshape(L, 1, H, HD, HD)
    out = (
        x[None, :NP_TOK], x[NP_TOK:, None], prompt(r["o_ckv"]), prompt(r["o_kr"]), gdn,
        r["o_conv"].transpose(0, 3, 2, 1).reshape(L, 1, 3, 768), mem[0], mem[1],
        r["o_ckv"][:, 0:NS_TOK, 2][:, :, None], r["o_kr"][:, 0:NS_TOK, 2][:, :, None],
        r["o_gdns"].reshape(L, NS_TOK, H, HD, HD),
        r["o_convs"].transpose(0, 4, 3, 2, 1).reshape(L, NS_TOK, 3, 768), r["o_gv"][:, :, None])
    return tuple(np.ascontiguousarray(a) for a in out)


def kernel(**inputs):
    import concourse.bacc as bacc
    from concourse.bass_utils import run_bass_kernel_spmd

    nc = bacc.Bacc("TRN2", target_bir_lowering=False, num_devices=1)
    arrays = arrange({k: np.asarray(v) for k, v in inputs.items()})
    A = {n: nc.dram_tensor("in_" + n, a.shape, mybir.dt.from_np(a.dtype), kind="ExternalInput").ap()
         for n, a in arrays.items()}
    for n, shape in OUTS.items():
        A[n] = nc.dram_tensor(n, shape, F32, kind="ExternalOutput").ap()
    A["combT"] = nc.dram_tensor("combT", (32, T), F32).ap()
    build(nc, A)
    return restore(run_bass_kernel_spmd(nc, [{"in_" + n: a for n, a in arrays.items()}], core_ids=[0]).results[0])
```

```python
from contextlib import ExitStack

import numpy as np

import concourse.bass as bass
from concourse import mybir

F32 = mybir.dt.float32
I32 = mybir.dt.int32
ALU = mybir.AluOpType
ACT = mybir.ActivationFunctionType
AX = mybir.AxisListType

P = 128
D_MODEL = 1024
KT = D_MODEL // P
DEPTH = 2
NP_TOK = 256
NS_TOK = 8
T = NP_TOK + NS_TOK
CHUNKS = ((0, P), (P, P), (NP_TOK, NS_TOK))
H = 4
HD = 64
ROPE = 32
QK = HD + ROPE
RANK = 128
PAGES = 8
NPG = NS_TOK * PAGES
POOL = 80
MEM = 256
EPS = 1e-6
FIRST_SEM = 110
NEG = -1e30
NE = 32
SLOTS = 2 * T
SCH = -(-SLOTS // P)
W = 128
ITEMS = NE + (SLOTS - NE) // W
assert ITEMS % 2 == 1
MLA_SCALE = QK ** -0.5
MEM_SCALE = HD ** -0.5

TM_V, TM_CKV, TM_KR, TM_BETA, TM_ALPHA, TM_W = 0, 256, 384, 416, 420, 424
FM_U, FM_CQ, FM_QKV, FM_ZG, FM_MQ, FM_N = 0, 2, 4, 10, 12, 14
GATE_TILES = 4 * KT

CONST_COLS = dict(ident=128, tri=128, blk=128, lev=7 * 128, causal=128, rope=96, m832=256, sel832=32,
                  selrow=8, qr=64, hsel=4, selg=512, mv=4, m16=16, seln=8, rev=8, mq=512,
                  stri=128, iota=SLOTS, valid=3, slot=SCH)
CONST_AT, _at = {}, 0
for _name, _n in CONST_COLS.items():
    CONST_AT[_name] = _at
    _at += _n
CONST_W = _at

VEC_COLS = dict(g1=8, cq_g=2, conv=24, gdn_g=1, mq_g=1, memn_g=8, g2=8, ws0=2, b0=2, kn_g=1)
VEC_AT, _at = {}, 0
for _name, _n in VEC_COLS.items():
    VEC_AT[_name] = _at
    _at += _n
VEC_W = _at

ROW_COLS = dict(gm_g=256, ckv_g=128, kr_g=32, qn_g=64, qr_g=32, kn_g=64, memk_g=64, a_log=4, dt=4,
                moe_b=36)
ROW_AT, _at = {}, 0
for _name, _n in ROW_COLS.items():
    ROW_AT[_name] = _at
    _at += _n
ROW_W = _at


def constants():
    c = np.zeros((P, CONST_W), np.float32)
    p = np.arange(P)

    def put(name, a):
        a = np.asarray(a, np.float32).reshape(-1, CONST_COLS[name])
        c[:a.shape[0], CONST_AT[name]:CONST_AT[name] + CONST_COLS[name]] = a

    put("ident", np.eye(P))
    put("tri", p[:, None] <= p[None, :])
    put("blk", p[:, None] // HD == p[None, :] // HD)
    lev = [(p[:, None] // (2 << k) == p[None, :] // (2 << k)) & (p[:, None] // (1 << k) % 2 == 0)
           & (p[None, :] // (1 << k) % 2 == 1) for k in range(7)]
    put("lev", np.stack(lev, 1))
    put("causal", np.where(p[None, :] <= p[:, None], 0.0, NEG))
    half = ROPE // 2
    inv = np.float32(10000.0) ** (-np.arange(half, dtype=np.float32) / np.float32(half))
    pos = np.stack([p, p + P, np.full(P, PAGES * P)], 1).astype(np.float32)
    ang = pos[:, :, None] * inv
    put("rope", np.stack([np.cos(ang), np.sin(ang)], 2))
    n = np.arange(NS_TOK)
    nh_n, nh_h = np.arange(32) // H, np.arange(32) % H
    put("m832", np.broadcast_to(n[:, None] == nh_n[None, :], (P, NS_TOK, 32)))
    put("sel832", n[:, None] == nh_n[None, :])
    put("selrow", nh_n[:, None] == n[None, :])
    put("qr", (4 * np.arange(2)[None, :, None] + (p // ROPE)[:, None, None]) == nh_n[None, None, :])
    put("hsel", nh_h[:, None] == np.arange(H)[None, :])
    gn, gh, gv = p // 16, p // 4 % 4, p % 4
    put("selg", (n[:, None, None] == gn) & (np.arange(H)[None, :, None] == gh))
    put("mv", gv[:, None] == np.arange(4))
    put("m16", (gh[:, None, None] == np.arange(H)[None, :, None]) & (gv[:, None, None] == np.arange(4)))
    put("seln", gn[:, None] == n)
    put("rev", np.broadcast_to(np.arange(8, 0, -1), (P, 8)))
    put("stri", p[:, None] < p[None, :])
    put("iota", np.broadcast_to(np.arange(SLOTS), (P, SLOTS)))
    put("valid", np.stack([p >= 0, p >= 0, p < NS_TOK], 1))
    put("slot", p[:, None] + P * np.arange(SCH))
    t = np.arange(2)
    put("mq", (n[None, :, None, None] == nh_n) & (2 * t[None, None, :, None] + (p // HD)[:, None, None, None]
                                                  == nh_h))
    return c


def build(nc, A):
    with ExitStack() as top:
        def alloc(ctx, name, shape, dt=F32):
            return ctx.enter_context(nc.sbuf_tensor(name, shape, dt))

        xT = alloc(top, "xT", [P, KT, T])
        hT = alloc(top, "hT", [P, KT, T])
        zT = alloc(top, "zT", [P, FM_N, T])
        tm = alloc(top, "tm", [P, 3, TM_W])
        brT = alloc(top, "brT", [P, 8, T])
        cst = alloc(top, "cst", [P, CONST_W])
        ones = alloc(top, "ones", [P, P])
        epsc = alloc(top, "epsc", [P, 1])
        vec = alloc(top, "vec", [P, VEC_W])
        row = alloc(top, "row", [P, ROW_W])
        bank = [top.enter_context(nc.psum_tensor(f"bank{i}", [P, 512], F32)) for i in range(8)]

        def C(name, *dims):
            a = cst[:, CONST_AT[name]:CONST_AT[name] + CONST_COLS[name]]
            if len(dims) == 2:
                return a.rearrange("p (a b) -> p a b", a=dims[0])
            if len(dims) == 3:
                return a.rearrange("p (a b c) -> p a b c", a=dims[0], b=dims[1])
            return a

        def V(name, i=0, n=1):
            return vec[:, VEC_AT[name] + i:VEC_AT[name] + i + n]

        def R(name):
            return row[:, ROW_AT[name]:ROW_AT[name] + ROW_COLS[name]]

        class Phase:

            def __init__(self, name):
                self.name, self.ctx, self.sems, self.count = name, ExitStack(), {}, {}

            def sb(self, name, shape, dt=F32):
                return alloc(self.ctx, f"{self.name}_{name}", shape, dt)

            def sem(self, name):
                if name not in self.sems:
                    self.sems[name] = self.ctx.enter_context(
                        nc.semaphore(f"{self.name}_{name}", num=FIRST_SEM + len(self.sems)))
                return self.sems[name]

            def __enter__(self):
                self.block = nc.Block(no_gpsimd_drain=True)
                self.b = self.block.__enter__()
                return self

            def __exit__(self, *e):
                self.block.__exit__(*e)
                if e[0] is None:
                    nc.all_engine_barrier(sems_to_clear=range(FIRST_SEM, FIRST_SEM + len(self.sems)))
                self.ctx.close()

        def stepper(ph, eng, default):
            count = {}

            def step(ins, name=default, wait=True):
                count[name] = count.get(name, 0) + 1
                ins.then_inc(ph.sem(name), 1)
                if wait:
                    eng.wait_ge(ph.sem(name), count[name])

            return step

        env = dict(locals())
        env.pop("nc"), env.pop("A")
        start(nc, A, env)
        with nc.Fori(0, DEPTH) as l:
            for phase in PHASES:
                phase(nc, A, env, l)
        finish(nc, A, env)


def start(nc, A, E):
    with E["Phase"]("start") as ph:
        @ph.b.sync
        def _(sp):
            sp.dma_start(E["xT"][:], A["xT"]).then_inc(ph.sem("loaded"), 16)
            sp.dma_start(E["cst"][:], A["cst"]).then_inc(ph.sem("loaded"), 16)
            sp.wait_ge(ph.sem("loaded"), 32)

        @ph.b.vector
        def _(dve):
            nc.vector.memset(E["tm"][:], 0.0)
            nc.vector.memset(E["ones"][:], 1.0)
            nc.vector.memset(E["epsc"][:], EPS).then_inc(ph.sem("set"), 1)
            dve.wait_ge(ph.sem("set"), 1)


def finish(nc, A, E):
    with E["Phase"]("finish") as ph:
        @ph.b.sync
        def _(sp):
            sp.dma_start(A["o_x"], E["xT"][:]).then_inc(ph.sem("stored"), 16)
            sp.wait_ge(ph.sem("stored"), 16)


def project(nc, A, E, l):
    xT, hT, zT, tm, ones, bank, V = (E[k] for k in ("xT", "hT", "zT", "tm", "ones", "bank", "V"))
    with E["Phase"]("proj") as ph:
        S = ph.sem
        sq = ph.sb("sq", [P, KT, T])
        rstd = ph.sb("rstd", [P, T])
        wtm = ph.sb("wtm", [P, KT, TM_W])
        wfm = [ph.sb(f"wfm{i}", [P, KT, P]) for i in range(2)]

        @ph.b.sync
        def _(sp):
            sp.dma_start(E["vec"][:], A["vec"][l]).then_inc(S("vec_loaded"), 16)
            sp.dma_start(E["row"][:], A["row"][l].partition_broadcast(P)).then_inc(S("row_loaded"), 16)
            sp.dma_start(wtm[:], A["w_tm"][l]).then_inc(S("wtm_loaded"), 16)
            for i in range(2):
                sp.dma_start(wfm[i][:], A["w_fm"][l, i]).then_inc(S(f"wfm{i}_loaded"), 16)
            with sp.Fori(1, FM_N // 2) as t:
                for i in range(2):
                    tile = A["w_fm"][l, 2 * t + i]
                    sp.wait_ge(S(f"fm{i}_done"), t)
                    sp.dma_start(wfm[i][:], tile).then_inc(S(f"wfm{i}_loaded"), 16)
            sp.wait_ge(S("row_loaded"), 16)

        @ph.b.vector
        def _(dve):
            nc.vector.tensor_tensor(sq[:], xT[:], xT[:], ALU.mult).then_inc(S("sq_ready"), 1)
            dve.wait_ge(S("root_ready"), 1)
            nc.vector.reciprocal(rstd[:], rstd[:]).then_inc(S("rstd_ready"), 1)
            dve.wait_ge(S("rstd_ready"), 1)
            dve.wait_ge(S("vec_loaded"), 16)
            for k in range(KT):
                nc.vector.scalar_tensor_tensor(hT[:, k, :], xT[:, k, :], V("g1", k), rstd[:], ALU.mult,
                                               ALU.mult).then_inc(S("h_ready"), 1)

        @ph.b.tensor
        def _(pe):
            pe.wait_ge(S("sq_ready"), 1)
            for k in range(KT):
                mm = pe.matmul(bank[0][:, 0:T], ones[:], sq[:, k, :], start=k == 0, stop=k == KT - 1)
            mm.then_inc(S("ss_done"), 1)
            pe.wait_ge(S("wtm_loaded"), 16)
            for c, (t0, n) in enumerate(CHUNKS):
                for k in range(KT):
                    if c == 0:
                        pe.wait_ge(S("h_ready"), k + 1)
                    mm = pe.matmul(bank[1 + c][0:n, 0:TM_W], hT[:, k, t0:t0 + n], wtm[:, k, :],
                                   start=k == 0, stop=k == KT - 1)
                mm.then_inc(S("tm_done"), 1)

            def tile(i):
                for k in range(KT):
                    mm = pe.matmul(bank[4 + i][:, 0:T], wfm[i][:, k, :], hT[:, k, :], start=k == 0,
                                   stop=k == KT - 1)
                mm.then_inc(S(f"fm{i}_done"), 1)

            for i in range(2):
                pe.wait_ge(S(f"wfm{i}_loaded"), 16)
                tile(i)
            with pe.Fori(1, FM_N // 2) as t:
                for i in range(2):
                    pe.wait_ge(S(f"wfm{i}_loaded"), 16 * t + 16)
                    pe.wait_ge(S(f"fm{i}_copied"), t)
                    tile(i)

        @ph.b.scalar
        def _(act):
            act.wait_ge(S("ss_done"), 1)
            nc.scalar.activation(rstd[:], bank[0][:, 0:T], ACT.Sqrt, bias=E["epsc"][:],
                                 scale=1.0 / D_MODEL).then_inc(S("root_ready"), 1)
            for c, (t0, n) in enumerate(CHUNKS):
                act.wait_ge(S("tm_done"), c + 1)
                nc.scalar.copy(tm[0:n, c, :], bank[1 + c][0:n, 0:TM_W])
            with act.Fori(0, FM_N // 2) as t:
                for i in range(2):
                    act.wait_ge(S(f"fm{i}_done"), t + 1)
                    nc.scalar.copy(zT[:, 2 * t + i, :], bank[4 + i][:, 0:T]).then_inc(S(f"fm{i}_copied"), 1)


def gmlp(nc, A, E, l):
    zT, tm, brT, bank, C, V, R = (E[k] for k in ("zT", "tm", "brT", "bank", "C", "V", "R"))
    with E["Phase"]("gmlp") as ph:
        S = ph.sem
        uT = ph.sb("uT", [P, 2, T])
        gv = ph.sb("gv", [P, 3, 256])
        sq = ph.sb("sq", [P, 3, 256])
        ss = ph.sb("ss", [P, 3])
        ws = ph.sb("ws", [P, H, P])
        bias = ph.sb("bias", [P, 2, P])
        mixed = ph.sb("mixed", [P, 2, T])

        @ph.b.sync
        def _(sp):
            sp.dma_start(ws[:], A["gm_ws"][l]).then_inc(S("ws_loaded"), 16)
            for g in range(2):
                sp.dma_start(bias[HD * g:HD * g + HD], A["gm_b"][l, g].partition_broadcast(HD))\
                    .then_inc(S("bias_loaded"), 16)
            sp.wait_ge(S("v_ready"), 2)
            sp.dma_start(A["o_gv"][l], gv[0:NS_TOK, 2, :]).then_inc(S("v_stored"), 16)
            sp.wait_ge(S("v_stored"), 16)

        @ph.b.scalar
        def _(act):
            nc.scalar.activation(gv[:], tm[:, :, TM_V:TM_V + 256], ACT.Gelu).then_inc(S("gelu_done"), 1)
            nc.scalar.activation(uT[:], zT[:, FM_U:FM_U + 2, :], ACT.Gelu).then_inc(S("u_ready"), 1)
            act.wait_ge(S("ss_ready"), 1)
            nc.scalar.activation(ss[:], ss[:], ACT.Sqrt, bias=E["epsc"][:], scale=1.0 / 256)\
                .then_inc(S("root_ready"), 1)

        @ph.b.vector
        def _(dve):
            step = E["stepper"](ph, dve, "dve_step")
            dve.wait_ge(S("gelu_done"), 1)
            step(nc.vector.tensor_tensor(sq[:], gv[:], gv[:], ALU.mult))
            step(nc.vector.tensor_reduce(ss[:], sq[:], AX.X, ALU.add), "ss_ready", wait=False)
            dve.wait_ge(S("ws_loaded"), 16)
            nc.vector.tensor_tensor(ws[:], ws[:], C("tri").unsqueeze(1).to_broadcast([P, H, P]), ALU.mult)\
                .then_inc(S("ws_ready"), 1)
            dve.wait_ge(S("root_ready"), 1)
            step(nc.vector.reciprocal(ss[:], ss[:]))
            step(nc.vector.tensor_tensor(gv[:], gv[:], ss[:].unsqueeze(2).to_broadcast([P, 3, 256]), ALU.mult),
                 "v_ready")
            step(nc.vector.tensor_tensor(gv[:], gv[:], R("gm_g").unsqueeze(1).to_broadcast([P, 3, 256]),
                                         ALU.mult), "v_ready", wait=False)
            dve.wait_ge(S("bias_loaded"), 32)
            for c in range(2):
                dve.wait_ge(S("mix_done"), c + 1)
                step(nc.vector.tensor_tensor(mixed[:, :, c * P:c * P + P],
                                             bank[c][:, 0:256].rearrange("p (a i) -> p a i", a=2), bias[:],
                                             ALU.add))
            dve.wait_ge(S("vT_done"), 1)
            for a in range(2):
                step(nc.vector.tensor_scalar(mixed[:, a, NP_TOK:T], bank[2][:, NS_TOK * a:NS_TOK * a + NS_TOK],
                                             V("ws0", a), V("b0", a), ALU.mult, ALU.add))
            dve.wait_ge(S("u_ready"), 1)
            step(nc.vector.tensor_tensor(brT[:, 0:2, :], mixed[:], uT[:], ALU.mult))

        @ph.b.tensor
        def _(pe):
            pe.wait_ge(S("v_ready"), 2)
            pe.wait_ge(S("ws_ready"), 1)
            for c in range(2):
                for g in range(H):
                    o = HD * (g % 2)
                    mm = pe.matmul(bank[c][o:o + HD, P * (g // 2):P * (g // 2) + P],
                                   gv[:, c, HD * g:HD * g + HD], ws[:, g, :], start=True, stop=True)
                mm.then_inc(S("mix_done"), 1)
            for a in range(2):
                mm = pe.transpose(bank[2][:, NS_TOK * a:NS_TOK * a + NS_TOK], gv[0:NS_TOK, 2, P * a:P * a + P],
                                  C("ident")[0:NS_TOK, 0:NS_TOK])
            mm.then_inc(S("vT_done"), 1)


def memory(nc, A, E, l):
    zT, brT, bank, C, V, R, ones = (E[k] for k in ("zT", "brT", "bank", "C", "V", "R", "ones"))
    with E["Phase"]("mem") as ph:
        S = ph.sem
        memT = ph.sb("memT", [P, KT, MEM])
        sq = ph.sb("sq", [P, KT, MEM])
        rstd = ph.sb("rstd", [P, MEM])
        wkv = ph.sb("wkv", [P, KT, 512])
        kv = ph.sb("kv", [P, 2, 512])
        ksq = ph.sb("ksq", [P, 2, 256])
        kss = ph.sb("kss", [P, 2, H])
        kT = ph.sb("kT", [P, 2, MEM])
        qT = ph.sb("qT", [P, 2, T])
        qsq = ph.sb("qsq", [P, 2, T])
        qblk = ph.sb("qblk", [P, 16, 32])
        sc = ph.sb("sc", [P, 2, H, MEM])
        scs = ph.sb("scs", [32, MEM])
        mx = ph.sb("mx", [P, 2, H])
        mxs = ph.sb("mxs", [32, 1])
        sm = ph.sb("sm", [P, 2, H])
        sms = ph.sb("sms", [32, 1])
        pT = ph.sb("pT", [P, 2, H, NP_TOK])
        psT = ph.sb("psT", [P, 2, 32])
        pblk = ph.sb("pblk", [P, 2, NS_TOK, 32])
        outs = ph.sb("outs", [32, H, HD])
        ckT = ph.sb("ckT", [P, NS_TOK, 2, MEM])
        cv = ph.sb("cv", [P, NS_TOK, 2, 256])

        @ph.b.sync
        def _(sp):
            sp.dma_start(memT[:], A["memT"]).then_inc(S("mem_loaded"), 16)
            sp.dma_start(wkv[:], A["w_kv"][l]).then_inc(S("wkv_loaded"), 16)
            sp.dma_start(ckT[:], A["memkT"][l]).then_inc(S("ck_loaded"), 16)
            sp.dma_start(cv[:], A["memv"][l]).then_inc(S("cv_loaded"), 16)
            sp.wait_ge(S("kv_ready"), 1)
            for i in range(2):
                sp.dma_start(A["o_mem"][l, :, i], kv[:, :, 256 * i:256 * i + 256]).then_inc(S("kv_stored"), 16)
            sp.wait_ge(S("kv_stored"), 32)

        @ph.b.tensor
        def _(pe):
            pe.wait_ge(S("memsq_ready"), 1)
            for k in range(KT):
                mm = pe.matmul(bank[0][:, 0:MEM], ones[:], sq[:, k, :], start=k == 0, stop=k == KT - 1)
            mm.then_inc(S("memss_done"), 1)
            pe.wait_ge(S("qsq_ready"), 1)
            for t in range(2):
                mm = pe.matmul(bank[1 + t][:, 0:T], C("blk"), qsq[:, t, :], start=True, stop=True)
            mm.then_inc(S("qss_done"), 1)
            pe.wait_ge(S("memh_ready"), KT)
            pe.wait_ge(S("wkv_loaded"), 16)
            for c in range(2):
                for k in range(KT):
                    mm = pe.matmul(bank[3 + c][:], memT[:, k, P * c:P * c + P], wkv[:, k, :], start=k == 0,
                                   stop=k == KT - 1)
                mm.then_inc(S("kv_done"), 1)
            pe.wait_ge(S("qblk_ready"), 16)
            pe.wait_ge(S("ck_loaded"), 16)
            for i in range(16):
                mm = pe.matmul(bank[5][0:32, 0:MEM], qblk[:, i, :], ckT[:, i // 2, i % 2, :], start=i == 0,
                               stop=i == 15)
            mm.then_inc(S("scs_done"), 1)
            pe.wait_ge(S("kv_ready"), 1)
            for c in range(2):
                for t in range(2):
                    at = P * (2 * t + c)
                    mm = pe.transpose(bank[6][:, at:at + P], kv[:, c, P * t:P * t + P], C("ident"))
            mm.then_inc(S("kT_done"), 1)
            pe.wait_ge(S("kT_ready"), 1)
            pe.wait_ge(S("q_ready"), 3)
            pe.wait_ge(S("kv_copied"), 2)
            for c in range(2):
                for h in range(H):
                    o = HD * (h % 2)
                    mm = pe.matmul(bank[2 * c + h % 2][:, MEM * (h // 2):MEM * (h // 2) + MEM],
                                   qT[o:o + HD, h // 2, P * c:P * c + P], kT[o:o + HD, h // 2, :],
                                   start=True, stop=True)
                    mm.then_inc(S("sc_done"), 1)
            pe.wait_ge(S("ps_ready"), 1)
            for half in range(2):
                mm = pe.transpose(bank[7][:, 32 * half:32 * half + 32], scs[:, P * half:P * half + P],
                                  C("ident")[0:32, 0:32])
            mm.then_inc(S("psT_done"), 1)
            pe.wait_ge(S("p_ready"), 1)
            pe.wait_ge(S("sc_copied"), 4)
            for c in range(2):
                for half in range(2):
                    for h in range(H):
                        mm = pe.transpose(bank[2 * c + half][:, P * h:P * h + P],
                                          sc[:, c, h, P * half:P * half + P], C("ident"))
                    mm.then_inc(S("pT_done"), 1)
            pe.wait_ge(S("pblk_ready"), 1)
            pe.wait_ge(S("cv_loaded"), 16)
            for i in range(16):
                mm = pe.matmul(bank[5][0:32, 0:256], pblk[:, i % 2, i // 2, :], cv[:, i // 2, i % 2, :],
                               start=i == 0, stop=i == 15)
            mm.then_inc(S("outs_done"), 1)
            pe.wait_ge(S("pT_copied"), 4)
            for h in range(H):
                o = HD * (h % 2)
                for half in range(2):
                    mm = pe.matmul(bank[6 + h // 2][o:o + HD, 0:NP_TOK],
                                   kv[:, half, 256 + HD * h:256 + HD * h + HD], pT[:, half, h, :],
                                   start=half == 0, stop=half == 1)
            mm.then_inc(S("out_done"), 1)
            pe.wait_ge(S("outs_ready"), 1)
            pe.wait_ge(S("pT_copied"), 4)
            for t in range(2):
                mm = pe.matmul(bank[t][:, 0:NS_TOK], outs[:, 2 * t:2 * t + 2, :].rearrange("p a b -> p (a b)"),
                               C("selrow")[0:32, :], start=True, stop=True)
            mm.then_inc(S("outsT_done"), 1)

        @ph.b.scalar
        def _(act):
            act.wait_ge(S("memss_done"), 1)
            nc.scalar.activation(rstd[:], bank[0][:, 0:MEM], ACT.Sqrt, bias=E["epsc"][:], scale=1.0 / D_MODEL)\
                .then_inc(S("root_ready"), 1)
            act.wait_ge(S("qss_done"), 1)
            for t in range(2):
                nc.scalar.activation(qsq[:, t, :], bank[1 + t][:, 0:T], ACT.Sqrt, bias=E["epsc"][:],
                                     scale=1.0 / HD).then_inc(S("qroot_ready"), 1)
            act.wait_ge(S("kss_ready"), 1)
            nc.scalar.activation(kss[:], kss[:], ACT.Sqrt, bias=E["epsc"][:], scale=1.0 / HD)\
                .then_inc(S("kroot_ready"), 1)
            act.wait_ge(S("shift_s"), 1)
            nc.scalar.activation(scs[:], scs[:], ACT.Exp, scale=MEM_SCALE).then_inc(S("exps_done"), 1)
            act.wait_ge(S("sc_copied"), 4)
            nc.scalar.activation(sc[:], sc[:], ACT.Exp, scale=MEM_SCALE).then_inc(S("exp_done"), 1)
            for i in range(4):
                c, half = i // 2, i % 2
                act.wait_ge(S("pT_done"), i + 1)
                nc.scalar.copy(pT[:, half, :, P * c:P * c + P], bank[i][:].rearrange("p (h t) -> p h t", h=H))\
                    .then_inc(S("pT_copied"), 1)

        @ph.b.vector
        def _(dve):
            step = E["stepper"](ph, dve, "dve_step")
            dve.wait_ge(S("mem_loaded"), 16)
            step(nc.vector.tensor_tensor(sq[:], memT[:], memT[:], ALU.mult), "memsq_ready", wait=False)
            mq = zT[:, FM_MQ:FM_MQ + 2, :]
            step(nc.vector.tensor_tensor(qsq[:], mq, mq, ALU.mult), "qsq_ready")
            dve.wait_ge(S("root_ready"), 1)
            step(nc.vector.reciprocal(rstd[:], rstd[:]))
            for k in range(KT):
                step(nc.vector.scalar_tensor_tensor(memT[:, k, :], memT[:, k, :], V("memn_g", k), rstd[:],
                                                    ALU.mult, ALU.mult), "memh_ready", wait=False)
            dve.wait_ge(S("qroot_ready"), 2)
            step(nc.vector.reciprocal(qsq[:], qsq[:]), "q_ready")
            step(nc.vector.tensor_tensor(qT[:], mq, qsq[:], ALU.mult), "q_ready")
            step(nc.vector.tensor_scalar(qT[:], qT[:], V("mq_g"), None, ALU.mult), "q_ready")
            for i in range(16):
                n, t = i // 2, i % 2
                last = nc.vector.tensor_scalar(qblk[:, i, :], C("mq", 16, 32)[:, i, :],
                                               qT[:, t, NP_TOK + n:NP_TOK + n + 1], None, ALU.mult)
                step(last, "qblk_ready", wait=False)
            for c in range(2):
                dve.wait_ge(S("kv_done"), c + 1)
                step(nc.vector.tensor_copy(kv[:, c, :], bank[3 + c][:]), "kv_copied")
            k4 = kv[:, :, 0:256].rearrange("p c (h e) -> p c h e", h=H)
            step(nc.vector.tensor_tensor(ksq[:], kv[:, :, 0:256], kv[:, :, 0:256], ALU.mult))
            step(nc.vector.tensor_reduce(kss[:], ksq[:].rearrange("p c (h e) -> p c h e", h=H), AX.X, ALU.add),
                 "kss_ready", wait=False)
            dve.wait_ge(S("kroot_ready"), 1)
            step(nc.vector.reciprocal(kss[:], kss[:]))
            for c in range(2):
                step(nc.vector.tensor_tensor(k4[:, c], k4[:, c], kss[:, c].unsqueeze(2).to_broadcast([P, H, HD]),
                                             ALU.mult))
                last = nc.vector.tensor_tensor(k4[:, c], k4[:, c],
                                               R("memk_g").unsqueeze(1).to_broadcast([P, H, HD]), ALU.mult)
                step(last, *(["kv_ready"] if c else []))
            dve.wait_ge(S("scs_done"), 1)
            step(nc.vector.tensor_reduce(mxs[:], bank[5][0:32, 0:MEM], AX.X, ALU.max))
            step(nc.vector.tensor_scalar(scs[:], bank[5][0:32, 0:MEM], mxs[:], None, ALU.subtract), "shift_s",
                 wait=False)
            dve.wait_ge(S("kT_done"), 1)
            step(nc.vector.tensor_copy(kT[:].rearrange("p t s -> p (t s)"), bank[6][:]), "kT_ready", wait=False)
            dve.wait_ge(S("exps_done"), 1)
            step(nc.vector.tensor_reduce(sms[:], scs[:], AX.X, ALU.add))
            step(nc.vector.reciprocal(sms[:], sms[:]))
            step(nc.vector.tensor_scalar(scs[:], scs[:], sms[:], None, ALU.mult), "ps_ready", wait=False)
            for i in range(4):
                c, a = i // 2, i % 2
                dve.wait_ge(S("sc_done"), 4 * c + 3 + a)
                two = bank[i][:].rearrange("p (h s) -> p h s", h=2)
                mxa = mx[:, c].rearrange("p (b a) -> p a b", a=2)[:, a]
                step(nc.vector.tensor_reduce(mxa, two, AX.X, ALU.max))
                step(nc.vector.tensor_tensor(sc[:, c].rearrange("p (b a) s -> p a b s", a=2)[:, a], two,
                                             mxa.unsqueeze(2).to_broadcast([P, 2, MEM]), ALU.subtract),
                     "sc_copied")
            dve.wait_ge(S("exp_done"), 1)
            step(nc.vector.tensor_reduce(sm[:], sc[:], AX.X, ALU.add))
            step(nc.vector.reciprocal(sm[:], sm[:]))
            flat = sc[:].rearrange("p c h s -> p (c h) s")
            step(nc.vector.tensor_tensor(flat, flat, sm[:].rearrange("p c h -> p (c h)").unsqueeze(2)
                                         .to_broadcast([P, 2 * H, MEM]), ALU.mult), "p_ready", wait=False)
            dve.wait_ge(S("psT_done"), 1)
            step(nc.vector.tensor_copy(psT[:].rearrange("p a b -> p (a b)"), bank[7][:, 0:64]))
            for half in range(2):
                last = nc.vector.tensor_tensor(pblk[:, half], C("m832", NS_TOK, 32),
                                               psT[:, half].unsqueeze(1).to_broadcast([P, NS_TOK, 32]), ALU.mult)
                step(last, *(["pblk_ready"] if half else []))
            dve.wait_ge(S("outs_done"), 1)
            step(nc.vector.tensor_tensor(outs[:], bank[5][0:32, 0:256].rearrange("p (h e) -> p h e", h=H),
                                         C("hsel")[0:32, :].unsqueeze(2).to_broadcast([32, H, HD]), ALU.mult),
                 "outs_ready", wait=False)
            dve.wait_ge(S("out_done"), 1)
            for t in range(2):
                step(nc.vector.tensor_copy(brT[:, 6 + t, 0:NP_TOK], bank[6 + t][:, 0:NP_TOK]))
            dve.wait_ge(S("outsT_done"), 1)
            for t in range(2):
                step(nc.vector.tensor_copy(brT[:, 6 + t, NP_TOK:T], bank[t][:, 0:NS_TOK]))


def mla(nc, A, E, l):
    with ExitStack() as both:
        sb = lambda name, shape, dt=F32: E["alloc"](both, f"mla_{name}", shape, dt)
        B = dict(
            q=sb("q", [P, 3, H * QK]),
            kc=sb("kc", [P, 3, H * QK]),
            ckvn=sb("ckvn", [P, 3, RANK]),
            latT=sb("latT", [P, H, T]),
            wuk=sb("wuk", [P, H * HD]),
            ids=sb("ids", [1, NPG], I32),
            ck=sb("ck", [P, NPG, RANK]),
            ckT=sb("ckT", [P, NPG, P]),
            krT=sb("krT", [P, 2, PAGES, P]))
        mla_prompt(nc, A, E, l, B)
        mla_decode(nc, A, E, l, B)


def rotate(step, nc, x, cos, sin, tmp, name="dve_step"):
    half = ROPE // 2
    x1, x2 = x[..., 0:half], x[..., half:ROPE]
    for i, (a, b) in enumerate(((x1, cos), (x2, sin), (x1, sin), (x2, cos))):
        step(nc.vector.tensor_tensor(tmp[i], a, b, ALU.mult))
    step(nc.vector.tensor_tensor(x1, tmp[0], tmp[1], ALU.subtract))
    step(nc.vector.tensor_tensor(x2, tmp[2], tmp[3], ALU.add), name)


def mla_prompt(nc, A, E, l, B):
    zT, tm, bank, C, V, R, ones = (E[k] for k in ("zT", "tm", "bank", "C", "V", "R", "ones"))
    q, kc, ckvn, latT, wuk = (B[k] for k in ("q", "kc", "ckvn", "latT", "wuk"))
    with E["Phase"]("mlap") as ph:
        S = ph.sem
        cqT = ph.sb("cqT", [P, 2, T])
        cqs = ph.sb("cqs", [P, 2, T])
        wuq = ph.sb("wuq", [P, 2, H * QK])
        sq = ph.sb("sq", [P, 3, H * QK])
        rs = ph.sb("rs", [P, 3, 2 * H])
        krn = ph.sb("krn", [P, 3, ROPE])
        crs = ph.sb("crs", [P, 3, 2])
        krss = ph.sb("krss", [P, 3, H])
        tmp = ph.sb("tmp", [P, 4, 3 * H * 16])
        ckvT = ph.sb("ckvT", [P, T])
        qT = ph.sb("qT", [QK, H, NP_TOK])
        kT = ph.sb("kT", [QK, H, NP_TOK])
        sc0 = ph.sb("sc0", [P, H, P])
        sc1 = ph.sb("sc1", [P, H, NP_TOK])
        mx = ph.sb("mx", [P, 2, H])
        pT0 = ph.sb("pT0", [P, 1, 512])
        pT1 = ph.sb("pT1", [P, 2, 512])
        cos, sin = C("rope", 3, 2, 16)[:, :, 0, :], C("rope", 3, 2, 16)[:, :, 1, :]

        @ph.b.sync
        def _(sp):
            sp.dma_start(wuq[:], A["w_uq"][l]).then_inc(S("wuq_loaded"), 16)
            sp.dma_start(wuk[:], A["w_uk"][l]).then_inc(S("wuk_loaded"), 16)
            sp.dma_start(B["ids"][:], A["pages"]).then_inc(S("ids_loaded"), 16)
            sp.wait_ge(S("ids_loaded"), 16)
            with sp.Fori(0, PAGES) as p:
                for g in range(2):
                    for j in range(4):
                        n = 4 * g + j
                        page = sp.value_load(B["ids"][0:1, bass.ds(p + PAGES * n, 1)], min_val=0, max_val=POOL - 1)
                        sp.dma_start(B["ck"][:, bass.ds(p + PAGES * n, 1), :].squeeze(1), A["ckv"][l, page])\
                            .then_inc(S("pages_loaded"), 16)
                        sp.dma_start(B["ckT"][:, bass.ds(p + PAGES * n, 1), :].squeeze(1), A["ckvT"][l, page])\
                            .then_inc(S("pages_loaded"), 16)
                        sp.dma_start(B["krT"][ROPE * j:ROPE * j + ROPE, g, bass.ds(p, 1), :].squeeze(1),
                                     A["krT"][l, page]).then_inc(S("pages_loaded"), 16)
            sp.wait_ge(S("latent_ready"), 2)
            sp.dma_start(A["o_ckv"][l], ckvn[:]).then_inc(S("latent_stored"), 16)
            sp.dma_start(A["o_kr"][l], krn[:]).then_inc(S("latent_stored"), 16)
            sp.wait_ge(S("latent_stored"), 32)
            sp.wait_ge(S("pages_loaded"), 16 * 3 * NPG)

        @ph.b.tensor
        def _(pe):
            pe.wait_ge(S("cqsq_ready"), 1)
            for t in range(2):
                mm = pe.matmul(bank[0][:, 0:T], ones[:], cqs[:, t, :], start=t == 0, stop=t == 1)
            mm.then_inc(S("cqss_done"), 1)
            pe.wait_ge(S("latent_ready"), 1)
            for c, (t0, n) in enumerate(CHUNKS):
                mm = pe.transpose(bank[4][:, t0:t0 + n], ckvn[0:n, c, :], C("ident")[0:n, 0:n])
            mm.then_inc(S("ckvT_done"), 1)
            pe.wait_ge(S("cq_ready"), 2)
            pe.wait_ge(S("wuq_loaded"), 16)
            for c, (t0, n) in enumerate(CHUNKS):
                for t in range(2):
                    mm = pe.matmul(bank[1 + c][0:n, 0:H * QK], cqT[:, t, t0:t0 + n], wuq[:, t, :], start=t == 0,
                                   stop=t == 1)
                mm.then_inc(S("q_done"), 1)
            pe.wait_ge(S("ckvT_ready"), 1)
            pe.wait_ge(S("wuk_loaded"), 16)
            for c, (t0, n) in enumerate(CHUNKS):
                mm = pe.matmul(bank[5 + c][0:n, 0:H * HD], ckvT[:, t0:t0 + n], wuk[:], start=True, stop=True)
                mm.then_inc(S("k_done"), 1)
            pe.wait_ge(S("qn_ready"), 1)
            for c in range(2):
                for h in range(H):
                    mm = pe.transpose(bank[c][0:QK, P * h:P * h + P], q[:, c, QK * h:QK * h + QK], C("ident"))
                mm.then_inc(S("qT_done"), 1)
            pe.wait_ge(S("kn_ready"), 1)
            for c in range(2):
                for h in range(H):
                    mm = pe.transpose(bank[2 + c][0:QK, P * h:P * h + P], kc[:, c, QK * h:QK * h + QK],
                                      C("ident"))
                mm.then_inc(S("kT_done"), 1)
            pe.wait_ge(S("qkT_ready"), 4)
            for h in range(H):
                mm = pe.matmul(bank[4][:, P * h:P * h + P], qT[:, h, 0:P], kT[:, h, 0:P], start=True, stop=True)
            mm.then_inc(S("sc_done"), 1)
            for h in range(H):
                mm = pe.matmul(bank[5 + h // 2][:, NP_TOK * (h % 2):NP_TOK * (h % 2) + NP_TOK], qT[:, h, P:2 * P],
                               kT[:, h, :], start=True, stop=True)
                if h % 2:
                    mm.then_inc(S("sc_done"), 1)
            pe.wait_ge(S("p0_ready"), 1)
            for h in range(H):
                mm = pe.transpose(bank[7][:, P * h:P * h + P], sc0[:, h, :], C("ident"))
            mm.then_inc(S("pT_done"), 1)
            pe.wait_ge(S("p1_ready"), 1)
            for s in range(2):
                for h in range(H):
                    mm = pe.transpose(bank[s][:, P * h:P * h + P], sc1[:, h, P * s:P * s + P], C("ident"))
                mm.then_inc(S("pT_done"), 1)
            pe.wait_ge(S("pT_ready"), 1)
            pe.matmul(bank[2][:], ckvn[:, 0, :], pT0[:, 0, :], start=True, stop=True).then_inc(S("lat_done"), 1)
            pe.wait_ge(S("pT_ready"), 3)
            for s in range(2):
                mm = pe.matmul(bank[3][:], ckvn[:, s, :], pT1[:, s, :], start=s == 0, stop=s == 1)
            mm.then_inc(S("lat_done"), 1)

        @ph.b.scalar
        def _(act):
            eps = E["epsc"][:]
            act.wait_ge(S("cqss_done"), 1)
            nc.scalar.activation(cqs[:, 0, :], bank[0][:, 0:T], ACT.Sqrt, bias=eps, scale=1.0 / 256)\
                .then_inc(S("cqroot_ready"), 1)
            act.wait_ge(S("ckvss_ready"), 2)
            for i, n in enumerate((RANK, ROPE)):
                nc.scalar.activation(crs[:, :, i], crs[:, :, i], ACT.Sqrt, bias=eps, scale=1.0 / n)\
                    .then_inc(S("ckvroot_ready"), 1)
            act.wait_ge(S("ckvT_done"), 1)
            nc.scalar.copy(ckvT[:], bank[4][:, 0:T]).then_inc(S("ckvT_ready"), 1)
            act.wait_ge(S("zeroed"), 2)
            for c, (t0, n) in enumerate(CHUNKS):
                act.wait_ge(S("q_done"), c + 1)
                nc.scalar.copy(q[0:n, c, :], bank[1 + c][0:n, 0:H * QK]).then_inc(S("q_ready"), 1)
            act.wait_ge(S("qss_ready"), 2)
            for i, n in enumerate((HD, ROPE)):
                nc.scalar.activation(rs[:, :, H * i:H * i + H], rs[:, :, H * i:H * i + H], ACT.Sqrt, bias=eps,
                                     scale=1.0 / n).then_inc(S("qroot_ready"), 1)
            for c, (t0, n) in enumerate(CHUNKS):
                act.wait_ge(S("k_done"), c + 1)
                nc.scalar.copy(kc[0:n, c, :].rearrange("p (h e) -> p h e", h=H)[:, :, 0:HD],
                               bank[5 + c][0:n, 0:H * HD].rearrange("p (h e) -> p h e", h=H))\
                    .then_inc(S("k_ready"), 1)
            act.wait_ge(S("kss_ready"), 1)
            nc.scalar.activation(krss[:], krss[:], ACT.Sqrt, bias=eps, scale=1.0 / HD).then_inc(S("kroot_ready"), 1)
            for c in range(2):
                act.wait_ge(S("qT_done"), c + 1)
                nc.scalar.copy(qT[:, :, P * c:P * c + P], bank[c][0:QK, :].rearrange("p (h t) -> p h t", h=H))\
                    .then_inc(S("qkT_ready"), 1)
            for c in range(2):
                act.wait_ge(S("kT_done"), c + 1)
                nc.scalar.copy(kT[:, :, P * c:P * c + P], bank[2 + c][0:QK, :].rearrange("p (h t) -> p h t", h=H))\
                    .then_inc(S("qkT_ready"), 1)
            act.wait_ge(S("shift0"), 1)
            nc.scalar.activation(sc0[:], sc0[:], ACT.Exp).then_inc(S("exp0_done"), 1)
            act.wait_ge(S("shift1"), 1)
            nc.scalar.activation(sc1[:], sc1[:], ACT.Exp).then_inc(S("exp1_done"), 1)
            act.wait_ge(S("pT_done"), 1)
            nc.scalar.copy(pT0[:, 0, :], bank[7][:]).then_inc(S("pT_ready"), 1)
            for s in range(2):
                act.wait_ge(S("pT_done"), s + 2)
                nc.scalar.copy(pT1[:, s, :], bank[s][:]).then_inc(S("pT_ready"), 1)
            for c in range(2):
                act.wait_ge(S("lat_done"), c + 1)
                nc.scalar.copy(latT[:, :, P * c:P * c + P], bank[2 + c][:].rearrange("p (h t) -> p h t", h=H))

        @ph.b.vector
        def _(dve):
            step = E["stepper"](ph, dve, "dve_step")
            tt, red = nc.vector.tensor_tensor, nc.vector.tensor_reduce
            step(nc.vector.memset(q[:], 0.0), "zeroed", wait=False)
            step(nc.vector.memset(kc[:], 0.0), "zeroed")
            cq = zT[:, FM_CQ:FM_CQ + 2, :]
            step(tt(cqs[:], cq, cq, ALU.mult), "cqsq_ready", wait=False)
            raw, rawr = tm[:, :, TM_CKV:TM_CKV + RANK], tm[:, :, TM_KR:TM_KR + ROPE]
            step(tt(sq[:, :, 0:RANK], raw, raw, ALU.mult), wait=False)
            step(tt(sq[:, :, RANK:RANK + ROPE], rawr, rawr, ALU.mult))
            step(red(crs[:, :, 0], sq[:, :, 0:RANK], AX.X, ALU.add), "ckvss_ready", wait=False)
            step(red(crs[:, :, 1], sq[:, :, RANK:RANK + ROPE], AX.X, ALU.add), "ckvss_ready", wait=False)
            dve.wait_ge(S("cqroot_ready"), 1)
            step(nc.vector.reciprocal(cqs[:, 1, :], cqs[:, 0, :]))
            for t in range(2):
                step(nc.vector.scalar_tensor_tensor(cqT[:, t, :], zT[:, FM_CQ + t, :], V("cq_g", t), cqs[:, 1, :],
                                                    ALU.mult, ALU.mult), "cq_ready", wait=False)
            dve.wait_ge(S("ckvroot_ready"), 2)
            step(nc.vector.reciprocal(crs[:], crs[:]))
            step(tt(ckvn[:], raw, crs[:, :, 0].unsqueeze(2).to_broadcast([P, 3, RANK]), ALU.mult), wait=False)
            step(tt(krn[:], rawr, crs[:, :, 1].unsqueeze(2).to_broadcast([P, 3, ROPE]), ALU.mult))
            step(tt(ckvn[:], ckvn[:], R("ckv_g").unsqueeze(1).to_broadcast([P, 3, RANK]), ALU.mult),
                 "latent_ready", wait=False)
            step(tt(krn[:], krn[:], R("kr_g").unsqueeze(1).to_broadcast([P, 3, ROPE]), ALU.mult))
            rotate(step, nc, krn[:], cos, sin,
                   [tmp[:, i, 0:48].rearrange("p (c e) -> p c e", c=3) for i in range(4)])
            kc4 = kc[:].rearrange("p c (h e) -> p c h e", h=H)
            step(tt(kc4[:, :, :, HD:QK], krn[:].unsqueeze(2).to_broadcast([P, 3, H, ROPE]),
                    krn[:].unsqueeze(2).to_broadcast([P, 3, H, ROPE]), ALU.max), "latent_ready", wait=False)
            dve.wait_ge(S("q_ready"), 3)
            q4, sq4 = (a.rearrange("p c (h e) -> p c h e", h=H) for a in (q[:], sq[:]))
            step(tt(sq[:], q[:], q[:], ALU.mult))
            step(red(rs[:, :, 0:H], sq4[:, :, :, 0:HD], AX.X, ALU.add), "qss_ready", wait=False)
            step(red(rs[:, :, H:2 * H], sq4[:, :, :, HD:QK], AX.X, ALU.add), "qss_ready", wait=False)
            dve.wait_ge(S("qroot_ready"), 2)
            step(nc.vector.reciprocal(rs[:], rs[:]))
            q12 = q[:].rearrange("p c (h e) -> p (c h) e", h=H)
            for part, o, n, g in ((0, 0, HD, "qn_g"), (1, HD, ROPE, "qr_g")):
                dims = [P, 3, H, n]
                step(tt(q4[:, :, :, o:o + n], q4[:, :, :, o:o + n],
                        rs[:, :, H * part:H * part + H].unsqueeze(3).to_broadcast(dims), ALU.mult))
                step(tt(q12[:, :, o:o + n], q12[:, :, o:o + n], R(g).unsqueeze(1).to_broadcast([P, 3 * H, n]),
                        ALU.mult))
            wide = [P, 3, H, 16]
            rotate(step, nc, q4[:, :, :, HD:QK], cos.unsqueeze(2).to_broadcast(wide),
                   sin.unsqueeze(2).to_broadcast(wide),
                   [tmp[:, i].rearrange("p (c h e) -> p c h e", c=3, h=H) for i in range(4)], "qn_ready")
            dve.wait_ge(S("k_ready"), 3)
            kn = kc[:].rearrange("p c (h e) -> p (c h) e", h=H)[:, :, 0:HD]
            step(tt(sq[:, :, 0:256].rearrange("p c (h e) -> p c h e", h=H), kc4[:, :, :, 0:HD],
                    kc4[:, :, :, 0:HD], ALU.mult))
            step(red(krss[:], sq[:, :, 0:256].rearrange("p c (h e) -> p c h e", h=H), AX.X, ALU.add), "kss_ready",
                 wait=False)
            dve.wait_ge(S("kroot_ready"), 1)
            step(nc.vector.reciprocal(krss[:], krss[:]))
            step(tt(kn, kn, krss[:].rearrange("p c h -> p (c h)").unsqueeze(2).to_broadcast([P, 3 * H, HD]),
                    ALU.mult))
            step(tt(kn, kn, R("kn_g").unsqueeze(1).to_broadcast([P, 3 * H, HD]), ALU.mult), "kn_ready")
            dve.wait_ge(S("sc_done"), 1)
            mask = C("causal")

            def rows(sc, m, n):
                step(red(m, sc, AX.X, ALU.max))
                return tt(sc, sc, m.unsqueeze(2).to_broadcast([P, H, n]), ALU.subtract)

            for h in range(H):
                step(nc.vector.scalar_tensor_tensor(sc0[:, h, :], bank[4][:, P * h:P * h + P], MLA_SCALE, mask,
                                                    ALU.mult, ALU.add))
            step(rows(sc0[:], mx[:, 0], P), "shift0", wait=False)
            for h in range(H):
                dve.wait_ge(S("sc_done"), 2 + h // 2)
                src = bank[5 + h // 2][:, NP_TOK * (h % 2):NP_TOK * (h % 2) + NP_TOK]
                step(nc.vector.tensor_scalar(sc1[:, h, 0:P], src[:, 0:P], MLA_SCALE, None, ALU.mult))
                step(nc.vector.scalar_tensor_tensor(sc1[:, h, P:2 * P], src[:, P:2 * P], MLA_SCALE, mask, ALU.mult,
                                                    ALU.add))
            step(rows(sc1[:], mx[:, 1], NP_TOK), "shift1", wait=False)
            for i, (sc, n) in enumerate(((sc0, P), (sc1, NP_TOK))):
                dve.wait_ge(S(f"exp{i}_done"), 1)
                step(red(mx[:, i], sc[:], AX.X, ALU.add))
                step(nc.vector.reciprocal(mx[:, i], mx[:, i]))
                step(tt(sc[:], sc[:], mx[:, i].unsqueeze(2).to_broadcast([P, H, n]), ALU.mult), f"p{i}_ready",
                     wait=False)


def mla_decode(nc, A, E, l, B):
    brT, bank, C, V, ones = (E[k] for k in ("brT", "bank", "C", "V", "ones"))
    q, kc, ckvn, latT, wuk, ck, ckT, krT = (B[k] for k in ("q", "kc", "ckvn", "latT", "wuk", "ck", "ckT", "krT"))
    N = NS_TOK
    RAW = 4
    with E["Phase"]("mlad") as ph:
        S = ph.sem
        wukT = ph.sb("wukT", [HD, H, RANK])
        wuv = ph.sb("wuv", [P, H * HD])
        qsT = ph.sb("qsT", [QK, H, N])
        qa = ph.sb("qa", [P, N, H])
        qblk = ph.sb("qblk", [P, N, 32])
        qrep = ph.sb("qrep", [N, H, 4, ROPE])
        qr = ph.sb("qr", [P, N, H])
        qrblk = ph.sb("qrblk", [P, 2, 32])
        prod = ph.sb("prod", [N, H * QK])
        so = ph.sb("so", [N, H])
        sox = ph.sb("sox", [N, N, H])
        sqr = ph.sb("sqr", [P, RAW, 512])
        ssq = ph.sb("ssq", [P, PAGES, 32])
        rT = ph.sb("rT", [32, PAGES * P])
        sc = ph.sb("sc", [32, PAGES * P + 1])
        mx = ph.sb("mx", [32, 1])
        pT = ph.sb("pT", [P, PAGES, 32])
        pblk = ph.sb("pblk", [P, PAGES, N, 32])
        own = ph.sb("own", [32, RANK])
        lat = ph.sb("lat", [32, RANK])

        @ph.b.sync
        def _(sp):
            sp.dma_start(wukT[:], A["w_ukT"][l]).then_inc(S("wukT_loaded"), 16)
            sp.dma_start(wuv[:], A["w_uv"][l]).then_inc(S("wuv_loaded"), 16)

        @ph.b.tensor
        def _(pe):
            ident = C("ident")
            for h in range(H):
                mm = pe.transpose(bank[0][0:QK, N * h:N * h + N], q[0:N, 2, QK * h:QK * h + QK], ident[0:N, 0:N])
            mm.then_inc(S("qsT_done"), 1)
            pe.wait_ge(S("qrep_ready"), 1)
            for h in range(H):
                mm = pe.matmul(bank[2][:, N * h:N * h + N], qrep[:, h].rearrange("p a b -> p (a b)"),
                               ident[0:N, 0:N], start=True, stop=True)
            mm.then_inc(S("qr_done"), 1)
            pe.wait_ge(S("sox_ready"), 1)
            pe.matmul(bank[3][0:32, 0:1], sox[:].rearrange("p a b -> p (a b)"), ones[0:N, 0:1], start=True,
                      stop=True).then_inc(S("own_done"), 1)
            pe.wait_ge(S("qsT_ready"), 1)
            pe.wait_ge(S("wukT_loaded"), 16)
            for h in range(H):
                mm = pe.matmul(bank[1][:, N * h:N * h + N], wukT[:, h, :], qsT[0:HD, h, :], start=True, stop=True)
            mm.then_inc(S("qa_done"), 1)
            for b in range(NPG // 2):
                if b >= RAW:
                    pe.wait_ge(S("squared"), b - RAW + 1)
                for j in range(2):
                    mm = pe.matmul(bank[4 + b % RAW][:, 256 * j:256 * j + 256], ckT[:, 2 * b + j, :], wuk[:],
                                   start=True, stop=True)
                mm.then_inc(S("raw_done"), 1)
            pe.wait_ge(S("qblk_ready"), 3)
            for half in range(2):
                for n in range(N):
                    at = PAGES * n + 4 * half
                    mm = pe.matmul(bank[half][0:32, :], qblk[:, n, :],
                                   ckT[:, at:at + 4, :].rearrange("p a b -> p (a b)"), start=n == 0, stop=n == N - 1)
                mm.then_inc(S("nope_done"), 1)
            for half in range(2):
                for g in range(2):
                    mm = pe.matmul(bank[2 + half][0:32, :], qrblk[:, g, :],
                                   krT[:, g, 4 * half:4 * half + 4, :].rearrange("p a b -> p (a b)"),
                                   start=g == 0, stop=g == 1)
                mm.then_inc(S("rope_done"), 1)
            pe.wait_ge(S("rinv_ready"), 1)
            for p in range(PAGES):
                mm = pe.transpose(bank[4 + p // 4][0:32, P * (p % 4):P * (p % 4) + P], ssq[:, p, :], ident)
            mm.then_inc(S("rT_done"), 1)
            pe.matmul(bank[6][0:32, 0:RANK], C("sel832")[0:N, :], ckvn[0:N, 2, :], start=True, stop=True)\
                .then_inc(S("rep_done"), 1)
            pe.wait_ge(S("p_ready"), 1)
            for p in range(PAGES):
                mm = pe.transpose(bank[7][:, 32 * p:32 * p + 32], sc[:, P * p:P * p + P], ident[0:32, 0:32])
            mm.then_inc(S("pT_done"), 1)
            pe.wait_ge(S("pblk_ready"), 1)
            for p in range(PAGES):
                for n in range(N):
                    i = N * p + n
                    mm = pe.matmul(bank[5][0:32, 0:RANK], pblk[:, p, n, :], ck[:, PAGES * n + p, :], start=i == 0,
                                   stop=i == NPG - 1)
            mm.then_inc(S("lat_done"), 1)
            pe.wait_ge(S("lat_ready"), 1)
            pe.transpose(bank[4][:, 0:32], lat[:], ident[0:32, 0:32]).then_inc(S("latT_done"), 1)
            pe.wait_ge(S("latT_ready"), 1)
            pe.wait_ge(S("wuv_loaded"), 16)
            for h in range(H):
                o = HD * (h % 2)
                mm = pe.matmul(bank[h // 2][o:o + HD, 0:T], wuv[:, HD * h:HD * h + HD], latT[:, h, :], start=True,
                               stop=True)
            mm.then_inc(S("out_done"), 1)

        @ph.b.scalar
        def _(act):
            for b in range(NPG // 2):
                act.wait_ge(S("raw_done"), b + 1)
                if b >= RAW:
                    act.wait_ge(S("summed"), b - RAW + 1)
                nc.scalar.activation(sqr[:, b % RAW, :], bank[4 + b % RAW][:], ACT.Square)\
                    .then_inc(S("squared"), 1)
            act.wait_ge(S("summed"), NPG // 2)
            nc.scalar.activation(ssq[:], ssq[:], ACT.Sqrt, bias=E["epsc"][:], scale=1.0 / HD)\
                .then_inc(S("root_ready"), 1)
            act.wait_ge(S("shift"), 1)
            nc.scalar.activation(sc[:], sc[:], ACT.Exp, scale=MLA_SCALE).then_inc(S("exp_done"), 1)
            act.wait_ge(S("out_done"), 1)
            for t in range(2):
                nc.scalar.copy(brT[:, 2 + t, :], bank[t][:, 0:T])

        @ph.b.vector
        def _(dve):
            step = E["stepper"](ph, dve, "dve_step")
            tt, red = nc.vector.tensor_tensor, nc.vector.tensor_reduce
            q3 = q[0:N, 2, :].rearrange("p (h e) -> p h e", h=H)
            step(nc.vector.tensor_copy(qrep[:], q3[:, :, HD:QK].unsqueeze(2).to_broadcast([N, H, 4, ROPE])),
                 "qrep_ready", wait=False)
            step(tt(prod[:], q[0:N, 2, :], kc[0:N, 2, :], ALU.mult))
            step(red(so[:], prod[:].rearrange("p (h e) -> p h e", h=H), AX.X, ALU.add))
            step(tt(sox[:], C("sel832")[0:N].rearrange("p (n h) -> p n h", n=N),
                    so[:].unsqueeze(1).to_broadcast([N, N, H]), ALU.mult), "sox_ready", wait=False)
            dve.wait_ge(S("qsT_done"), 1)
            step(nc.vector.tensor_scalar(qsT[0:HD].rearrange("p h n -> p (h n)"), bank[0][0:HD, 0:H * N],
                                         V("kn_g")[0:HD], None, ALU.mult), "qsT_ready", wait=False)
            dve.wait_ge(S("qr_done"), 1)
            step(nc.vector.tensor_copy(qr[:], bank[2][:, 0:H * N].rearrange("p (h n) -> p n h", h=H)))
            step(tt(qrblk[:], C("qr", 2, 32), qr[:].rearrange("p n h -> p (n h)").unsqueeze(1)
                    .to_broadcast([P, 2, 32]), ALU.mult), "qblk_ready", wait=False)
            dve.wait_ge(S("qa_done"), 1)
            step(nc.vector.tensor_copy(qa[:], bank[1][:, 0:H * N].rearrange("p (h n) -> p n h", h=H)))
            step(tt(qblk[:], C("m832", N, 32), qa[:].rearrange("p n h -> p (n h)").unsqueeze(1)
                    .to_broadcast([P, N, 32]), ALU.mult), "qblk_ready", wait=False)
            dve.wait_ge(S("own_done"), 1)
            step(nc.vector.tensor_copy(sc[:, PAGES * P:], bank[3][0:32, 0:1]), "qblk_ready")
            for b in range(NPG // 2):
                n, p = b // 4, 2 * (b % 4)
                dve.wait_ge(S("squared"), b + 1)
                step(red(ssq[:, p:p + 2, H * n:H * n + H],
                         sqr[:, b % RAW, :].rearrange("p (j h e) -> p j h e", j=2, h=H), AX.X, ALU.add), "summed",
                     wait=False)
            dve.wait_ge(S("root_ready"), 1)
            step(nc.vector.reciprocal(ssq[:], ssq[:]), "rinv_ready", wait=False)
            dve.wait_ge(S("rT_done"), 1)
            for half in range(2):
                step(nc.vector.tensor_copy(rT[:, 512 * half:512 * half + 512], bank[4 + half][0:32, :]))
            for half in range(2):
                at = slice(512 * half, 512 * half + 512)
                dve.wait_ge(S("nope_done"), half + 1)
                step(tt(sc[:, at], rT[:, at], bank[half][0:32, :], ALU.mult))
                dve.wait_ge(S("rope_done"), half + 1)
                step(tt(sc[:, at], sc[:, at], bank[2 + half][0:32, :], ALU.add))
            step(red(mx[:], sc[:], AX.X, ALU.max))
            step(nc.vector.tensor_scalar(sc[:], sc[:], mx[:], None, ALU.subtract), "shift", wait=False)
            dve.wait_ge(S("exp_done"), 1)
            step(red(mx[:], sc[:], AX.X, ALU.add))
            step(nc.vector.reciprocal(mx[:], mx[:]))
            step(nc.vector.tensor_scalar(sc[:], sc[:], mx[:], None, ALU.mult), "p_ready")
            dve.wait_ge(S("rep_done"), 1)
            step(nc.vector.tensor_copy(own[:], bank[6][0:32, 0:RANK]))
            dve.wait_ge(S("pT_done"), 1)
            step(nc.vector.tensor_copy(pT[:].rearrange("p a b -> p (a b)"), bank[7][:, 0:PAGES * 32]))
            for p in range(PAGES):
                last = tt(pblk[:, p], C("m832", N, 32), pT[:, p].unsqueeze(1).to_broadcast([P, N, 32]), ALU.mult)
                step(last, *(["pblk_ready"] if p == PAGES - 1 else []))
            dve.wait_ge(S("lat_done"), 1)
            step(nc.vector.scalar_tensor_tensor(lat[:], own[:], sc[:, PAGES * P:], bank[5][0:32, 0:RANK], ALU.mult,
                                                ALU.add), "lat_ready", wait=False)
            dve.wait_ge(S("latT_done"), 1)
            step(nc.vector.tensor_copy(latT[:, :, NP_TOK:T], bank[4][:, 0:32].rearrange("p (n h) -> p h n", h=H)),
                 "latT_ready", wait=False)


def gdn(nc, A, E, l):
    zT, tm, brT, bank, C, V, R, ones = (E[k] for k in ("zT", "tm", "brT", "bank", "C", "V", "R", "ones"))
    N = NS_TOK
    GS = 3 * HD + 2
    with E["Phase"]("gdn") as ph:
        S = ph.sem
        y = ph.sb("y", [P, 6, T])
        sq = ph.sb("sq", [P, 4, T])
        buf = ph.sb("buf", [P, 6, 3, N])
        gb = ph.sb("gb", [P, 2, 3, H])
        e1 = ph.sb("e1", [P, 2, 3, H])
        sp1 = ph.sb("sp1", [P, 3, 3, H])
        alog = ph.sb("alog", [P, H])
        G = ph.sb("G", [P, 2, H])
        wG = ph.sb("wG", [P, 3, 2, H])
        rep = ph.sb("rep", [P, 2, 2, H, P])
        D = ph.sb("D", [P, 2, H, P])
        EG = ph.sb("EG", [P, 2, H, P])
        bB = ph.sb("bB", [P, 2, H, P])
        AT = ph.sb("AT", [P, 2, H, P])
        PT = ph.sb("PT", [P, 2, H, P])
        MT = ph.sb("MT", [P, 2, H, P])
        P1 = ph.sb("P1", [P, 2, H, P])
        X = ph.sb("X", [P, 2, H, P])
        XT = ph.sb("XT", [P, 2, H, P])
        qg = ph.sb("qg", [P, 2, NP_TOK])
        kv = ph.sb("kv", [P, 2, 512])
        ST = ph.sb("ST", [P, 2, HD])
        Rr = ph.sb("Rr", [P, 2, H, HD])
        u = ph.sb("u", [P, 2, H, HD])
        oT = ph.sb("oT", [P, 2, T])
        osq = ph.sb("osq", [P, 2, T])
        zg = ph.sb("zg", [P, 2, T])
        gs = ph.sb("gs", [N, H, GS])
        rs = ph.sb("rs", [P, GS])
        st = ph.sb("st", [P, 16, HD])
        pr = ph.sb("pr", [P, 16, HD])
        v16 = ph.sb("v16", [P, 4, 16])
        sc1 = ph.sb("sc1", [P, 2])
        oX = ph.sb("oX", [P, 16, 16])
        raw = zT[:, FM_QKV:FM_QKV + 6, :]
        ident = C("ident")

        def by_parity(a, par):
            return a.rearrange("p (a b) t -> p b a t", b=2)[:, par]

        @ph.b.sync
        def _(sp):
            sp.dma_start(buf[:], A["sconv"][l]).then_inc(S("buf_loaded"), 16)
            sp.dma_start(st[:], A["sgdn"][l]).then_inc(S("state_loaded"), 16)
            sp.dma_start(A["o_conv"][l], raw[:, :, NP_TOK - 3:NP_TOK]).then_inc(S("stored"), 16)
            sp.dma_start(A["o_convs"][l, :, :, 2, :], raw[:, :, NP_TOK:T]).then_inc(S("stored"), 16)
            sp.wait_ge(S("buf_loaded"), 16)
            for i in range(2):
                sp.dma_start(A["o_convs"][l, :, :, i, :], buf[:, :, i + 1, :]).then_inc(S("stored"), 16)
            sp.wait_ge(S("state_s_ready"), 1)
            sp.dma_start(A["o_gdns"][l], st[:]).then_inc(S("stored"), 16)
            sp.wait_ge(S("state_ready"), 8)
            sp.dma_start(A["o_gdn"][l], ST[:]).then_inc(S("stored"), 16)
            sp.wait_ge(S("stored"), 96)

        @ph.b.tensor
        def _(pe):
            pe.wait_ge(S("sq_ready"), 1)
            for t in range(4):
                mm = pe.matmul(bank[t][:, 0:T], C("blk"), sq[:, t, :], start=True, stop=True)
            mm.then_inc(S("ss_done"), 1)
            pe.wait_ge(S("gb_ready"), 3)
            for j in range(2):
                mm = pe.matmul(bank[4 + j][:, 0:H], C("tri"), gb[:, 1, j, :], start=True, stop=True)
            mm.then_inc(S("G_done"), 1)
            pe.wait_ge(S("rep_ready"), 4)
            pe.wait_ge(S("G_ready"), 2)
            pe.wait_ge(S("roots_taken"), 4)
            pe.wait_ge(S("qk_ready"), 2)
            for j in range(2):
                for h in range(H):
                    pe.matmul(bank[4 * j][:, P * h:P * h + P], rep[:, 1, j, h, :], C("tri"), start=True, stop=True)
                for h in range(H):
                    mm = pe.matmul(bank[4 * j + 1][:, P * h:P * h + P], rep[:, 0, j, h, :], ident, start=True,
                                   stop=True)
                mm.then_inc(S("rows_done"), 1)
                for h in range(H):
                    o, a, c = HD * (h % 2), h // 2, slice(P * j, P * j + P)
                    for i in range(2):
                        mm = pe.matmul(bank[4 * j + 2 + h % 2][:, P * (2 * i + a):P * (2 * i + a) + P],
                                       y[o:o + HD, 2 + a, c], y[o:o + HD, 2 * (1 - i) + a, c], start=True, stop=True)
                    mm.then_inc(S("kq_done"), 1)
            for j in range(2):
                pe.wait_ge(S(f"mt{j}_ready"), 1)
                pe.wait_ge(S("kq_read"), 8)
                for h in range(H):
                    mm = pe.matmul(bank[4 * j][:, P * h:P * h + P], MT[:, j, h, :], ident, start=True, stop=True)
                mm.then_inc(S(f"p1{j}_done"), 1)
            with pe.Fori(1, 7) as k:
                for j in range(2):
                    pe.wait_ge(S(f"mt{j}_ready"), k + 1)
                    pe.wait_ge(S(f"x{j}_ready"), 2 * k)
                    for h in range(H):
                        mm = pe.matmul(bank[4 * j][:, P * h:P * h + P], MT[:, j, h, :], X[:, j, h, :], start=True,
                                       stop=True)
                    mm.then_inc(S(f"p1{j}_done"), 1)
                for j in range(2):
                    pe.wait_ge(S(f"p1{j}_copied"), k)
                    for h in range(H):
                        mm = pe.matmul(bank[4 * j + 1][:, P * h:P * h + P], XT[:, j, h, :], P1[:, j, h, :],
                                       start=True, stop=True)
                    for h in range(H):
                        mm = pe.matmul(bank[4 * j + 2][:, P * h:P * h + P], P1[:, j, h, :], XT[:, j, h, :],
                                       start=True, stop=True)
                    mm.then_inc(S(f"xp{j}_done"), 1)
            pe.wait_ge(S("x0_ready"), 14)
            pe.wait_ge(S("x1_ready"), 14)
            for j in range(2):
                for i in range(4):
                    mm = pe.transpose(bank[j][:, P * i:P * i + P], y[:, 2 + i, P * j:P * j + P], ident)
                mm.then_inc(S("kvT_done"), 1)
            for i in range(6):
                mm = pe.transpose(bank[2 + i // 4][0:N, P * (i % 4):P * (i % 4) + P], y[:, i, NP_TOK:T], ident)
            mm.then_inc(S("sT_done"), 1)
            pe.wait_ge(S("gs_ready"), 4)
            for h in range(H):
                mm = pe.matmul(bank[7][:, 0:GS], C("selg", H, P)[0:N, h, :], gs[:, h, :], start=h == 0,
                               stop=h == H - 1)
            mm.then_inc(S("rs_done"), 1)
            pe.wait_ge(S("kv_ready"), 2)
            pe.wait_ge(S("qg_ready"), 8)
            for j in range(2):
                c = slice(P * j, P * j + P)
                pe.wait_ge(S("state_ready"), 4 * j) if j else pe.wait_ge(S("state_zeroed"), 1)
                for h in range(H):
                    o, a = HD * (h % 2), h // 2
                    mm = pe.matmul(bank[h % 2][:, HD * a:HD * a + HD], y[o:o + HD, 2 + a, c], ST[o:o + HD, a, :],
                                   start=True, stop=True)
                mm.then_inc(S("kS_done"), 1)
                if j:
                    pe.wait_ge(S("o_read"), 2)
                for h in range(H):
                    o, a = HD * (h % 2), h // 2
                    mm = pe.matmul(bank[3 + h % 2][o:o + HD, P * a:P * a + P], ST[o:o + HD, a, :], qg[o:o + HD, a, c],
                                   start=True, stop=True)
                pe.wait_ge(S("R_ready"), j + 1)
                for h in range(H):
                    mm = pe.matmul(bank[2][:, HD * h:HD * h + HD], XT[:, j, h, :], Rr[:, j, h, :], start=True,
                                   stop=True)
                mm.then_inc(S("u_done"), 1)
                pe.wait_ge(S("u_ready"), 2 * j + 1)
                for h in range(H):
                    o, a = HD * (h % 2), h // 2
                    mm = pe.matmul(bank[5][o:o + HD, P * a:P * a + P], u[:, 0, h, :], PT[:, j, h, :], start=True,
                                   stop=True)
                mm.then_inc(S("o_done"), 1)
                pe.wait_ge(S("u_ready"), 2 * j + 2)
                for h in range(H):
                    o, a = HD * (h % 2), h // 2
                    mm = pe.matmul(bank[6][o:o + HD, HD * a:HD * a + HD], kv[:, j, HD * h:HD * h + HD],
                                   u[:, 1, h, :], start=True, stop=True)
                mm.then_inc(S("ku_done"), 1)
            pe.wait_ge(S("oX_ready"), 1)
            for t in range(2):
                mm = pe.matmul(bank[7][:, N * t:N * t + N], oX[:, 8 * t:8 * t + 8, :].rearrange("p a b -> p (a b)"),
                               C("seln"), start=True, stop=True)
            mm.then_inc(S("os_done"), 1)
            pe.wait_ge(S("osq_ready"), 1)
            for t in range(2):
                mm = pe.matmul(bank[t][:, 0:T], C("blk"), osq[:, t, :], start=True, stop=True)
            mm.then_inc(S("oss_done"), 1)

        @ph.b.scalar
        def _(act):
            eps = E["epsc"][:]
            act.wait_ge(S("conv_ready"), 1)
            nc.scalar.activation(y[:], y[:], ACT.Silu).then_inc(S("silu_done"), 1)
            nc.scalar.activation(zg[:], zT[:, FM_ZG:FM_ZG + 2, :], ACT.Silu)
            act.wait_ge(S("ss_done"), 1)
            for t in range(4):
                nc.scalar.activation(sq[:, t, :], bank[t][:, 0:T], ACT.Sqrt, bias=eps).then_inc(S("roots_taken"), 1)
            act.wait_ge(S("neg_ready"), 2)
            nc.scalar.activation(e1[:], e1[:], ACT.Exp, scale=-1.0).then_inc(S("e1_done"), 1)
            nc.scalar.activation(alog[:], R("a_log"), ACT.Exp).then_inc(S("e1_done"), 1)
            act.wait_ge(S("one_plus_ready"), 2)
            nc.scalar.activation(sp1[:, 1], sp1[:, 0], ACT.Ln).then_inc(S("ln_done"), 1)
            for j in range(2):
                act.wait_ge(S("rows_done"), j + 1)
                nc.scalar.activation(EG[:, j].rearrange("p h t -> p (h t)"), bank[4 * j][:], ACT.Exp)\
                    .then_inc(S("EG_done"), 1)
                nc.scalar.copy(bB[:, j].rearrange("p h t -> p (h t)"), bank[4 * j + 1][:]).then_inc(S("bB_done"), 1)
                act.wait_ge(S("D_shifted"), j + 1)
                nc.scalar.activation(D[:, j], D[:, j], ACT.Exp).then_inc(S("D_done"), 1)
            act.wait_ge(S("wG_shifted"), 2)
            nc.scalar.activation(wG[:, 2], wG[:, 2], ACT.Exp).then_inc(S("wG_done"), 1)
            nc.scalar.activation(wG[:, 0], G[:], ACT.Exp).then_inc(S("wG_done"), 1)
            nc.scalar.activation(e1[:, 1], gb[:, 1], ACT.Exp).then_inc(S("wG_done"), 1)
            with act.Fori(1, 7) as k:
                for j in range(2):
                    act.wait_ge(S(f"p1{j}_done"), k + 1)
                    nc.scalar.copy(P1[:, j].rearrange("p h t -> p (h t)"), bank[4 * j][:])\
                        .then_inc(S(f"p1{j}_copied"), 1)
            for j in range(2):
                act.wait_ge(S("kvT_done"), j + 1)
                nc.scalar.copy(kv[:, j], bank[j][:]).then_inc(S("kv_ready"), 1)
            act.wait_ge(S("oss_done"), 1)
            for t in range(2):
                nc.scalar.activation(osq[:, t, :], bank[t][:, 0:T], ACT.Sqrt, bias=eps, scale=1.0 / HD)\
                    .then_inc(S("oroot_ready"), 1)

        @ph.b.vector
        def _(dve):
            step = E["stepper"](ph, dve, "dve_step")
            v = nc.vector
            tt, ts, stt, red = v.tensor_tensor, v.tensor_scalar, v.scalar_tensor_tensor, v.tensor_reduce
            for t in range(6):
                step(ts(y[:, t, :], raw[:, t, :], V("conv", 18 + t), None, ALU.mult), wait=t == 5)
            for i in range(1, 4):
                for t in range(6):
                    step(stt(y[:, t, i:NP_TOK], raw[:, t, 0:NP_TOK - i], V("conv", 6 * (3 - i) + t),
                             y[:, t, i:NP_TOK], ALU.mult, ALU.add), wait=t == 5)
            dve.wait_ge(S("buf_loaded"), 16)
            for i in range(3):
                for t in range(6):
                    last = stt(y[:, t, NP_TOK:T], buf[:, t, i, :], V("conv", 6 * i + t), y[:, t, NP_TOK:T], ALU.mult,
                               ALU.add)
                    if i == 2 and t == 5:
                        step(last, "conv_ready", wait=False)
                    else:
                        step(last, wait=t == 5)
            dve.wait_ge(S("silu_done"), 1)
            step(tt(sq[:], y[:, 0:4, :], y[:, 0:4, :], ALU.mult), "sq_ready", wait=False)
            step(v.tensor_copy(e1[:, 0], tm[:, :, TM_BETA:TM_BETA + H]), "neg_ready")
            step(tt(gb[:, 1], tm[:, :, TM_ALPHA:TM_ALPHA + H], R("dt").unsqueeze(1).to_broadcast([P, 3, H]), ALU.add))
            step(ts(sp1[:, 0], gb[:, 1], -1.0, None, ALU.mult))
            step(tt(e1[:, 1], gb[:, 1], sp1[:, 0], ALU.max), "neg_ready")
            dve.wait_ge(S("e1_done"), 2)
            step(ts(sp1[:, 0], e1[:, 1], 1.0, None, ALU.add), "one_plus_ready")
            step(ts(gb[:, 0], e1[:, 0], 1.0, None, ALU.add), "one_plus_ready")
            step(v.reciprocal(gb[:, 0], gb[:, 0]), "gb_ready")
            step(ts(sp1[:, 2], sp1[:, 0], -1.0, None, ALU.add))
            dve.wait_ge(S("ln_done"), 1)
            step(ts(sp1[:, 0], sp1[:, 2], 1e-30, None, ALU.max))
            step(v.reciprocal(sp1[:, 0], sp1[:, 0]))
            step(tt(sp1[:, 1], sp1[:, 1], sp1[:, 0], ALU.mult))
            step(ts(sp1[:, 2], sp1[:, 2], 0.0, None, ALU.is_equal))
            step(tt(sp1[:, 1], sp1[:, 1], sp1[:, 2], ALU.add))
            step(tt(sp1[:, 1], sp1[:, 1], e1[:, 1], ALU.mult))
            step(stt(gb[:, 1], gb[:, 1], 0.0, sp1[:, 1], ALU.max, ALU.add), "gb_ready")
            step(stt(gb[:, 1], gb[:, 1], -1.0, alog[:].unsqueeze(1).to_broadcast([P, 3, H]), ALU.mult, ALU.mult),
                 "gb_ready")
            for i in range(2):
                for j in range(2):
                    step(v.tensor_copy(rep[:, i, j], gb[:, i, j].unsqueeze(2).to_broadcast([P, H, P])), "rep_ready",
                         wait=False)
            dve.wait_ge(S("roots_taken"), 4)
            step(v.reciprocal(sq[:], sq[:]))
            step(stt(y[:, 0:2, :], y[:, 0:2, :], HD ** -0.5, sq[:, 0:2, :], ALU.mult, ALU.mult), "qk_ready",
                 wait=False)
            step(tt(y[:, 2:4, :], y[:, 2:4, :], sq[:, 2:4, :], ALU.mult), "qk_ready")
            dve.wait_ge(S("G_done"), 1)
            for j in range(2):
                step(v.tensor_copy(G[:, j], bank[4 + j][:, 0:H]), "G_ready")
            for j in range(2):
                dve.wait_ge(S("rows_done"), j + 1)
                g4 = bank[4 * j][:].rearrange("p (h t) -> p h t", h=H)
                dve.wait_ge(S("EG_done"), j + 1)
                step(tt(D[:, j], g4, G[:, j].unsqueeze(2).to_broadcast([P, H, P]), ALU.subtract))
                step(tt(wG[:, 2, j], g4[:, :, P - 1], G[:, j], ALU.subtract), "wG_shifted")
                step(ts(D[:, j], D[:, j], 0.0, None, ALU.min), "D_shifted", wait=False)
                dve.wait_ge(S("D_done"), j + 1)
                step(tt(D[:, j], D[:, j], C("tri").unsqueeze(1).to_broadcast([P, H, P]), ALU.mult))
                dve.wait_ge(S("bB_done"), j + 1)
                dve.wait_ge(S("kq_done"), 4 * j + 4)
                for par in range(2):
                    kq = bank[4 * j + 2 + par][:].rearrange("p (i a t) -> p i a t", i=2, a=2)
                    step(tt(by_parity(AT[:, j], par), kq[:, 0], by_parity(D[:, j], par), ALU.mult), "kq_read")
                    step(tt(by_parity(PT[:, j], par), kq[:, 1], by_parity(D[:, j], par), ALU.mult), "kq_read")
                step(tt(AT[:, j], AT[:, j], bB[:, j], ALU.mult))
                step(tt(MT[:, j], AT[:, j], C("lev", 7, P)[:, 0:1].to_broadcast([P, H, P]), ALU.mult),
                     f"mt{j}_ready")
            eye = ident.unsqueeze(1).to_broadcast([P, H, P])
            for j in range(2):
                step(tt(XT[:, j], eye, MT[:, j], ALU.subtract), f"x{j}_ready", wait=False)
                dve.wait_ge(S(f"p1{j}_done"), 1)
                step(tt(X[:, j], eye, bank[4 * j][:].rearrange("p (h t) -> p h t", h=H), ALU.subtract),
                     f"x{j}_ready", wait=False)
            with dve.Fori(1, 7) as k:
                for j in range(2):
                    dve.wait_ge(S(f"p1{j}_done"), k)
                    dve.wait_ge(S(f"x{j}_ready"), 2 * k)
                    tt(MT[:, j], AT[:, j], C("lev", 7, P)[:, bass.ds(k, 1)].to_broadcast([P, H, P]), ALU.mult)\
                        .then_inc(S(f"mt{j}_ready"), 1)
                for j in range(2):
                    dve.wait_ge(S(f"xp{j}_done"), k)
                    tt(X[:, j].rearrange("p h t -> p (h t)"), X[:, j].rearrange("p h t -> p (h t)"),
                       bank[4 * j + 1][:], ALU.subtract).then_inc(S(f"x{j}_ready"), 1)
                    tt(XT[:, j].rearrange("p h t -> p (h t)"), XT[:, j].rearrange("p h t -> p (h t)"),
                       bank[4 * j + 2][:], ALU.subtract).then_inc(S(f"x{j}_ready"), 1)
            dve.wait_ge(S("wG_done"), 3)
            step(tt(wG[:, 1], wG[:, 0], gb[:, 0, 0:2], ALU.mult))
            for j in range(2):
                for h in range(H):
                    o, a = HD * (h % 2), h // 2
                    c = slice(P * j, P * j + P)
                    step(tt(qg[o:o + HD, a, c], y[o:o + HD, a, c], EG[o:o + HD, j, h, :], ALU.mult), "qg_ready",
                         wait=False)
            step(v.memset(ST[:], 0.0), "state_zeroed")
            dve.wait_ge(S("sT_done"), 1)
            step(v.tensor_copy(gs[:, :, 0:2 * HD].rearrange("p h (s e) -> p h s e", s=2),
                               bank[2][0:N, :].rearrange("p (s h e) -> p h s e", s=2, h=H)), "gs_ready")
            step(v.tensor_copy(gs[:, :, 2 * HD:3 * HD], bank[3][0:N, 0:256].rearrange("p (h e) -> p h e", h=H)),
                 "gs_ready")
            step(v.tensor_copy(gs[:, :, 3 * HD], gb[0:N, 0, 2, :]), "gs_ready")
            step(v.tensor_copy(gs[:, :, 3 * HD + 1], e1[0:N, 1, 2, :]), "gs_ready")
            for j in range(2):
                dve.wait_ge(S("kv_ready"), j + 1)
                step(tt(Rr[:, j], kv[:, j, 256:512].rearrange("p (h e) -> p h e", h=H),
                        gb[:, 0, j].unsqueeze(2).to_broadcast([P, H, HD]), ALU.mult))
                dve.wait_ge(S("kS_done"), j + 1)
                for par in range(2):
                    w = wG[:, 1, j].rearrange("p (a b) -> p b a", b=2)[:, par].unsqueeze(2).to_broadcast([P, 2, HD])
                    step(tt(by_parity(u[:, 1], par), bank[par][:, 0:P].rearrange("p (a e) -> p a e", a=2), w,
                            ALU.mult))
                step(tt(Rr[:, j], Rr[:, j], u[:, 1], ALU.subtract), "R_ready", wait=False)
                dve.wait_ge(S("u_done"), j + 1)
                u4 = bank[2][:, 0:H * HD].rearrange("p (h e) -> p h e", h=H)
                step(v.tensor_copy(u[:, 0], u4), "u_ready", wait=False)
                step(tt(u[:, 1], u4, wG[:, 2, j].unsqueeze(2).to_broadcast([P, H, HD]), ALU.mult), "u_ready",
                     wait=False)
                dve.wait_ge(S("o_done"), j + 1)
                for par in range(2):
                    o = HD * par
                    p4 = bank[3 + par][o:o + HD, 0:256].rearrange("p (a t) -> p a t", a=2)
                    step(v.tensor_copy(oT[o:o + HD, :, P * j:P * j + P], p4))
                    step(tt(oT[o:o + HD, :, P * j:P * j + P], oT[o:o + HD, :, P * j:P * j + P],
                            bank[5][o:o + HD, 0:256].rearrange("p (a t) -> p a t", a=2), ALU.add), "o_read")
                dve.wait_ge(S("ku_done"), j + 1)
                for h in range(H):
                    o, a = HD * (h % 2), h // 2
                    step(stt(ST[o:o + HD, a, :], ST[o:o + HD, a, :], EG[o:o + HD, j, h, P - 1:P],
                             bank[6][o:o + HD, HD * a:HD * a + HD], ALU.mult, ALU.add), "state_ready")
            dve.wait_ge(S("rs_done"), 1)
            step(v.tensor_copy(rs[:], bank[7][:, 0:GS]))
            dve.wait_ge(S("state_loaded"), 16)
            qv, kvec, beta, eg = rs[:, 0:HD], rs[:, HD:2 * HD], rs[:, 3 * HD:3 * HD + 1], rs[:, 3 * HD + 1:GS]
            wide = [P, 16, HD]
            step(tt(v16[:], rs[:, 2 * HD:3 * HD].rearrange("p (a b) -> p a b", a=4),
                    C("mv").unsqueeze(2).to_broadcast([P, 4, 16]), ALU.mult))
            step(red(oX[:, 0, :], v16[:].rearrange("p a b -> p b a"), AX.X, ALU.add))
            step(tt(pr[:], st[:], kvec.unsqueeze(1).to_broadcast(wide), ALU.mult))
            step(red(v16[:, 0, :], pr[:], AX.X, ALU.add))
            step(tt(pr[:], st[:], qv.unsqueeze(1).to_broadcast(wide), ALU.mult))
            step(red(v16[:, 1, :], pr[:], AX.X, ALU.add))
            step(ts(v16[:, 0, :], v16[:, 0, :], eg, beta, ALU.mult, ALU.mult))
            step(stt(v16[:, 2, :], oX[:, 0, :], beta, v16[:, 0, :], ALU.mult, ALU.subtract))
            step(tt(pr[:, 0, :], qv, kvec, ALU.mult))
            step(red(sc1[:, 0:1], pr[:, 0, :], AX.X, ALU.add))
            step(ts(v16[:, 1, :], v16[:, 1, :], eg, None, ALU.mult))
            step(stt(v16[:, 3, :], v16[:, 2, :], sc1[:, 0:1], v16[:, 1, :], ALU.mult, ALU.add))
            step(tt(pr[:], v16[:, 2, :].unsqueeze(2).to_broadcast(wide), kvec.unsqueeze(1).to_broadcast(wide),
                    ALU.mult))
            step(stt(st[:].rearrange("p a b -> p (a b)"), st[:].rearrange("p a b -> p (a b)"), eg,
                     pr[:].rearrange("p a b -> p (a b)"), ALU.mult, ALU.add), "state_s_ready", wait=False)
            step(tt(oX[:], C("m16").unsqueeze(2).to_broadcast([P, 16, 16]),
                    v16[:, 3, :].unsqueeze(1).to_broadcast([P, 16, 16]), ALU.mult), "oX_ready")
            dve.wait_ge(S("os_done"), 1)
            step(v.tensor_copy(oT[:, :, NP_TOK:T], bank[7][:, 0:2 * N].rearrange("p (t n) -> p t n", t=2)))
            step(tt(osq[:], oT[:], oT[:], ALU.mult), "osq_ready", wait=False)
            dve.wait_ge(S("oroot_ready"), 2)
            step(v.reciprocal(osq[:], osq[:]))
            step(tt(oT[:], oT[:], osq[:], ALU.mult))
            step(stt(brT[:, 4:6, :], oT[:], V("gdn_g"), zg[:], ALU.mult, ALU.mult))


def mix(nc, A, E, l):
    xT, hT, brT, bank = (E[k] for k in ("xT", "hT", "brT", "bank"))
    with E["Phase"]("mix") as ph:
        S = ph.sem
        w = [ph.sb(f"w{b}", [P, KT + 2, P]) for b in range(4)]
        wo = [ph.sb(f"wo{i}", [P, KT, P]) for i in range(4)]
        gate = ph.sb("gate", [P, 4, T])
        mixT = ph.sb("mixT", [P, KT, T])

        @ph.b.sync
        def _(sp):
            for b in range(4):
                sp.dma_start(w[b][:], A["w_gb"][l, 0, b]).then_inc(S(f"w{b}_loaded"), 16)
            for i in range(4):
                sp.dma_start(wo[i][:], A["w_out"][l, i]).then_inc(S(f"wo{i}_loaded"), 16)
            with sp.Fori(1, KT) as dt:
                for b in range(4):
                    src = A["w_gb"][l, dt, b]
                    sp.wait_ge(S(f"p{b}_done"), dt)
                    sp.dma_start(w[b][:], src).then_inc(S(f"w{b}_loaded"), 16)
            for i in range(4):
                sp.wait_ge(S("o_done"), i + 1)
                sp.dma_start(wo[i][:], A["w_out"][l, 4 + i]).then_inc(S(f"wo{i}_loaded"), 16)

        @ph.b.tensor
        def _(pe):
            def tile(dt):
                for b in range(4):
                    pe.wait_ge(S(f"w{b}_loaded"), 16 * dt + 16)
                    if not isinstance(dt, int):
                        pe.wait_ge(S(f"g{b}_read"), dt)
                    for k in range(KT):
                        mm = pe.matmul(bank[b][:, 0:T], w[b][:, k, :], hT[:, k, :], start=k == 0, stop=k == KT - 1)
                    mm.then_inc(S(f"g{b}_done"), 1)
                    if not isinstance(dt, int):
                        pe.wait_ge(S(f"p{b}_read"), dt)
                    for k in range(2):
                        mm = pe.matmul(bank[4 + b][:, 0:T], w[b][:, KT + k, :], brT[:, 2 * b + k, :], start=k == 0,
                                       stop=k == 1)
                    mm.then_inc(S(f"p{b}_done"), 1)

            tile(0)
            with pe.Fori(1, KT) as dt:
                tile(dt)
            pe.wait_ge(S("mix_ready"), KT)
            for dt in range(KT):
                i = dt % 4
                pe.wait_ge(S(f"wo{i}_loaded"), 16 * (dt // 4) + 16)
                if dt >= 4:
                    pe.wait_ge(S("x_ready"), dt - 3)
                for k in range(KT):
                    mm = pe.matmul(bank[i][:, 0:T], wo[i][:, k, :], mixT[:, k, :], start=k == 0, stop=k == KT - 1)
                mm.then_inc(S("o_done"), 1)

        @ph.b.scalar
        def _(act):
            def tile(dt):
                for b in range(4):
                    act.wait_ge(S(f"g{b}_done"), dt + 1)
                    if not isinstance(dt, int):
                        act.wait_ge(S(f"p{b}_read"), dt)
                    nc.scalar.activation(gate[:, b, :], bank[b][:, 0:T], ACT.Sigmoid).then_inc(S(f"g{b}_read"), 1)

            tile(0)
            with act.Fori(1, KT) as dt:
                tile(dt)

        @ph.b.vector
        def _(dve):
            with dve.Fori(0, KT) as dt:
                for b in range(4):
                    dve.wait_ge(S(f"g{b}_read"), dt + 1)
                    dve.wait_ge(S(f"p{b}_done"), dt + 1)
                    nc.vector.tensor_tensor(gate[:, b, :], gate[:, b, :], bank[4 + b][:, 0:T], ALU.mult)\
                        .then_inc(S(f"m{b}_done"), 1)
                    if b == 1:
                        dve.wait_ge(S("m0_done"), dt + 1)
                        dve.wait_ge(S("m1_done"), dt + 1)
                        nc.vector.tensor_tensor(mixT[:, bass.ds(dt, 1), :].squeeze(1), gate[:, 0, :], gate[:, 1, :],
                                                ALU.add).then_inc(S("a1_done"), 1)
                    if b >= 2:
                        dve.wait_ge(S(f"m{b}_done"), dt + 1)
                        dve.wait_ge(S(f"a{b - 1}_done"), dt + 1)
                        nc.vector.tensor_tensor(mixT[:, bass.ds(dt, 1), :].squeeze(1),
                                                mixT[:, bass.ds(dt, 1), :].squeeze(1), gate[:, b, :], ALU.add)\
                            .then_inc(S(f"a{b}_done" if b < 3 else "mix_ready"), 1)
                dve.wait_ge(S("mix_ready"), dt + 1)
                for b in range(4):
                    dve.sem_inc(S(f"p{b}_read"), 1)
            for dt in range(KT):
                dve.wait_ge(S("o_done"), dt + 1)
                nc.vector.tensor_tensor(xT[:, dt, :], xT[:, dt, :], bank[dt % 4][:, 0:T], ALU.add)\
                    .then_inc(S("x_ready"), 1)


def route(nc, A, E, l, M):
    xT, hT, ones, bank, C, V, R = (E[k] for k in ("xT", "hT", "ones", "bank", "C", "V", "R"))
    with E["Phase"]("route") as ph:
        S = ph.sem
        sq = ph.sb("sq", [P, KT, T])
        rstd = ph.sb("rstd", [P, T])
        wrt = ph.sb("wrt", [P, KT, 36])
        lg = ph.sb("lg", [P, 3, 36])
        m = ph.sb("m", [P, 8, 3])
        eg = ph.sb("eg", [P, 3, 4])
        ohg = ph.sb("ohg", [P, 3, 4])
        sel = ph.sb("sel", [P, 3, 4, 8])
        le = ph.sb("le", [P, 3, 8])
        oh = [ph.sb(f"oh{i}", [P, 3, 8]) for i in range(2)]
        OH = [ph.sb(f"OH{i}", [P, 3, NE]) for i in range(2)]
        both = ph.sb("both", [P, 3, NE])
        rank = ph.sb("rank", [P, 3, NE])
        tok = ph.sb("tok", [P, 3, 4])
        tokT = ph.sb("tokT", [4, T])
        selr = ph.sb("selr", [4, 4, P])
        rows = ph.sb("rows", [P, 4, T])
        ncnt = ph.sb("ncnt", [NE, 8])
        nrep = ph.sb("nrep", [NE, P])
        blk = ph.sb("blk", [NE, 1])
        jj = ph.sb("jj", [NE, ITEMS])
        table = ph.sb("table", [NE, 2, ITEMS])
        hTM = ph.sb("hTM", [P, 3, D_MODEL])
        G = ph.sb("G", [P, 3, SLOTS])
        HS, Q = M["HS"], M["Q"]

        @ph.b.sync
        def _(sp):
            sp.dma_start(wrt[:], A["w_rt"][l]).then_inc(S("wrt_loaded"), 16)
            sp.wait_ge(S("wrt_loaded"), 16)

        @ph.b.tensor
        def _(pe):
            ident = C("ident")
            pe.wait_ge(S("sq_ready"), 1)
            for k in range(KT):
                mm = pe.matmul(bank[0][:, 0:T], ones[:], sq[:, k, :], start=k == 0, stop=k == KT - 1)
            mm.then_inc(S("ss_done"), 1)
            pe.wait_ge(S("wrt_loaded"), 16)
            pe.wait_ge(S("h_ready"), KT)
            for c, (t0, n) in enumerate(CHUNKS):
                for k in range(KT):
                    mm = pe.matmul(bank[1 + c][0:n, 0:36], hT[:, k, t0:t0 + n], wrt[:, k, :], start=k == 0,
                                   stop=k == KT - 1)
                mm.then_inc(S("lg_done"), 1)
            for c, (t0, n) in enumerate(CHUNKS):
                for i in range(2):
                    b = 2 * c + i
                    if b >= 4:
                        pe.wait_ge(S("hTM_ready"), b - 3)
                    for k in range(4):
                        mm = pe.transpose(bank[4 + b % 4][0:n, P * k:P * k + P], hT[:, 4 * i + k, t0:t0 + n], ident)
                    mm.then_inc(S("hTM_done"), 1)
            pe.wait_ge(S("both_ready"), 1)
            for c in range(3):
                for b in range(c + 1):
                    mm = pe.matmul(bank[0][:, NE * c:NE * c + NE], C("stri") if b == c else ones[:], both[:, b, :],
                                   start=b == 0, stop=b == c)
            mm.then_inc(S("rank_done"), 1)
            for c in range(3):
                mm = pe.matmul(bank[1][0:NE, 0:1], both[:, c, :], ones[:, 0:1], start=c == 0, stop=c == 2)
            mm.then_inc(S("count_done"), 1)
            pe.wait_ge(S("count_ready"), 2)
            pe.matmul(bank[2][:, 0:NE], nrep[:], C("stri")[0:NE, 0:NE], start=True, stop=True)\
                .then_inc(S("off_done"), 1)
            pe.matmul(bank[3][0:NE, 0:2], C("stri")[0:NE, 0:NE], ncnt[:, 0:2], start=True, stop=True)
            pe.matmul(bank[3][0:NE, 2:4], ones[0:NE, 0:NE], ncnt[:, 0:2], start=True, stop=True)\
                .then_inc(S("off_done"), 1)
            pe.wait_ge(S("table_ready"), 1)
            pe.matmul(bank[1][:, 0:2 * ITEMS], ones[0:NE, :], table[:].rearrange("p a b -> p (a b)"), start=True,
                      stop=True).then_inc(S("items_done"), 1)
            pe.wait_ge(S("tok_ready"), 4)
            for c, (t0, n) in enumerate(CHUNKS):
                mm = pe.transpose(bank[2][0:4, t0:t0 + n], tok[0:n, c, :], ident[0:n, 0:n])
            mm.then_inc(S("tokT_done"), 1)
            pe.wait_ge(S("G_ready"), 3)
            pe.wait_ge(S("hTM_ready"), 6)
            for b in range(2 * KT):
                k, half = b // 2, b % 2
                if b >= 4:
                    pe.wait_ge(S("HS_ready"), b - 3)
                for c, (t0, n) in enumerate(CHUNKS):
                    mm = pe.matmul(bank[4 + b % 4][:, 0:T], hTM[0:n, c, P * k:P * k + P],
                                   G[0:n, c, T * half:T * half + T], start=c == 0, stop=c == 2)
                mm.then_inc(S("HS_done"), 1)
            pe.wait_ge(S("tokT_ready"), 1)
            for r in range(4):
                mm = pe.matmul(bank[r][:, 0:T], selr[:, r, :], tokT[:], start=True, stop=True)
            mm.then_inc(S("rows_done"), 1)

        @ph.b.scalar
        def _(act):
            act.wait_ge(S("ss_done"), 1)
            nc.scalar.activation(rstd[:], bank[0][:, 0:T], ACT.Sqrt, bias=E["epsc"][:], scale=1.0 / D_MODEL)\
                .then_inc(S("root_ready"), 1)
            for c, (t0, n) in enumerate(CHUNKS):
                for i in range(2):
                    b = 2 * c + i
                    act.wait_ge(S("hTM_done"), b + 1)
                    nc.scalar.copy(hTM[0:n, c, 512 * i:512 * i + 512], bank[4 + b % 4][0:n, :])\
                        .then_inc(S("hTM_ready"), 1)
            act.wait_ge(S("eg_shifted"), 1)
            nc.scalar.activation(eg[:], eg[:], ACT.Exp).then_inc(S("exp_done"), 1)
            act.wait_ge(S("p2_shifted"), 1)
            nc.scalar.activation(m[:, 5], m[:, 5], ACT.Exp).then_inc(S("exp_done"), 1)
            for b in range(2 * KT):
                k, half = b // 2, b % 2
                act.wait_ge(S("HS_done"), b + 1)
                nc.scalar.copy(HS[:, k, T * half:T * half + T], bank[4 + b % 4][:, 0:T]).then_inc(S("HS_ready"), 1)
            act.wait_ge(S("rows_done"), 1)
            for r in range(4):
                nc.scalar.copy(rows[:, r, :], bank[r][:, 0:T]).then_inc(S("rows_ready"), 1)

        @ph.b.vector
        def _(dve):
            step = E["stepper"](ph, dve, "dve_step")
            v = nc.vector
            tt, ts, stt, red = v.tensor_tensor, v.tensor_scalar, v.scalar_tensor_tensor, v.tensor_reduce
            step(tt(sq[:], xT[:], xT[:], ALU.mult), "sq_ready", wait=False)
            step(v.memset(lg[:], 0.0))
            step(v.memset(HS[:, :, SLOTS:SLOTS + W], 0.0), wait=False)
            step(v.tensor_copy(selr[:], C("ident")[0:4, 0:4].unsqueeze(2).to_broadcast([4, 4, P])), wait=False)
            dve.wait_ge(S("root_ready"), 1)
            step(v.reciprocal(rstd[:], rstd[:]))
            for k in range(KT):
                step(stt(hT[:, k, :], xT[:, k, :], V("g2", k), rstd[:], ALU.mult, ALU.mult), "h_ready", wait=False)
            for c, (t0, n) in enumerate(CHUNKS):
                dve.wait_ge(S("lg_done"), c + 1)
                step(tt(lg[0:n, c, :], bank[1 + c][0:n, 0:36], R("moe_b")[0:n], ALU.add))

            def first_max(onehot, x, top, at, n):
                wide = [P, 3, n]
                step(red(top, x, AX.X, ALU.max))
                step(tt(onehot, x, top.unsqueeze(2).to_broadcast(wide), ALU.is_equal))
                step(tt(onehot, onehot, C("rev")[:, 0:n].unsqueeze(1).to_broadcast(wide), ALU.mult))
                step(red(at, onehot, AX.X, ALU.max))
                step(tt(onehot, onehot, at.unsqueeze(2).to_broadcast(wide), ALU.is_equal))

            lgg = lg[:, :, 0:4]
            first_max(ohg[:], lgg, m[:, 0], m[:, 1], 4)
            step(tt(eg[:], lgg, m[:, 0].unsqueeze(2).to_broadcast([P, 3, 4]), ALU.subtract), "eg_shifted",
                 wait=False)
            step(tt(sel[:], lg[:, :, 4:36].rearrange("p c (g e) -> p c g e", g=4),
                    ohg[:].unsqueeze(3).to_broadcast([P, 3, 4, 8]), ALU.mult))
            step(red(le[:], sel[:].rearrange("p c g e -> p c e g"), AX.X, ALU.add))
            first_max(oh[0][:], le[:], m[:, 2], m[:, 1], 8)
            step(stt(le[:], oh[0][:], NEG, le[:], ALU.mult, ALU.add))
            first_max(oh[1][:], le[:], m[:, 3], m[:, 1], 8)
            step(tt(m[:, 5], m[:, 3], m[:, 2], ALU.subtract), "p2_shifted", wait=False)
            step(tt(ohg[:], ohg[:], C("valid").unsqueeze(2).to_broadcast([P, 3, 4]), ALU.mult))
            for i in range(2):
                for c in range(3):
                    step(tt(OH[i][:, c].rearrange("p (g e) -> p g e", g=4),
                            ohg[:, c].unsqueeze(2).to_broadcast([P, 4, 8]),
                            oh[i][:, c].unsqueeze(1).to_broadcast([P, 4, 8]), ALU.mult), wait=c == 2)
            step(tt(both[:], OH[0][:], OH[1][:], ALU.add), "both_ready")
            dve.wait_ge(S("count_done"), 1)
            step(v.tensor_copy(ncnt[:, 0:1], bank[1][0:NE, 0:1]))
            step(ts(nrep[:], ones[0:NE, :], ncnt[:, 0:1], None, ALU.mult), "count_ready")
            step(ts(ncnt[:, 1:2], ncnt[:, 0:1], 0.0, None, ALU.is_gt))
            for b in range(1, -(-T // W)):
                step(stt(ncnt[:, 1:2], ncnt[:, 0:1], float(b * W), ncnt[:, 1:2], ALU.is_gt, ALU.add),
                     *(["count_ready"] if b == -(-T // W) - 1 else []))
            dve.wait_ge(S("rank_done"), 1)
            dve.wait_ge(S("off_done"), 2)
            step(v.tensor_copy(rank[:], bank[0][:, 0:3 * NE].rearrange("p (c e) -> p c e", c=3)))
            step(tt(rank[:], rank[:], bank[2][:, 0:NE].unsqueeze(1).to_broadcast([P, 3, NE]), ALU.add))
            step(v.tensor_copy(ncnt[:, 2:6], bank[3][0:NE, 0:4]))
            for i in range(2):
                step(tt(OH[i][:], OH[i][:], rank[:], ALU.mult))
                step(red(tok[:, :, i], OH[i][:], AX.X, ALU.add), "tok_ready")
            step(ts(blk[:], ncnt[:, 5:6], -1.0, None, ALU.add))
            step(ts(jj[:], C("iota")[0:NE, 0:ITEMS], blk[:], None, ALU.min))
            step(tt(ncnt[:, 6:7], ncnt[:, 3:4], ncnt[:, 1:2], ALU.add))
            step(ts(table[:, 0], jj[:], ncnt[:, 6:7], None, ALU.is_ge))
            step(ts(table[:, 1], jj[:], ncnt[:, 3:4], None, ALU.is_ge))
            step(tt(table[:, 1], table[:, 1], table[:, 0], ALU.subtract))
            step(ts(jj[:], jj[:], ncnt[:, 3:4], float(W), ALU.subtract, ALU.mult))
            step(stt(table[:, 1], jj[:], ncnt[:, 2:3], table[:, 1], ALU.add, ALU.mult), "table_ready", wait=False)
            for c, (t0, n) in enumerate(CHUNKS):
                step(ts(G[:, c], C("iota"), tok[:, c, 0:1], None, ALU.is_equal))
                step(stt(G[:, c], C("iota"), tok[:, c, 1:2], G[:, c], ALU.is_equal, ALU.add), "G_ready")
            dve.wait_ge(S("exp_done"), 2)
            step(red(m[:, 4], eg[:], AX.X, ALU.add))
            step(ts(m[:, 6], m[:, 5], 1.0, None, ALU.add))
            step(tt(m[:, 6], m[:, 6], m[:, 4], ALU.mult))
            step(v.reciprocal(m[:, 6], m[:, 6]))
            step(v.tensor_copy(tok[:, :, 2], m[:, 6]), "tok_ready")
            step(tt(tok[:, :, 3], m[:, 6], m[:, 5], ALU.mult), "tok_ready")
            dve.wait_ge(S("items_done"), 1)
            step(v.tensor_copy(M["items"][:], bank[1][0:1, 0:2 * ITEMS]))
            dve.wait_ge(S("tokT_done"), 1)
            step(v.tensor_copy(tokT[:], bank[2][0:4, 0:T]), "tokT_ready")
            dve.wait_ge(S("rows_ready"), 4)
            for c in range(SCH):
                s = C("slot")[:, c:c + 1]
                step(stt(Q[:, c], rows[:, 0], s, rows[:, 2], ALU.is_equal, ALU.mult), wait=False)
                step(stt(G[:, 0, 0:T], rows[:, 1], s, rows[:, 3], ALU.is_equal, ALU.mult))
                step(tt(Q[:, c], Q[:, c], G[:, 0, 0:T], ALU.add))


def experts(nc, A, E, l, M):
    bank = E["bank"]
    HS, YS, items = M["HS"], M["YS"], M["items"]
    FT = 2
    PAIRS = ITEMS // 2
    with E["Phase"]("moe") as ph:
        S = ph.sem
        wg = [ph.sb(f"wg{s}", [P, KT, FT * P]) for s in range(2)]
        wu = [ph.sb(f"wu{s}", [P, KT, FT * P]) for s in range(2)]
        wd = [ph.sb(f"wd{s}", [P, FT, D_MODEL]) for s in range(2)]
        hb = [ph.sb(f"hb{s}", [P, KT, W]) for s in range(2)]
        sg = [ph.sb(f"sg{s}", [P, FT * W]) for s in range(2)]

        @ph.b.sync
        def _(sp):
            def load(i, s, what, first=False):
                j = 2 * i + s
                e = sp.value_load(items[0:1, bass.ds(j, 1)], min_val=0, max_val=NE - 1)
                if what == "gu":
                    g, u = A["w_g"][l, e], A["w_u"][l, e]
                    if not first:
                        sp.wait_ge(S("gu_done"), j - 1)
                    sp.dma_start(wg[s][:], g).then_inc(S(f"gu{s}_loaded"), 16)
                    sp.dma_start(wu[s][:], u).then_inc(S(f"gu{s}_loaded"), 16)
                else:
                    d = A["w_d"][l, e]
                    if not first:
                        sp.wait_ge(S("y_done"), 2 * j - 2)
                    sp.dma_start(wd[s][:], d).then_inc(S(f"d{s}_loaded"), 16)

            load(0, 0, "gu", first=True)
            load(0, 1, "gu", first=True)
            load(0, 0, "d", first=True)
            load(0, 1, "d", first=True)
            with sp.Fori(1, PAIRS) as i:
                for s in range(2):
                    load(i, s, "gu")
                    load(i, s, "d")
            load(PAIRS, 0, "gu")
            load(PAIRS, 0, "d")

        @ph.b.tensor
        def _(pe):
            def gate_up(i, s, first=False):
                j = 2 * i + s
                pe.wait_ge(S(f"gu{s}_loaded"), 32 * i + 32)
                pe.wait_ge(S("hb_ready"), j + 1)
                if not first:
                    pe.wait_ge(S("act_ready"), j - 1)
                for w, b in ((wg[s], s), (wu[s], 2 + s)):
                    for f in range(FT):
                        for k in range(KT):
                            mm = pe.matmul(bank[b][:, W * f:W * f + W], w[:, k, P * f:P * f + P], hb[s][:, k, :],
                                           start=k == 0, stop=k == KT - 1)
                    mm.then_inc(S("g_done" if b < 2 else "gu_done"), 1)

            def down(i, s, first=False):
                j = 2 * i + s
                pe.wait_ge(S(f"d{s}_loaded"), 16 * i + 16)
                pe.wait_ge(S("act_ready"), j + 1)
                if not first:
                    pe.wait_ge(S("y_copied"), 2 * j - 2)
                for half in range(2):
                    for dt in range(4):
                        at = P * (4 * half + dt)
                        for f in range(FT):
                            mm = pe.matmul(bank[4 + 2 * s + half][:, W * dt:W * dt + W], wd[s][:, f, at:at + P],
                                           sg[s][:, W * f:W * f + W], start=f == 0, stop=f == FT - 1)
                    mm.then_inc(S("y_done"), 1)

            gate_up(0, 0, first=True)
            gate_up(0, 1, first=True)
            down(0, 0, first=True)
            gate_up(1, 0)
            down(0, 1, first=True)
            with pe.Fori(1, PAIRS) as i:
                gate_up(i, 1)
                down(i, 0)
                gate_up(i + 1, 0)
                down(i, 1)
            down(PAIRS, 0)

        @ph.b.scalar
        def _(act):
            def fetch(i, s, first=False):
                j = 2 * i + s
                at = act.value_load(items[0:1, bass.ds(j + ITEMS, 1)], min_val=0, max_val=SLOTS - 1)
                if not first:
                    act.wait_ge(S("gu_done"), j - 1)
                nc.scalar.copy(hb[s][:], HS[:, :, bass.ds(at, W)]).then_inc(S("hb_ready"), 1)

            def silu(i, s, first=False):
                j = 2 * i + s
                act.wait_ge(S("g_done"), j + 1)
                if not first:
                    act.wait_ge(S("y_done"), 2 * j - 2)
                nc.scalar.activation(sg[s][:], bank[s][:, 0:FT * W], ACT.Silu).then_inc(S("silu_done"), 1)

            fetch(0, 0, first=True)
            fetch(0, 1, first=True)
            silu(0, 0, first=True)
            fetch(1, 0)
            silu(0, 1, first=True)
            fetch(1, 1)
            with act.Fori(1, PAIRS - 1) as i:
                for s in range(2):
                    silu(i, s)
                    fetch(i + 1, s)
            silu(PAIRS - 1, 0)
            fetch(PAIRS, 0)
            silu(PAIRS - 1, 1)
            silu(PAIRS, 0)

        @ph.b.vector
        def _(dve):
            def product(i, s):
                j = 2 * i + s
                dve.wait_ge(S("gu_done"), j + 1)
                dve.wait_ge(S("silu_done"), j + 1)
                nc.vector.tensor_tensor(sg[s][:], sg[s][:], bank[2 + s][:, 0:FT * W], ALU.mult)\
                    .then_inc(S("act_ready"), 1)

            def store(i, s, first=False):
                j = 2 * i + s
                at = dve.value_load(items[0:1, bass.ds(j + ITEMS, 1)], min_val=0, max_val=SLOTS - 1)
                if not first:
                    dve.wait_ge(S("y_copied"), 2 * j)
                for half in range(2):
                    dve.wait_ge(S("y_done"), 2 * j + half + 1)
                    nc.vector.tensor_copy(YS[:, 4 * half:4 * half + 4, bass.ds(at, W)],
                                          bank[4 + 2 * s + half][:].rearrange("p (a b) -> p a b", a=4))\
                        .then_inc(S("y_copied"), 1)

            product(0, 0)
            product(0, 1)
            store(0, 0, first=True)
            product(1, 0)
            store(0, 1)
            with dve.Fori(1, PAIRS) as i:
                product(i, 1)
                store(i, 0)
                product(i + 1, 0)
                store(i, 1)
            store(PAIRS, 0)


def combine(nc, A, E, l, M):
    xT, bank, C = (E[k] for k in ("xT", "bank", "C"))
    YS, Q = M["YS"], M["Q"]
    slots = [min(P, SLOTS - P * c) for c in range(SCH)]
    with E["Phase"]("comb") as ph:
        S = ph.sem
        yTM = ph.sb("yTM", [P, SCH, D_MODEL])

        @ph.b.tensor
        def _(pe):
            for b in range(2 * SCH):
                c, i = b // 2, b % 2
                if b >= 4:
                    pe.wait_ge(S("y_ready"), b - 3)
                for k in range(4):
                    mm = pe.transpose(bank[b % 4][0:slots[c], P * k:P * k + P],
                                      YS[:, 4 * i + k, P * c:P * c + slots[c]], C("ident"))
                mm.then_inc(S("yT_done"), 1)
            pe.wait_ge(S("y_ready"), 2 * SCH)
            for dt in range(KT):
                if dt >= 4:
                    pe.wait_ge(S("x_ready"), dt - 3)
                for c, n in enumerate(slots):
                    mm = pe.matmul(bank[4 + dt % 4][:, 0:T], yTM[0:n, c, P * dt:P * dt + P], Q[0:n, c, :],
                                   start=c == 0, stop=c == SCH - 1)
                mm.then_inc(S("sum_done"), 1)

        @ph.b.scalar
        def _(act):
            for b in range(2 * SCH):
                c, i = b // 2, b % 2
                act.wait_ge(S("yT_done"), b + 1)
                nc.scalar.copy(yTM[0:slots[c], c, 512 * i:512 * i + 512], bank[b % 4][0:slots[c], :])\
                    .then_inc(S("y_ready"), 1)

        @ph.b.vector
        def _(dve):
            for dt in range(KT):
                dve.wait_ge(S("sum_done"), dt + 1)
                nc.vector.tensor_tensor(xT[:, dt, :], xT[:, dt, :], bank[4 + dt % 4][:, 0:T], ALU.add)\
                    .then_inc(S("x_ready"), 1)


def moe(nc, A, E, l):
    with ExitStack() as shared:
        sb = lambda name, shape, dt=F32: E["alloc"](shared, f"m_{name}", shape, dt)
        M = dict(HS=sb("HS", [P, KT, SLOTS + W]), YS=sb("YS", [P, KT, SLOTS + W]), Q=sb("Q", [P, SCH, T]),
                 items=sb("items", [1, 2 * ITEMS], I32))
        route(nc, A, E, l, M)
        experts(nc, A, E, l, M)
        combine(nc, A, E, l, M)


PHASES = [project, gmlp, gdn, mla, memory, mix, moe]

OUTS = dict(
    o_x=(P, KT, T), o_ckv=(DEPTH, P, 3, RANK), o_kr=(DEPTH, P, 3, ROPE), o_gdn=(DEPTH, P, 2, HD),
    o_conv=(DEPTH, P, 6, 3), o_mem=(DEPTH, P, 2, 2, MEM), o_gdns=(DEPTH, P, 16, HD),
    o_convs=(DEPTH, P, 6, 3, NS_TOK), o_gv=(DEPTH, NS_TOK, 256))


def arrange(I):
    f = np.ascontiguousarray
    L = DEPTH
    w_in = I["w_in"].reshape(L, KT, P, -1).transpose(0, 2, 1, 3)
    off = dict(u=0, v=256, cq=512, ckv=768, kr=896, qkv=928, zg=1696, b=1952, alpha=1956, mq=1960, gate=2216)

    def cols(name, n):
        return w_in[..., off[name]:off[name] + n]

    fm = np.concatenate([cols("u", 256), cols("cq", 256), cols("qkv", 768), cols("zg", 256), cols("mq", 256)], -1)
    gate = cols("gate", 4096).reshape(L, P, KT, 4, KT, P)
    part = lambda a, n: a.reshape(L, n, P).transpose(0, 2, 1)
    twice = lambda a: np.concatenate([a, a], -1)[..., None]
    rep = lambda a: np.repeat(a.reshape(L, 2, 2), HD, 2).transpose(0, 2, 1)
    return {
        "xT": f(np.concatenate([I["x_prompt"][0], I["x_sample"][:, 0]]).reshape(T, KT, P).transpose(2, 1, 0)),
        "memT": f(I["mem_prompt"][0].reshape(MEM, KT, P).transpose(2, 1, 0)),
        "cst": constants(),
        "vec": f(np.concatenate([
            part(I["norm1_g"], 8), part(I["mla_cq_g"], 2),
            I["gdn_conv_w"].reshape(L, 4, 6, P).transpose(0, 3, 1, 2).reshape(L, P, 24),
            twice(I["gdn_out_g"]), twice(I["mem_qn_g"]), part(I["mem_norm_g"], 8), part(I["norm2_g"], 8),
            rep(I["gm_ws"][:, :, 0, 0]), rep(I["gm_b"][:, :, 0]), twice(I["mla_kn_g"])], -1)),
        "row": f(np.concatenate([
            I["gm_norm_g"], I["mla_ckv_g"], I["mla_kr_g"], I["mla_qn_g"], I["mla_qr_g"], I["mla_kn_g"],
            I["mem_kn_g"], I["gdn_a_log"], I["gdn_dt_bias"], I["moe_bg"], I["moe_be"]], -1)),
        "w_tm": f(np.concatenate([cols("v", 256), cols("ckv", 128), cols("kr", 32), cols("b", 4),
                                  cols("alpha", 4)], -1)),
        "w_fm": f(fm.reshape(L, P, KT, FM_N, P).transpose(0, 3, 1, 2, 4)),
        "w_gb": f(np.concatenate([gate.transpose(0, 4, 3, 1, 2, 5),
                                  I["w_branch"].reshape(L, 4, 2, P, KT, P).transpose(0, 4, 1, 3, 2, 5)], 4)),
        "gm_ws": f(I["gm_ws"].transpose(0, 3, 1, 2)),
        "gm_b": f(I["gm_b"].reshape(L, 2, 2, P).transpose(0, 2, 1, 3)),
        "w_uq": f(I["mla_w_uq"].reshape(L, 2, P, H * QK).transpose(0, 2, 1, 3)),
        "w_uk": f(I["mla_w_uk"].reshape(L, P, H * HD)),
        "w_ukT": f(I["mla_w_uk"].transpose(0, 3, 2, 1)),
        "w_uv": f(I["mla_w_uv"].reshape(L, P, H * HD)),
        "ckv": f(I["cache_mla_ckv"]),
        "ckvT": f(I["cache_mla_ckv"].transpose(0, 1, 3, 2)),
        "krT": f(I["cache_mla_kr"].transpose(0, 1, 3, 2)),
        "pages": f(I["page_table"].reshape(1, NPG)),
        "sgdn": f(I["state_gdn"].reshape(L, P, 16, HD)),
        "sconv": f(I["state_conv"].reshape(L, NS_TOK, 3, 6, P).transpose(0, 4, 3, 2, 1)),
        "w_kv": f(I["mem_w_kv"].reshape(L, KT, P, 512).transpose(0, 2, 1, 3)),
        "memkT": f(I["cache_mem_k"].reshape(L, NS_TOK, MEM, 2, P).transpose(0, 4, 1, 3, 2)),
        "memv": f(I["cache_mem_v"].reshape(L, NS_TOK, 2, P, 256).transpose(0, 3, 1, 2, 4)),
        "w_out": f(I["w_out"].reshape(L, KT, P, KT, P).transpose(0, 3, 2, 1, 4)),
        "w_rt": f(np.concatenate([I["moe_wg"], I["moe_we"]], -1).reshape(L, KT, P, 36).transpose(0, 2, 1, 3)),
        "w_g": f(I["moe_w_gate"].reshape(L, 32, KT, P, 256).transpose(0, 1, 3, 2, 4)),
        "w_u": f(I["moe_w_up"].reshape(L, 32, KT, P, 256).transpose(0, 1, 3, 2, 4)),
        "w_d": f(I["moe_w_down"].reshape(L, 32, 2, P, D_MODEL).transpose(0, 1, 3, 2, 4)),
    }


def restore(r):
    L = DEPTH
    x = r["o_x"].transpose(2, 1, 0).reshape(T, D_MODEL)
    prompt = lambda a: a[:, :, 0:2].transpose(0, 2, 1, 3).reshape(L, 1, NP_TOK, -1)
    mem = r["o_mem"].transpose(2, 0, 3, 1, 4).reshape(2, L, 1, MEM, H, HD)
    gdn = r["o_gdn"].reshape(L, 2, HD, 2, HD).transpose(0, 3, 1, 4, 2).reshape(L, 1, H, HD, HD)
    out = (
        x[None, :NP_TOK], x[NP_TOK:, None], prompt(r["o_ckv"]), prompt(r["o_kr"]), gdn,
        r["o_conv"].transpose(0, 3, 2, 1).reshape(L, 1, 3, 768), mem[0], mem[1],
        r["o_ckv"][:, 0:NS_TOK, 2][:, :, None], r["o_kr"][:, 0:NS_TOK, 2][:, :, None],
        r["o_gdns"].reshape(L, NS_TOK, H, HD, HD),
        r["o_convs"].transpose(0, 4, 3, 2, 1).reshape(L, NS_TOK, 3, 768), r["o_gv"][:, :, None])
    return tuple(np.ascontiguousarray(a) for a in out)


def kernel(**inputs):
    import concourse.bacc as bacc
    from concourse.bass_utils import run_bass_kernel_spmd

    nc = bacc.Bacc("TRN2", target_bir_lowering=False, num_devices=1)
    arrays = arrange({k: np.asarray(v) for k, v in inputs.items()})
    A = {n: nc.dram_tensor("in_" + n, a.shape, mybir.dt.from_np(a.dtype), kind="ExternalInput").ap()
         for n, a in arrays.items()}
    for n, shape in OUTS.items():
        A[n] = nc.dram_tensor(n, shape, F32, kind="ExternalOutput").ap()
    build(nc, A)
    return restore(run_bass_kernel_spmd(nc, [{"in_" + n: a for n, a in arrays.items()}], core_ids=[0]).results[0])
```

```python
from contextlib import ExitStack

import numpy as np

import concourse.bass as bass
from concourse import mybir

F32 = mybir.dt.float32
F32R = mybir.dt.float32r
I32 = mybir.dt.int32
U32 = mybir.dt.uint32
ALU = mybir.AluOpType
ACT = mybir.ActivationFunctionType
AX = mybir.AxisListType

P = 128
D_MODEL = 1024
KT = D_MODEL // P
DEPTH = 2
NP_TOK = 256
NS_TOK = 8
T = NP_TOK + NS_TOK
CHUNKS = ((0, P), (P, P), (NP_TOK, NS_TOK))
H = 4
HD = 64
ROPE = 32
QK = HD + ROPE
RANK = 128
PAGES = 8
SUB = 16
NPG = NS_TOK * PAGES
POOL = 80
MEM = 256
EPS = 1e-6
FIRST_SEM = 110
NEG = -1e30
NE = 32
SLOTS = 2 * T
SCH = -(-SLOTS // P)
W = 128
ITEMS = NE + (SLOTS - NE) // W
assert ITEMS % 2 == 1
MLA_SCALE = QK ** -0.5
MEM_SCALE = HD ** -0.5

TM_V, TM_CKV, TM_KR, TM_BETA, TM_ALPHA, TM_W = 0, 256, 384, 416, 420, 424
FM_U, FM_CQ, FM_QKV, FM_ZG, FM_MQ, FM_N = 0, 2, 4, 10, 12, 14
GATE_TILES = 4 * KT

CONST_COLS = dict(ident=128, tri=128, blk=128, lev=7 * 128, causal=128, rope=96, m832=256, sel832=32,
                  selrow=8, qr=64, hsel=4, selg=512, mv=4, m16=16, seln=8, rev=8, mq=512,
                  stri=128, sub=1, iota=SLOTS, valid=3, slot=SCH)
CONST_AT, _at = {}, 0
for _name, _n in CONST_COLS.items():
    CONST_AT[_name] = _at
    _at += _n
CONST_W = _at

VEC_COLS = dict(g1=8, cq_g=2, conv=24, gdn_g=1, mq_g=1, memn_g=8, g2=8, ws0=2, b0=2, kn_g=1)
VEC_AT, _at = {}, 0
for _name, _n in VEC_COLS.items():
    VEC_AT[_name] = _at
    _at += _n
VEC_W = _at

ROW_COLS = dict(gm_g=256, ckv_g=128, kr_g=32, qn_g=64, qr_g=32, kn_g=64, memk_g=64, a_log=4, dt=4,
                moe_b=36)
ROW_AT, _at = {}, 0
for _name, _n in ROW_COLS.items():
    ROW_AT[_name] = _at
    _at += _n
ROW_W = _at


def constants():
    c = np.zeros((P, CONST_W), np.float32)
    p = np.arange(P)

    def put(name, a):
        a = np.asarray(a, np.float32).reshape(-1, CONST_COLS[name])
        c[:a.shape[0], CONST_AT[name]:CONST_AT[name] + CONST_COLS[name]] = a

    put("ident", np.eye(P))
    put("tri", p[:, None] <= p[None, :])
    put("blk", p[:, None] // HD == p[None, :] // HD)
    lev = [(p[:, None] // (2 << k) == p[None, :] // (2 << k)) & (p[:, None] // (1 << k) % 2 == 0)
           & (p[None, :] // (1 << k) % 2 == 1) for k in range(7)]
    put("lev", np.stack(lev, 1))
    put("causal", np.where(p[None, :] <= p[:, None], 0.0, NEG))
    half = ROPE // 2
    inv = np.float32(10000.0) ** (-np.arange(half, dtype=np.float32) / np.float32(half))
    pos = np.stack([p, p + P, np.full(P, PAGES * P)], 1).astype(np.float32)
    ang = pos[:, :, None] * inv
    put("rope", np.stack([np.cos(ang), np.sin(ang)], 2))
    n = np.arange(NS_TOK)
    nh_n, nh_h = np.arange(32) // H, np.arange(32) % H
    put("m832", np.broadcast_to(n[:, None] == nh_n[None, :], (P, NS_TOK, 32)))
    put("sel832", n[:, None] == nh_n[None, :])
    put("selrow", nh_n[:, None] == n[None, :])
    put("qr", (4 * np.arange(2)[None, :, None] + (p // ROPE)[:, None, None]) == nh_n[None, None, :])
    put("hsel", nh_h[:, None] == np.arange(H)[None, :])
    gn, gh, gv = p // 16, p // 4 % 4, p % 4
    put("selg", (n[:, None, None] == gn) & (np.arange(H)[None, :, None] == gh))
    put("mv", gv[:, None] == np.arange(4))
    put("m16", (gh[:, None, None] == np.arange(H)[None, :, None]) & (gv[:, None, None] == np.arange(4)))
    put("seln", gn[:, None] == n)
    put("rev", np.broadcast_to(np.arange(8, 0, -1), (P, 8)))
    put("sub", p % SUB)
    put("stri", p[:, None] < p[None, :])
    put("iota", np.broadcast_to(np.arange(SLOTS), (P, SLOTS)))
    put("valid", np.stack([p >= 0, p >= 0, p < NS_TOK], 1))
    put("slot", p[:, None] + P * np.arange(SCH))
    t = np.arange(2)
    put("mq", (n[None, :, None, None] == nh_n) & (2 * t[None, None, :, None] + (p // HD)[:, None, None, None]
                                                  == nh_h))
    return c


def build(nc, A):
    with ExitStack() as top:
        def alloc(ctx, name, shape, dt=F32):
            return ctx.enter_context(nc.sbuf_tensor(name, shape, dt))

        xT = alloc(top, "xT", [P, KT, T])
        hT = alloc(top, "hT", [P, KT, T])
        zT = alloc(top, "zT", [P, FM_N, T])
        tm = alloc(top, "tm", [P, 3, TM_W])
        brT = alloc(top, "brT", [P, 8, T])
        cst = alloc(top, "cst", [P, CONST_W])
        ones = alloc(top, "ones", [P, P])
        epsc = alloc(top, "epsc", [P, 1])
        idf = alloc(top, "idf", [P, NS_TOK])
        vec = alloc(top, "vec", [P, VEC_W])
        row = alloc(top, "row", [P, ROW_W])
        bank = [top.enter_context(nc.psum_tensor(f"bank{i}", [P, 512], F32)) for i in range(8)]

        def C(name, *dims):
            a = cst[:, CONST_AT[name]:CONST_AT[name] + CONST_COLS[name]]
            if len(dims) == 2:
                return a.rearrange("p (a b) -> p a b", a=dims[0])
            if len(dims) == 3:
                return a.rearrange("p (a b c) -> p a b c", a=dims[0], b=dims[1])
            return a

        def V(name, i=0, n=1):
            return vec[:, VEC_AT[name] + i:VEC_AT[name] + i + n]

        def R(name):
            return row[:, ROW_AT[name]:ROW_AT[name] + ROW_COLS[name]]

        ck_loaded = top.enter_context(nc.semaphore("ck_loaded", num=FIRST_SEM - 2))
        kr_loaded = top.enter_context(nc.semaphore("kr_loaded", num=FIRST_SEM - 1))

        class Phase:

            def __init__(self, name):
                self.name, self.ctx, self.sems, self.count = name, ExitStack(), {}, {}

            def sb(self, name, shape, dt=F32):
                return alloc(self.ctx, f"{self.name}_{name}", shape, dt)

            def sem(self, name):
                if name not in self.sems:
                    self.sems[name] = self.ctx.enter_context(
                        nc.semaphore(f"{self.name}_{name}", num=FIRST_SEM + len(self.sems)))
                return self.sems[name]

            def __enter__(self):
                self.block = nc.Block(no_gpsimd_drain=True)
                self.b = self.block.__enter__()
                return self

            def __exit__(self, *e):
                self.block.__exit__(*e)
                if e[0] is None:
                    nc.all_engine_barrier(sems_to_clear=range(FIRST_SEM, FIRST_SEM + len(self.sems)))
                self.ctx.close()

        def stepper(ph, eng, default):
            count = {}

            def step(ins, name=default, wait=True):
                count[name] = count.get(name, 0) + 1
                ins.then_inc(ph.sem(name), 1)
                if wait:
                    eng.wait_ge(ph.sem(name), count[name])

            return step

        env = dict(locals())
        env.pop("nc"), env.pop("A")
        start(nc, A, env)
        with nc.Fori(0, DEPTH) as l:
            for phase in PHASES:
                phase(nc, A, env, l)
        finish(nc, A, env)


def start(nc, A, E):
    with E["Phase"]("start") as ph:
        pages = ph.sb("pages", [P, NS_TOK], I32)

        @ph.b.sync
        def _(sp):
            sp.dma_start(E["xT"][:], A["xT"]).then_inc(ph.sem("loaded"), 16)
            sp.dma_start(E["cst"][:], A["cst"]).then_inc(ph.sem("loaded"), 16)
            sp.dma_start(pages[:], A["pages"]).then_inc(ph.sem("loaded"), 16)
            sp.wait_ge(ph.sem("loaded"), 48)

        @ph.b.vector
        def _(dve):
            nc.vector.memset(E["tm"][:], 0.0)
            nc.vector.memset(E["ones"][:], 1.0)
            nc.vector.memset(E["epsc"][:], EPS).then_inc(ph.sem("set"), 1)
            dve.wait_ge(ph.sem("set"), 1)
            dve.wait_ge(ph.sem("loaded"), 48)
            nc.vector.tensor_scalar(E["idf"][:], pages[:], float(SUB), E["C"]("sub"), ALU.mult, ALU.add)\
                .then_inc(ph.sem("set"), 1)
            dve.wait_ge(ph.sem("set"), 2)


def finish(nc, A, E):
    with E["Phase"]("finish") as ph:
        @ph.b.sync
        def _(sp):
            sp.dma_start(A["o_x"], E["xT"][:]).then_inc(ph.sem("stored"), 16)
            sp.wait_ge(ph.sem("stored"), 16)



def high_part(nc, high, x):
    return nc.vector.tensor_copy(high, x)


def low_part(engine, low, x, high):
    return engine.tensor_tensor(low, x, high.bitcast(F32), ALU.subtract)


def multiply_split(pe, out, weights, x, start=True, stop=True):
    (wh, wl), (xh, xl) = weights, x
    pe.matmul(out, wh, xh, start=start, stop=False)
    pe.matmul(out, wh, xl, start=False, stop=False)
    return pe.matmul(out, wl, xh, start=False, stop=stop)


def project(nc, A, E, l, F):
    xT, hT, zT, tm, brT, ones, bank, C, V, R = (
        E[k] for k in ("xT", "hT", "zT", "tm", "brT", "ones", "bank", "C", "V", "R"))
    MIX_AT = 4
    with E["Phase"]("proj") as ph:
        S = ph.sem
        sq = ph.sb("sq", [P, KT, T])
        rstd = ph.sb("rstd", [P, T])
        wtm = ph.sb("wtm", [P, KT, TM_W])
        wfm = [ph.sb(f"wfm{i}", [P, KT, P]) for i in range(2)]
        wsp = [[ph.sb(f"wsp{i}{part}", [P, KT, P], F32R) for part in range(2)] for i in range(2)]
        hsp = [ph.sb(f"hsp{part}", [P, KT, T], F32R) for part in range(2)]
        uT = ph.sb("uT", [P, 2, T])
        gv = ph.sb("gv", [P, 3, 256])
        gsq = ph.sb("gsq", [P, 3, 256])
        ss = ph.sb("ss", [P, 3])
        ws = ph.sb("ws", [P, H, P])
        bias = ph.sb("bias", [P, 2, P])
        mixed = ph.sb("mixed", [P, 2, T])

        @ph.b.sync
        def _(sp):
            sp.dma_start(wtm[:], A["w_tm"][l]).then_inc(S("wtm_loaded"), 16)
            sp.dma_start(E["vec"][:], A["vec"][l]).then_inc(S("vec_loaded"), 16)
            for i in range(2):
                sp.dma_start(wfm[i][:], A["w_fm"][l, i]).then_inc(S(f"wfm{i}_loaded"), 16)
            sp.dma_start(E["row"][:], A["row"][l].partition_broadcast(P)).then_inc(S("row_loaded"), 16)
            sp.dma_start(ws[:], A["gm_ws"][l]).then_inc(S("ws_loaded"), 16)
            for g in range(2):
                sp.dma_start(bias[HD * g:HD * g + HD], A["gm_b"][l, g].partition_broadcast(HD))\
                    .then_inc(S("bias_loaded"), 16)
            with sp.Fori(1, FM_N // 2) as t:
                for i in range(2):
                    tile = A["w_fm"][l, 2 * t + i]
                    sp.wait_ge(S(f"w{i}_split"), t)
                    sp.dma_start(wfm[i][:], tile).then_inc(S(f"wfm{i}_loaded"), 16)
            for i in range(2):
                gate_load(sp, S, A, l, F, i, i)
            for i in range(2):
                sp.wait_ge(S(f"gw{i}_loaded"), 16)
            sp.wait_ge(S("v_ready"), 2)
            sp.dma_start(A["o_gv"][l], gv[0:NS_TOK, 2, :]).then_inc(S("v_stored"), 16)
            sp.wait_ge(S("v_stored"), 16)

        @ph.b.vector
        def _(dve):
            step = E["stepper"](ph, dve, "dve_step")
            tt = nc.vector.tensor_tensor
            half = KT // 2
            for i in range(2):
                ks = slice(half * i, half * i + half)
                tt(sq[:, ks], xT[:, ks], xT[:, ks], ALU.mult).then_inc(S("sq_ready"), 1)
            dve.wait_ge(S("root_ready"), 1)
            nc.vector.reciprocal(rstd[:], rstd[:]).then_inc(S("rstd_ready"), 1)
            dve.wait_ge(S("rstd_ready"), 1)
            dve.wait_ge(S("vec_loaded"), 16)
            for k in range(KT):
                nc.vector.scalar_tensor_tensor(hT[:, k, :], xT[:, k, :], V("g1", k), rstd[:], ALU.mult,
                                               ALU.mult).then_inc(S("h_ready"), 1)
            dve.wait_ge(S("h_ready"), KT)
            for i in range(2):
                ks = slice(half * i, half * i + half)
                high_part(nc, hsp[0][:, ks], hT[:, ks]).then_inc(S("h_high"), 1)
            for i in range(2):
                ks = slice(half * i, half * i + half)
                dve.wait_ge(S("h_high"), i + 1)
                low_part(nc.vector, hsp[1][:, ks], hT[:, ks], hsp[0][:, ks]).then_inc(S("h_split"), 1)

            def split(t):
                for i in range(2):
                    if not isinstance(t, int) or t > 0:
                        dve.wait_ge(S(f"fm{i}_done"), t)
                    dve.wait_ge(S(f"wfm{i}_loaded"), 16 * t + 16)
                    high_part(nc, wsp[i][0][:], wfm[i][:]).then_inc(S(f"w{i}_high"), 1)
                    dve.wait_ge(S(f"w{i}_high"), t + 1)
                    low_part(nc.vector, wsp[i][1][:], wfm[i][:], wsp[i][0][:]).then_inc(S(f"w{i}_split"), 1)

            split(0)
            dve.wait_ge(S("ws_loaded"), 16)
            tt(ws[:], ws[:], C("tri").unsqueeze(1).to_broadcast([P, H, P]), ALU.mult).then_inc(S("ws_ready"), 1)
            dve.wait_ge(S("gelu_done"), 1)
            step(tt(gsq[:], gv[:], gv[:], ALU.mult))
            step(nc.vector.tensor_reduce(ss[:], gsq[:], AX.X, ALU.add), "ss_ready", wait=False)
            split(1)
            split(2)
            dve.wait_ge(S("vroot_ready"), 1)
            step(nc.vector.reciprocal(ss[:], ss[:]))
            step(tt(gv[:], gv[:], ss[:].unsqueeze(2).to_broadcast([P, 3, 256]), ALU.mult), "v_ready")
            dve.wait_ge(S("row_loaded"), 16)
            step(tt(gv[:], gv[:], R("gm_g").unsqueeze(1).to_broadcast([P, 3, 256]), ALU.mult), "v_ready",
                 wait=False)
            with dve.Fori(3, MIX_AT + 1) as t:
                split(t)
            dve.wait_ge(S("bias_loaded"), 32)
            for c in range(2):
                dve.wait_ge(S("mix_done"), c + 1)
                step(tt(mixed[:, :, c * P:c * P + P], bank[6 + c][:, 0:256].rearrange("p (a i) -> p a i", a=2),
                        bias[:], ALU.add))
            dve.wait_ge(S("vT_done"), 1)
            for a in range(2):
                step(nc.vector.tensor_scalar(mixed[:, a, NP_TOK:T], bank[0][:, NS_TOK * a:NS_TOK * a + NS_TOK],
                                             V("ws0", a), V("b0", a), ALU.mult, ALU.add))
            dve.wait_ge(S("u_ready"), 1)
            step(tt(brT[:, 0:2, :], mixed[:], uT[:], ALU.mult))
            with dve.Fori(MIX_AT + 1, FM_N // 2) as t:
                split(t)

        @ph.b.tensor
        def _(pe):
            for k in range(KT):
                pe.wait_ge(S("sq_ready"), 1 + 2 * k // KT)
                mm = pe.matmul(bank[0][:, 0:T], ones[:], sq[:, k, :], start=k == 0, stop=k == KT - 1)
            mm.then_inc(S("ss_done"), 1)
            pe.wait_ge(S("wtm_loaded"), 16)
            for c, (t0, n) in enumerate(CHUNKS):
                for k in range(KT):
                    if c == 0:
                        pe.wait_ge(S("h_ready"), k + 1)
                    mm = pe.matmul(bank[1 + c][0:n, 0:TM_W], hT[:, k, t0:t0 + n], wtm[:, k, :],
                                   start=k == 0, stop=k == KT - 1)
                mm.then_inc(S("tm_done"), 1)

            def tile(i):
                for k in range(KT):
                    mm = multiply_split(pe, bank[4 + i][:, 0:T], [w[:, k, :] for w in wsp[i]],
                                        [h[:, k, :] for h in hsp], start=k == 0, stop=k == KT - 1)
                mm.then_inc(S(f"fm{i}_done"), 1)

            def pair(t):
                for i in range(2):
                    pe.wait_ge(S(f"w{i}_split"), t + 1)
                    pe.wait_ge(S(f"fm{i}_copied"), t)
                    tile(i)

            pe.wait_ge(S("h_split"), 2)
            for i in range(2):
                pe.wait_ge(S(f"w{i}_split"), 1)
                tile(i)
            with pe.Fori(1, MIX_AT) as t:
                pair(t)
            pe.wait_ge(S("v_ready"), 2)
            pe.wait_ge(S("ws_ready"), 1)
            for c in range(2):
                for g in range(H):
                    o = HD * (g % 2)
                    mm = pe.matmul(bank[6 + c][o:o + HD, P * (g // 2):P * (g // 2) + P],
                                   gv[:, c, HD * g:HD * g + HD], ws[:, g, :], start=True, stop=True)
                mm.then_inc(S("mix_done"), 1)
            for a in range(2):
                mm = pe.transpose(bank[0][:, NS_TOK * a:NS_TOK * a + NS_TOK], gv[0:NS_TOK, 2, P * a:P * a + P],
                                  C("ident")[0:NS_TOK, 0:NS_TOK])
            mm.then_inc(S("vT_done"), 1)
            with pe.Fori(MIX_AT, FM_N // 2) as t:
                pair(t)

        @ph.b.scalar
        def _(act):
            act.wait_ge(S("ss_done"), 1)
            nc.scalar.activation(rstd[:], bank[0][:, 0:T], ACT.Sqrt, bias=E["epsc"][:],
                                 scale=1.0 / D_MODEL).then_inc(S("root_ready"), 1)
            for c, (t0, n) in enumerate(CHUNKS):
                act.wait_ge(S("tm_done"), c + 1)
                nc.scalar.copy(tm[0:n, c, :], bank[1 + c][0:n, 0:TM_W]).then_inc(S("tm_copied"), 1)
            act.wait_ge(S("tm_copied"), 3)
            nc.scalar.activation(gv[:], tm[:, :, TM_V:TM_V + 256], ACT.Gelu).then_inc(S("gelu_done"), 1)

            def pair(t):
                for i in range(2):
                    act.wait_ge(S(f"fm{i}_done"), t + 1)
                    nc.scalar.copy(zT[:, 2 * t + i, :] if isinstance(t, int)
                                   else zT[:, bass.ds(2 * t + i, 1), :].squeeze(1), bank[4 + i][:, 0:T])\
                        .then_inc(S(f"fm{i}_copied"), 1)

            pair(0)
            for i in range(2):
                act.wait_ge(S(f"fm{i}_copied"), 1)
            nc.scalar.activation(uT[:], zT[:, FM_U:FM_U + 2, :], ACT.Gelu).then_inc(S("u_ready"), 1)
            pair(1)
            act.wait_ge(S("ss_ready"), 1)
            nc.scalar.activation(ss[:], ss[:], ACT.Sqrt, bias=E["epsc"][:], scale=1.0 / 256)\
                .then_inc(S("vroot_ready"), 1)
            with act.Fori(2, FM_N // 2) as t:
                pair(t)


MLA_TILES, GDN_TILES = 8, 16


def gate_load(sp, S, A, l, F, slot, tile, used=None):
    src = A["w_gate"][l, tile]
    if used is not None:
        sp.wait_ge(S("gate_done"), used)
    sp.dma_start(F["wf"][slot][:], src).then_inc(S(f"gw{slot}_loaded"), 16)


def gate_multiply(pe, S, E, F, slot, loads, to, copied=None):
    if not isinstance(loads, int) or loads:
        pe.wait_ge(S(f"gw{slot}_loaded"), 16 * loads)
    if copied is not None:
        pe.wait_ge(S("gate_copied"), copied)
    for k in range(KT):
        mm = pe.matmul(E["bank"][to][:, 0:T], F["wf"][slot][:, k, :], E["hT"][:, k, :], start=k == 0,
                       stop=k == KT - 1)
    mm.then_inc(S("gate_done"), 1)


def gate_copy(nc, act, S, E, F, r, of):
    act.wait_ge(S("gate_done"), r + 1)
    at = F["at"] + r
    dst = F["gT"][:, at, :] if isinstance(at, int) else F["gT"][:, bass.ds(at, 1), :].squeeze(1)
    nc.scalar.copy(dst, E["bank"][of][:, 0:T]).then_inc(S("gate_copied"), 1)


def memory(nc, A, E, l, F):
    zT, brT, bank, C, V, R, ones = (E[k] for k in ("zT", "brT", "bank", "C", "V", "R", "ones"))
    with E["Phase"]("mem") as ph:
        S = ph.sem
        memT = F["memT"]
        sq = ph.sb("sq", [P, KT, MEM])
        rstd = ph.sb("rstd", [P, MEM])
        wkv = ph.sb("wkv", [P, KT, 512])
        kv = ph.sb("kv", [P, 2, 512])
        ksq = ph.sb("ksq", [P, 2, 256])
        kss = ph.sb("kss", [P, 2, H])
        kT = ph.sb("kT", [P, 2, MEM])
        qT = ph.sb("qT", [P, 2, T])
        qsq = ph.sb("qsq", [P, 2, T])
        qblk = ph.sb("qblk", [P, 16, 32])
        sc = ph.sb("sc", [P, 2, H, MEM])
        scs = ph.sb("scs", [32, MEM])
        mx = ph.sb("mx", [P, 2, H])
        mxs = ph.sb("mxs", [32, 1])
        sm = ph.sb("sm", [P, 2, H])
        sms = ph.sb("sms", [32, 1])
        pT = sq[:].rearrange("p k m -> p (k m)").rearrange("p (s h t) -> p s h t", s=2, h=H)
        psT = ph.sb("psT", [P, 2, 32])
        pblk = ph.sb("pblk", [P, 2, NS_TOK, 32])
        outs = ph.sb("outs", [32, H, HD])
        ckT = ph.sb("ckT", [P, NS_TOK, 2, MEM])
        cv = ph.sb("cv", [P, NS_TOK, 2, 256])

        @ph.b.sync
        def _(sp):
            q0 = MLA_TILES + GDN_TILES
            sp.dma_start(wkv[:], A["w_kv"][l]).then_inc(S("wkv_loaded"), 16)
            for r in range(2, GATE_TILES - q0):
                gate_load(sp, S, A, l, F, r % 2, q0 + r, used=r - 1)
                if r == 3:
                    sp.dma_start(ckT[:], A["memkT"][l]).then_inc(S("ck_loaded"), 16)
                if r == 5:
                    sp.dma_start(cv[:], A["memv"][l]).then_inc(S("cv_loaded"), 16)
            sp.wait_ge(S("kv_ready"), 1)
            for i in range(2):
                sp.dma_start(A["o_mem"][l, :, i], kv[:, :, 256 * i:256 * i + 256]).then_inc(S("kv_stored"), 16)
            for i in range(2):
                sp.dma_start(F["wbr"][i][:], A["w_br"][l, i]).then_inc(S("wbr_loaded"), 16)
            sp.wait_ge(S("wbr_loaded"), 32)
            sp.wait_ge(S("kv_stored"), 32)

        @ph.b.tensor
        def _(pe):
            for r in range(2):
                gate_multiply(pe, S, E, F, r, 0, 6 + r)
            pe.wait_ge(S("memsq_ready"), 1)
            for k in range(KT):
                mm = pe.matmul(bank[0][:, 0:MEM], ones[:], sq[:, k, :], start=k == 0, stop=k == KT - 1)
            mm.then_inc(S("memss_done"), 1)
            pe.wait_ge(S("qsq_ready"), 1)
            for t in range(2):
                mm = pe.matmul(bank[1 + t][:, 0:T], C("blk"), qsq[:, t, :], start=True, stop=True)
            mm.then_inc(S("qss_done"), 1)
            for r in range(2, 6):
                gate_multiply(pe, S, E, F, r % 2, r // 2, 6 + r % 2, r - 1)
            pe.wait_ge(S("memh_ready"), KT)
            pe.wait_ge(S("wkv_loaded"), 16)
            for c in range(2):
                for k in range(KT):
                    mm = pe.matmul(bank[3 + c][:], memT[:, k, P * c:P * c + P], wkv[:, k, :], start=k == 0,
                                   stop=k == KT - 1)
                mm.then_inc(S("kv_done"), 1)
            pe.wait_ge(S("qblk_ready"), 16)
            pe.wait_ge(S("ck_loaded"), 16)
            for i in range(16):
                mm = pe.matmul(bank[5][0:32, 0:MEM], qblk[:, i, :], ckT[:, i // 2, i % 2, :], start=i == 0,
                               stop=i == 15)
            mm.then_inc(S("scs_done"), 1)
            pe.wait_ge(S("kv_ready"), 1)
            pe.wait_ge(S("gate_copied"), 6)
            for c in range(2):
                for t in range(2):
                    at = P * (2 * t + c)
                    mm = pe.transpose(bank[6][:, at:at + P], kv[:, c, P * t:P * t + P], C("ident"))
            mm.then_inc(S("kT_done"), 1)
            pe.wait_ge(S("kT_ready"), 1)
            pe.wait_ge(S("q_ready"), 3)
            pe.wait_ge(S("kv_copied"), 2)
            for c in range(2):
                for h in range(H):
                    o = HD * (h % 2)
                    mm = pe.matmul(bank[2 * c + h % 2][:, MEM * (h // 2):MEM * (h // 2) + MEM],
                                   qT[o:o + HD, h // 2, P * c:P * c + P], kT[o:o + HD, h // 2, :],
                                   start=True, stop=True)
                    mm.then_inc(S("sc_done"), 1)
            pe.wait_ge(S("ps_ready"), 1)
            for half in range(2):
                mm = pe.transpose(bank[7][:, 32 * half:32 * half + 32], scs[:, P * half:P * half + P],
                                  C("ident")[0:32, 0:32])
            mm.then_inc(S("psT_done"), 1)
            for r in range(6, 8):
                gate_multiply(pe, S, E, F, r % 2, 3, 4 if r == 6 else 6)
            pe.wait_ge(S("p_ready"), 1)
            pe.wait_ge(S("sc_copied"), 4)
            for c in range(2):
                for half in range(2):
                    for h in range(H):
                        mm = pe.transpose(bank[2 * c + half][:, P * h:P * h + P],
                                          sc[:, c, h, P * half:P * half + P], C("ident"))
                    mm.then_inc(S("pT_done"), 1)
            pe.wait_ge(S("pblk_ready"), 1)
            pe.wait_ge(S("cv_loaded"), 16)
            for i in range(16):
                mm = pe.matmul(bank[5][0:32, 0:256], pblk[:, i % 2, i // 2, :], cv[:, i // 2, i % 2, :],
                               start=i == 0, stop=i == 15)
            mm.then_inc(S("outs_done"), 1)
            pe.wait_ge(S("pT_copied"), 4)
            pe.wait_ge(S("gate_copied"), 8)
            for h in range(H):
                o = HD * (h % 2)
                for half in range(2):
                    mm = pe.matmul(bank[6 + h // 2][o:o + HD, 0:NP_TOK],
                                   kv[:, half, 256 + HD * h:256 + HD * h + HD], pT[:, half, h, :],
                                   start=half == 0, stop=half == 1)
            mm.then_inc(S("out_done"), 1)
            pe.wait_ge(S("outs_ready"), 1)
            pe.wait_ge(S("pT_copied"), 4)
            for t in range(2):
                mm = pe.matmul(bank[t][:, 0:NS_TOK], outs[:, 2 * t:2 * t + 2, :].rearrange("p a b -> p (a b)"),
                               C("selrow")[0:32, :], start=True, stop=True)
            mm.then_inc(S("outsT_done"), 1)

        @ph.b.scalar
        def _(act):
            def gates(*tiles):
                for r in tiles:
                    gate_copy(nc, act, S, E, F, r, 4 if r == 6 else 6 if r == 7 else 6 + r % 2)

            gates(0, 1)
            act.wait_ge(S("memss_done"), 1)
            nc.scalar.activation(rstd[:], bank[0][:, 0:MEM], ACT.Sqrt, bias=E["epsc"][:], scale=1.0 / D_MODEL)\
                .then_inc(S("root_ready"), 1)
            act.wait_ge(S("qss_done"), 1)
            for t in range(2):
                nc.scalar.activation(qsq[:, t, :], bank[1 + t][:, 0:T], ACT.Sqrt, bias=E["epsc"][:],
                                     scale=1.0 / HD).then_inc(S("qroot_ready"), 1)
            gates(2, 3, 4, 5)
            act.wait_ge(S("kss_ready"), 1)
            nc.scalar.activation(kss[:], kss[:], ACT.Sqrt, bias=E["epsc"][:], scale=1.0 / HD)\
                .then_inc(S("kroot_ready"), 1)
            act.wait_ge(S("shift_s"), 1)
            nc.scalar.activation(scs[:], scs[:], ACT.Exp, scale=MEM_SCALE).then_inc(S("exps_done"), 1)
            act.wait_ge(S("sc_copied"), 4)
            nc.scalar.activation(sc[:], sc[:], ACT.Exp, scale=MEM_SCALE).then_inc(S("exp_done"), 1)
            gates(6, 7)
            for i in range(4):
                c, half = i // 2, i % 2
                act.wait_ge(S("pT_done"), i + 1)
                nc.scalar.copy(pT[:, half, :, P * c:P * c + P], bank[i][:].rearrange("p (h t) -> p h t", h=H))\
                    .then_inc(S("pT_copied"), 1)

        @ph.b.vector
        def _(dve):
            step = E["stepper"](ph, dve, "dve_step")
            step(nc.vector.tensor_tensor(sq[:], memT[:], memT[:], ALU.mult), "memsq_ready", wait=False)
            mq = zT[:, FM_MQ:FM_MQ + 2, :]
            step(nc.vector.tensor_tensor(qsq[:], mq, mq, ALU.mult), "qsq_ready")
            dve.wait_ge(S("root_ready"), 1)
            step(nc.vector.reciprocal(rstd[:], rstd[:]))
            for k in range(KT):
                step(nc.vector.scalar_tensor_tensor(memT[:, k, :], memT[:, k, :], V("memn_g", k), rstd[:],
                                                    ALU.mult, ALU.mult), "memh_ready", wait=False)
            dve.wait_ge(S("qroot_ready"), 2)
            step(nc.vector.reciprocal(qsq[:], qsq[:]), "q_ready")
            step(nc.vector.tensor_tensor(qT[:], mq, qsq[:], ALU.mult), "q_ready")
            step(nc.vector.tensor_scalar(qT[:], qT[:], V("mq_g"), None, ALU.mult), "q_ready")
            for i in range(16):
                n, t = i // 2, i % 2
                last = nc.vector.tensor_scalar(qblk[:, i, :], C("mq", 16, 32)[:, i, :],
                                               qT[:, t, NP_TOK + n:NP_TOK + n + 1], None, ALU.mult)
                step(last, "qblk_ready", wait=False)
            for c in range(2):
                dve.wait_ge(S("kv_done"), c + 1)
                step(nc.vector.tensor_copy(kv[:, c, :], bank[3 + c][:]), "kv_copied")
            k4 = kv[:, :, 0:256].rearrange("p c (h e) -> p c h e", h=H)
            step(nc.vector.tensor_tensor(ksq[:], kv[:, :, 0:256], kv[:, :, 0:256], ALU.mult))
            step(nc.vector.tensor_reduce(kss[:], ksq[:].rearrange("p c (h e) -> p c h e", h=H), AX.X, ALU.add),
                 "kss_ready", wait=False)
            dve.wait_ge(S("kroot_ready"), 1)
            step(nc.vector.reciprocal(kss[:], kss[:]))
            for c in range(2):
                step(nc.vector.tensor_tensor(k4[:, c], k4[:, c], kss[:, c].unsqueeze(2).to_broadcast([P, H, HD]),
                                             ALU.mult))
                last = nc.vector.tensor_tensor(k4[:, c], k4[:, c],
                                               R("memk_g").unsqueeze(1).to_broadcast([P, H, HD]), ALU.mult)
                step(last, *(["kv_ready"] if c else []))
            dve.wait_ge(S("scs_done"), 1)
            step(nc.vector.tensor_reduce(mxs[:], bank[5][0:32, 0:MEM], AX.X, ALU.max))
            step(nc.vector.tensor_scalar(scs[:], bank[5][0:32, 0:MEM], mxs[:], None, ALU.subtract), "shift_s",
                 wait=False)
            dve.wait_ge(S("kT_done"), 1)
            step(nc.vector.tensor_copy(kT[:].rearrange("p t s -> p (t s)"), bank[6][:]), "kT_ready", wait=False)
            dve.wait_ge(S("exps_done"), 1)
            step(nc.vector.tensor_reduce(sms[:], scs[:], AX.X, ALU.add))
            step(nc.vector.reciprocal(sms[:], sms[:]))
            step(nc.vector.tensor_scalar(scs[:], scs[:], sms[:], None, ALU.mult), "ps_ready", wait=False)
            for i in range(4):
                c, a = i // 2, i % 2
                dve.wait_ge(S("sc_done"), 4 * c + 3 + a)
                two = bank[i][:].rearrange("p (h s) -> p h s", h=2)
                mxa = mx[:, c].rearrange("p (b a) -> p a b", a=2)[:, a]
                step(nc.vector.tensor_reduce(mxa, two, AX.X, ALU.max))
                step(nc.vector.tensor_tensor(sc[:, c].rearrange("p (b a) s -> p a b s", a=2)[:, a], two,
                                             mxa.unsqueeze(2).to_broadcast([P, 2, MEM]), ALU.subtract),
                     "sc_copied")
            dve.wait_ge(S("exp_done"), 1)
            step(nc.vector.tensor_reduce(sm[:], sc[:], AX.X, ALU.add))
            step(nc.vector.reciprocal(sm[:], sm[:]))
            flat = sc[:].rearrange("p c h s -> p (c h) s")
            step(nc.vector.tensor_tensor(flat, flat, sm[:].rearrange("p c h -> p (c h)").unsqueeze(2)
                                         .to_broadcast([P, 2 * H, MEM]), ALU.mult), "p_ready", wait=False)
            dve.wait_ge(S("psT_done"), 1)
            step(nc.vector.tensor_copy(psT[:].rearrange("p a b -> p (a b)"), bank[7][:, 0:64]))
            for half in range(2):
                last = nc.vector.tensor_tensor(pblk[:, half], C("m832", NS_TOK, 32),
                                               psT[:, half].unsqueeze(1).to_broadcast([P, NS_TOK, 32]), ALU.mult)
                step(last, *(["pblk_ready"] if half else []))
            dve.wait_ge(S("outs_done"), 1)
            step(nc.vector.tensor_tensor(outs[:], bank[5][0:32, 0:256].rearrange("p (h e) -> p h e", h=H),
                                         C("hsel")[0:32, :].unsqueeze(2).to_broadcast([32, H, HD]), ALU.mult),
                 "outs_ready", wait=False)
            dve.wait_ge(S("out_done"), 1)
            for t in range(2):
                step(nc.vector.tensor_copy(brT[:, 6 + t, 0:NP_TOK], bank[6 + t][:, 0:NP_TOK]))
            dve.wait_ge(S("outsT_done"), 1)
            for t in range(2):
                step(nc.vector.tensor_copy(brT[:, 6 + t, NP_TOK:T], bank[t][:, 0:NS_TOK]))


def mla(nc, A, E, l, F):
    with ExitStack() as both:
        sb = lambda name, shape, dt=F32: E["alloc"](both, f"mla_{name}", shape, dt)
        B = dict(
            q=sb("q", [P, 3, H * QK]),
            kc=sb("kc", [P, 3, H * QK]),
            ckvn=sb("ckvn", [P, 3, RANK]),
            latT=sb("latT", [P, H, T]),
            wuk=sb("wuk", [P, H * HD]),
            ck=sb("ck", [P, NS_TOK, PAGES * RANK]),
            kr=sb("kr", [P, NS_TOK, PAGES * ROPE]),
            krp=sb("krp", [P, 2, PAGES, 4 * ROPE]),
            ids=sb("ids", [P, NS_TOK], U32))
        mla_prompt(nc, A, E, l, B, F)
        mla_decode(nc, A, E, l, B, F)


def rotate(step, nc, x, cos, sin, tmp, name="dve_step"):
    half = ROPE // 2
    x1, x2 = x[..., 0:half], x[..., half:ROPE]
    for i, (a, b) in enumerate(((x1, cos), (x2, sin), (x1, sin), (x2, cos))):
        step(nc.vector.tensor_tensor(tmp[i], a, b, ALU.mult))
    step(nc.vector.tensor_tensor(x1, tmp[0], tmp[1], ALU.subtract))
    step(nc.vector.tensor_tensor(x2, tmp[2], tmp[3], ALU.add), name)


def mla_prompt(nc, A, E, l, B, F):
    zT, tm, bank, C, V, R, ones = (E[k] for k in ("zT", "tm", "bank", "C", "V", "R", "ones"))
    q, kc, ckvn, latT, wuk = (B[k] for k in ("q", "kc", "ckvn", "latT", "wuk"))
    with E["Phase"]("mlap") as ph:
        S = ph.sem
        cqT = ph.sb("cqT", [P, 2, T])
        cqs = ph.sb("cqs", [P, 2, T])
        wuq = ph.sb("wuq", [P, 2, H * QK])
        sq = ph.sb("sq", [P, 3, H * QK])
        rs = ph.sb("rs", [P, 3, 2 * H])
        krn = ph.sb("krn", [P, 3, ROPE])
        crs = ph.sb("crs", [P, 3, 2])
        krss = ph.sb("krss", [P, 3, H])
        tmp = ph.sb("tmp", [P, 4, 3 * H * 16])
        ckvT = ph.sb("ckvT", [P, T])
        qT = ph.sb("qT", [QK, H, NP_TOK])
        kT = ph.sb("kT", [QK, H, NP_TOK])
        sc0 = ph.sb("sc0", [P, H, P])
        sc1 = ph.sb("sc1", [P, H, NP_TOK])
        mx = ph.sb("mx", [P, 2, H])
        pT0 = ph.sb("pT0", [P, 1, 512])
        pT1 = ph.sb("pT1", [P, 2, 512])
        cos, sin = C("rope", 3, 2, 16)[:, :, 0, :], C("rope", 3, 2, 16)[:, :, 1, :]

        @ph.b.sync
        def _(sp):
            sp.dma_start(wuq[:], A["w_uq"][l]).then_inc(S("wuq_loaded"), 16)
            sp.dma_start(wuk[:], A["w_uk"][l]).then_inc(S("wuk_loaded"), 16)
            for r in range(2, MLA_TILES):
                gate_load(sp, S, A, l, F, r % 2, r, used=r - 1)
            sp.wait_ge(S("latent_ready"), 2)
            sp.dma_start(A["o_ckv"][l], ckvn[:]).then_inc(S("latent_stored"), 16)
            sp.dma_start(A["o_kr"][l], krn[:]).then_inc(S("latent_stored"), 16)
            sp.wait_ge(S("latent_stored"), 32)

        @ph.b.gpsimd
        def _(pool):
            pool.wait_ge(S("ids_ready"), 1)
            for n in range(NS_TOK):
                rows = bass.IndirectOffsetOnAxis(ap=B["ids"][:, n:n + 1], axis=0)
                pool.indirect_dma_start(B["ck"][:, n, :], None, A["ckv"], rows).then_inc(E["ck_loaded"], 16)
                pool.indirect_dma_start(B["kr"][:, n, :], None, A["kr"], rows).then_inc(E["kr_loaded"], 16)
            pool.wait_ge(E["kr_loaded"], 16 * NS_TOK * (l + 1))
            pool.sem_inc(S("kr_here"), 1)
            pool.wait_ge(S("kr_here"), 1)
            for g in range(2):
                nc.gpsimd.tensor_copy(B["krp"][:, g].rearrange("p i (j d) -> p i j d", j=4),
                                      B["kr"][:, 4 * g:4 * g + 4, :].rearrange("p j (i d) -> p i j d", i=PAGES))\
                    .then_inc(S("krp_ready"), 1)
            pool.wait_ge(S("krp_ready"), 2)
            pool.wait_ge(E["ck_loaded"], 16 * NS_TOK * (l + 1))

        @ph.b.tensor
        def _(pe):
            def gate(r, to):
                gate_multiply(pe, S, E, F, r % 2, r // 2, to)

            gate(0, 5)
            pe.wait_ge(S("cqsq_ready"), 1)
            for t in range(2):
                mm = pe.matmul(bank[0][:, 0:T], ones[:], cqs[:, t, :], start=t == 0, stop=t == 1)
            mm.then_inc(S("cqss_done"), 1)
            gate(1, 6)
            pe.wait_ge(S("latent_ready"), 1)
            for c, (t0, n) in enumerate(CHUNKS):
                mm = pe.transpose(bank[4][:, t0:t0 + n], ckvn[0:n, c, :], C("ident")[0:n, 0:n])
            mm.then_inc(S("ckvT_done"), 1)
            pe.wait_ge(S("cq_ready"), 2)
            pe.wait_ge(S("wuq_loaded"), 16)
            for c, (t0, n) in enumerate(CHUNKS):
                for t in range(2):
                    mm = pe.matmul(bank[1 + c][0:n, 0:H * QK], cqT[:, t, t0:t0 + n], wuq[:, t, :], start=t == 0,
                                   stop=t == 1)
                mm.then_inc(S("q_done"), 1)
            pe.wait_ge(S("ckvT_ready"), 1)
            pe.wait_ge(S("wuk_loaded"), 16)
            pe.wait_ge(S("gate_copied"), 2)
            for c, (t0, n) in enumerate(CHUNKS):
                mm = pe.matmul(bank[5 + c][0:n, 0:H * HD], ckvT[:, t0:t0 + n], wuk[:], start=True, stop=True)
                mm.then_inc(S("k_done"), 1)
            pe.wait_ge(S("cqroot_ready"), 1)
            gate(2, 0)
            gate(3, 4)
            pe.wait_ge(S("qn_ready"), 1)
            pe.wait_ge(S("gate_copied"), 3)
            for c in range(2):
                for h in range(H):
                    mm = pe.transpose(bank[c][0:QK, P * h:P * h + P], q[:, c, QK * h:QK * h + QK], C("ident"))
                mm.then_inc(S("qT_done"), 1)
            pe.wait_ge(S("k_ready"), 3)
            gate(4, 7)
            pe.wait_ge(S("kn_ready"), 1)
            for c in range(2):
                for h in range(H):
                    mm = pe.transpose(bank[2 + c][0:QK, P * h:P * h + P], kc[:, c, QK * h:QK * h + QK],
                                      C("ident"))
                mm.then_inc(S("kT_done"), 1)
            pe.wait_ge(S("qkT_ready"), 4)
            pe.wait_ge(S("gate_copied"), 4)
            for h in range(H):
                mm = pe.matmul(bank[4][:, P * h:P * h + P], qT[:, h, 0:P], kT[:, h, 0:P], start=True, stop=True)
            mm.then_inc(S("sc_done"), 1)
            for h in range(H):
                mm = pe.matmul(bank[5 + h // 2][:, NP_TOK * (h % 2):NP_TOK * (h % 2) + NP_TOK], qT[:, h, P:2 * P],
                               kT[:, h, :], start=True, stop=True)
                if h % 2:
                    mm.then_inc(S("sc_done"), 1)
            gate(5, 0)
            gate(6, 1)
            pe.wait_ge(S("gate_copied"), 5)
            pe.wait_ge(S("p0_ready"), 1)
            for h in range(H):
                mm = pe.transpose(bank[7][:, P * h:P * h + P], sc0[:, h, :], C("ident"))
            mm.then_inc(S("pT_done"), 1)
            pe.wait_ge(S("p1_ready"), 1)
            pe.wait_ge(S("gate_copied"), 7)
            for s in range(2):
                for h in range(H):
                    mm = pe.transpose(bank[s][:, P * h:P * h + P], sc1[:, h, P * s:P * s + P], C("ident"))
                mm.then_inc(S("pT_done"), 1)
            gate(7, 3)
            pe.wait_ge(S("pT_ready"), 1)
            pe.matmul(bank[2][:], ckvn[:, 0, :], pT0[:, 0, :], start=True, stop=True).then_inc(S("lat_done"), 1)
            pe.wait_ge(S("pT_ready"), 3)
            pe.wait_ge(S("gate_copied"), 8)
            for s in range(2):
                mm = pe.matmul(bank[3][:], ckvn[:, s, :], pT1[:, s, :], start=s == 0, stop=s == 1)
            mm.then_inc(S("lat_done"), 1)

        @ph.b.scalar
        def _(act):
            def gate(r, of):
                gate_copy(nc, act, S, E, F, r, of)

            eps = E["epsc"][:]
            act.wait_ge(S("cqss_done"), 1)
            nc.scalar.activation(cqs[:, 0, :], bank[0][:, 0:T], ACT.Sqrt, bias=eps, scale=1.0 / 256)\
                .then_inc(S("cqroot_ready"), 1)
            act.wait_ge(S("ckvss_ready"), 2)
            for i, n in enumerate((RANK, ROPE)):
                nc.scalar.activation(crs[:, :, i], crs[:, :, i], ACT.Sqrt, bias=eps, scale=1.0 / n)\
                    .then_inc(S("ckvroot_ready"), 1)
            gate(0, 5)
            gate(1, 6)
            act.wait_ge(S("ckvT_done"), 1)
            nc.scalar.copy(ckvT[:], bank[4][:, 0:T]).then_inc(S("ckvT_ready"), 1)
            act.wait_ge(S("zeroed"), 2)
            for c, (t0, n) in enumerate(CHUNKS):
                act.wait_ge(S("q_done"), c + 1)
                nc.scalar.copy(q[0:n, c, :], bank[1 + c][0:n, 0:H * QK]).then_inc(S("q_ready"), 1)
            act.wait_ge(S("qss_ready"), 2)
            for i, n in enumerate((HD, ROPE)):
                nc.scalar.activation(rs[:, :, H * i:H * i + H], rs[:, :, H * i:H * i + H], ACT.Sqrt, bias=eps,
                                     scale=1.0 / n).then_inc(S("qroot_ready"), 1)
            for c, (t0, n) in enumerate(CHUNKS):
                act.wait_ge(S("k_done"), c + 1)
                nc.scalar.copy(kc[0:n, c, :].rearrange("p (h e) -> p h e", h=H)[:, :, 0:HD],
                               bank[5 + c][0:n, 0:H * HD].rearrange("p (h e) -> p h e", h=H))\
                    .then_inc(S("k_ready"), 1)
            act.wait_ge(S("kss_ready"), 1)
            nc.scalar.activation(krss[:], krss[:], ACT.Sqrt, bias=eps, scale=1.0 / HD).then_inc(S("kroot_ready"), 1)
            gate(2, 0)
            gate(3, 4)
            for c in range(2):
                act.wait_ge(S("qT_done"), c + 1)
                nc.scalar.copy(qT[:, :, P * c:P * c + P], bank[c][0:QK, :].rearrange("p (h t) -> p h t", h=H))\
                    .then_inc(S("qkT_ready"), 1)
            gate(4, 7)
            for c in range(2):
                act.wait_ge(S("kT_done"), c + 1)
                nc.scalar.copy(kT[:, :, P * c:P * c + P], bank[2 + c][0:QK, :].rearrange("p (h t) -> p h t", h=H))\
                    .then_inc(S("qkT_ready"), 1)
            act.wait_ge(S("shift0"), 1)
            nc.scalar.activation(sc0[:], sc0[:], ACT.Exp).then_inc(S("exp0_done"), 1)
            gate(5, 0)
            act.wait_ge(S("shift1"), 1)
            nc.scalar.activation(sc1[:], sc1[:], ACT.Exp).then_inc(S("exp1_done"), 1)
            gate(6, 1)
            act.wait_ge(S("pT_done"), 1)
            nc.scalar.copy(pT0[:, 0, :], bank[7][:]).then_inc(S("pT_ready"), 1)
            for s in range(2):
                act.wait_ge(S("pT_done"), s + 2)
                nc.scalar.copy(pT1[:, s, :], bank[s][:]).then_inc(S("pT_ready"), 1)
            gate(7, 3)
            for c in range(2):
                act.wait_ge(S("lat_done"), c + 1)
                nc.scalar.copy(latT[:, :, P * c:P * c + P], bank[2 + c][:].rearrange("p (h t) -> p h t", h=H))

        @ph.b.vector
        def _(dve):
            step = E["stepper"](ph, dve, "dve_step")
            tt, red = nc.vector.tensor_tensor, nc.vector.tensor_reduce
            idf = E["idf"]
            step(nc.vector.tensor_copy(B["ids"][:], idf[:]), "ids_ready")
            step(nc.vector.tensor_scalar(idf[:], idf[:], float(POOL * SUB), None, ALU.add), wait=False)
            step(nc.vector.memset(q[:], 0.0), "zeroed", wait=False)
            step(nc.vector.memset(kc[:], 0.0), "zeroed")
            cq = zT[:, FM_CQ:FM_CQ + 2, :]
            step(tt(cqs[:], cq, cq, ALU.mult), "cqsq_ready", wait=False)
            raw, rawr = tm[:, :, TM_CKV:TM_CKV + RANK], tm[:, :, TM_KR:TM_KR + ROPE]
            step(tt(sq[:, :, 0:RANK], raw, raw, ALU.mult), wait=False)
            step(tt(sq[:, :, RANK:RANK + ROPE], rawr, rawr, ALU.mult))
            step(red(crs[:, :, 0], sq[:, :, 0:RANK], AX.X, ALU.add), "ckvss_ready", wait=False)
            step(red(crs[:, :, 1], sq[:, :, RANK:RANK + ROPE], AX.X, ALU.add), "ckvss_ready", wait=False)
            dve.wait_ge(S("cqroot_ready"), 1)
            step(nc.vector.reciprocal(cqs[:, 1, :], cqs[:, 0, :]))
            for t in range(2):
                step(nc.vector.scalar_tensor_tensor(cqT[:, t, :], zT[:, FM_CQ + t, :], V("cq_g", t), cqs[:, 1, :],
                                                    ALU.mult, ALU.mult), "cq_ready", wait=False)
            dve.wait_ge(S("ckvroot_ready"), 2)
            step(nc.vector.reciprocal(crs[:], crs[:]))
            step(tt(ckvn[:], raw, crs[:, :, 0].unsqueeze(2).to_broadcast([P, 3, RANK]), ALU.mult), wait=False)
            step(tt(krn[:], rawr, crs[:, :, 1].unsqueeze(2).to_broadcast([P, 3, ROPE]), ALU.mult))
            step(tt(ckvn[:], ckvn[:], R("ckv_g").unsqueeze(1).to_broadcast([P, 3, RANK]), ALU.mult),
                 "latent_ready", wait=False)
            step(tt(krn[:], krn[:], R("kr_g").unsqueeze(1).to_broadcast([P, 3, ROPE]), ALU.mult))
            rotate(step, nc, krn[:], cos, sin,
                   [tmp[:, i, 0:48].rearrange("p (c e) -> p c e", c=3) for i in range(4)])
            kc4 = kc[:].rearrange("p c (h e) -> p c h e", h=H)
            step(tt(kc4[:, :, :, HD:QK], krn[:].unsqueeze(2).to_broadcast([P, 3, H, ROPE]),
                    krn[:].unsqueeze(2).to_broadcast([P, 3, H, ROPE]), ALU.max), "latent_ready", wait=False)
            dve.wait_ge(S("q_ready"), 3)
            q4, sq4 = (a.rearrange("p c (h e) -> p c h e", h=H) for a in (q[:], sq[:]))
            step(tt(sq[:], q[:], q[:], ALU.mult))
            step(red(rs[:, :, 0:H], sq4[:, :, :, 0:HD], AX.X, ALU.add), "qss_ready", wait=False)
            step(red(rs[:, :, H:2 * H], sq4[:, :, :, HD:QK], AX.X, ALU.add), "qss_ready", wait=False)
            dve.wait_ge(S("qroot_ready"), 2)
            step(nc.vector.reciprocal(rs[:], rs[:]))
            q12 = q[:].rearrange("p c (h e) -> p (c h) e", h=H)
            for part, o, n, g in ((0, 0, HD, "qn_g"), (1, HD, ROPE, "qr_g")):
                dims = [P, 3, H, n]
                step(tt(q4[:, :, :, o:o + n], q4[:, :, :, o:o + n],
                        rs[:, :, H * part:H * part + H].unsqueeze(3).to_broadcast(dims), ALU.mult))
                step(tt(q12[:, :, o:o + n], q12[:, :, o:o + n], R(g).unsqueeze(1).to_broadcast([P, 3 * H, n]),
                        ALU.mult))
            wide = [P, 3, H, 16]
            rotate(step, nc, q4[:, :, :, HD:QK], cos.unsqueeze(2).to_broadcast(wide),
                   sin.unsqueeze(2).to_broadcast(wide),
                   [tmp[:, i].rearrange("p (c h e) -> p c h e", c=3, h=H) for i in range(4)], "qn_ready")
            dve.wait_ge(S("k_ready"), 3)
            kn = kc[:].rearrange("p c (h e) -> p (c h) e", h=H)[:, :, 0:HD]
            step(tt(sq[:, :, 0:256].rearrange("p c (h e) -> p c h e", h=H), kc4[:, :, :, 0:HD],
                    kc4[:, :, :, 0:HD], ALU.mult))
            step(red(krss[:], sq[:, :, 0:256].rearrange("p c (h e) -> p c h e", h=H), AX.X, ALU.add), "kss_ready",
                 wait=False)
            dve.wait_ge(S("kroot_ready"), 1)
            step(nc.vector.reciprocal(krss[:], krss[:]))
            step(tt(kn, kn, krss[:].rearrange("p c h -> p (c h)").unsqueeze(2).to_broadcast([P, 3 * H, HD]),
                    ALU.mult))
            step(tt(kn, kn, R("kn_g").unsqueeze(1).to_broadcast([P, 3 * H, HD]), ALU.mult), "kn_ready")
            dve.wait_ge(S("sc_done"), 1)
            mask = C("causal")

            def rows(sc, m, n):
                step(red(m, sc, AX.X, ALU.max))
                return tt(sc, sc, m.unsqueeze(2).to_broadcast([P, H, n]), ALU.subtract)

            for h in range(H):
                step(nc.vector.scalar_tensor_tensor(sc0[:, h, :], bank[4][:, P * h:P * h + P], MLA_SCALE, mask,
                                                    ALU.mult, ALU.add))
            step(rows(sc0[:], mx[:, 0], P), "shift0", wait=False)
            for h in range(H):
                dve.wait_ge(S("sc_done"), 2 + h // 2)
                src = bank[5 + h // 2][:, NP_TOK * (h % 2):NP_TOK * (h % 2) + NP_TOK]
                step(nc.vector.tensor_scalar(sc1[:, h, 0:P], src[:, 0:P], MLA_SCALE, None, ALU.mult))
                step(nc.vector.scalar_tensor_tensor(sc1[:, h, P:2 * P], src[:, P:2 * P], MLA_SCALE, mask, ALU.mult,
                                                    ALU.add))
            step(rows(sc1[:], mx[:, 1], NP_TOK), "shift1", wait=False)
            for i, (sc, n) in enumerate(((sc0, P), (sc1, NP_TOK))):
                dve.wait_ge(S(f"exp{i}_done"), 1)
                step(red(mx[:, i], sc[:], AX.X, ALU.add))
                step(nc.vector.reciprocal(mx[:, i], mx[:, i]))
                step(tt(sc[:], sc[:], mx[:, i].unsqueeze(2).to_broadcast([P, H, n]), ALU.mult), f"p{i}_ready",
                     wait=False)


def mla_decode(nc, A, E, l, B, F):
    brT, bank, C, V, ones = (E[k] for k in ("brT", "bank", "C", "V", "ones"))
    q, kc, ckvn, latT, wuk, ck, krp = (B[k] for k in ("q", "kc", "ckvn", "latT", "wuk", "ck", "krp"))
    N = NS_TOK
    RAW = 4
    with E["Phase"]("mlad") as ph:
        S = ph.sem
        ckT = ph.sb("ckT", [P, NPG, P])
        krT = ph.sb("krT", [P, 2, PAGES, P])
        wukT = ph.sb("wukT", [HD, H, RANK])
        wuv = ph.sb("wuv", [P, H * HD])
        qsT = ph.sb("qsT", [QK, H, N])
        qa = ph.sb("qa", [P, N, H])
        qblk = ph.sb("qblk", [P, N, 32])
        qrep = ph.sb("qrep", [N, H, 4, ROPE])
        qr = ph.sb("qr", [P, N, H])
        qrblk = ph.sb("qrblk", [P, 2, 32])
        prod = ph.sb("prod", [N, H * QK])
        so = ph.sb("so", [N, H])
        sox = ph.sb("sox", [N, N, H])
        sqr = B["kr"][:].rearrange("p n c -> p (n c)").rearrange("p (r c) -> p r c", r=RAW)
        ssq = ph.sb("ssq", [P, PAGES, 32])
        rT = ph.sb("rT", [32, PAGES * P])
        sc = ph.sb("sc", [32, PAGES * P + 1])
        mx = ph.sb("mx", [32, 3])
        pT = ph.sb("pT", [P, PAGES, 32])
        pblk = B["kr"][:].rearrange("p n c -> p (n c)").rearrange("p (a n b) -> p a n b", a=PAGES, n=N)
        own = ph.sb("own", [32, RANK])
        lat = ph.sb("lat", [32, RANK])

        @ph.b.sync
        def _(sp):
            sp.dma_start(wukT[:], A["w_ukT"][l]).then_inc(S("wukT_loaded"), 16)
            sp.dma_start(wuv[:], A["w_uv"][l]).then_inc(S("wuv_loaded"), 16)
            for i in range(2):
                gate_load(sp, S, A, l, F, i, MLA_TILES + i)
            for i in range(2):
                sp.wait_ge(S(f"gw{i}_loaded"), 16)

        @ph.b.tensor
        def _(pe):
            ident = C("ident")
            for h in range(H):
                mm = pe.transpose(bank[0][0:QK, N * h:N * h + N], q[0:N, 2, QK * h:QK * h + QK], ident[0:N, 0:N])
            mm.then_inc(S("qsT_done"), 1)
            pe.wait_ge(S("qrep_ready"), 1)
            for h in range(H):
                mm = pe.matmul(bank[2][:, N * h:N * h + N], qrep[:, h].rearrange("p a b -> p (a b)"),
                               ident[0:N, 0:N], start=True, stop=True)
            mm.then_inc(S("qr_done"), 1)
            pe.wait_ge(S("sox_ready"), 1)
            pe.matmul(bank[3][0:32, 0:1], sox[:].rearrange("p a b -> p (a b)"), ones[0:N, 0:1], start=True,
                      stop=True).then_inc(S("own_done"), 1)
            pe.wait_ge(S("qsT_ready"), 1)
            pe.wait_ge(S("wukT_loaded"), 16)
            for h in range(H):
                mm = pe.matmul(bank[1][:, N * h:N * h + N], wukT[:, h, :], qsT[0:HD, h, :], start=True, stop=True)
            mm.then_inc(S("qa_done"), 1)
            for b in range(NPG // 4 + 4):
                if b >= 4:
                    pe.wait_ge(S("ckT_odd" if b % 2 else "ckT_even"), b // 2 - 1)
                for j in range(4):
                    if b < NPG // 4:
                        n, i = b // 2, 4 * (b % 2) + j
                        src = ck[:, n, RANK * i:RANK * i + RANK]
                    else:
                        g, i = (b - NPG // 4) // 2, 4 * (b % 2) + j
                        src = krp[:, g, i, :]
                    mm = pe.transpose(bank[4 + b % 4][:, P * j:P * j + P], src, ident)
                mm.then_inc(S("ckT_done"), 1)
            for b in range(NPG // 2):
                if b == 0:
                    pe.wait_ge(S("ckT_even"), NPG // 8 + 2)
                    pe.wait_ge(S("ckT_odd"), NPG // 8 + 2)
                if b >= RAW:
                    pe.wait_ge(S("squared"), b - RAW + 1)
                for j in range(2):
                    mm = pe.matmul(bank[4 + b % RAW][:, 256 * j:256 * j + 256], ckT[:, 2 * b + j, :], wuk[:],
                                   start=True, stop=True)
                mm.then_inc(S("raw_done"), 1)
            pe.wait_ge(S("qblk_ready"), 3)
            for half in range(2):
                for n in range(N):
                    at = PAGES * n + 4 * half
                    mm = pe.matmul(bank[half][0:32, :], qblk[:, n, :],
                                   ckT[:, at:at + 4, :].rearrange("p a b -> p (a b)"), start=n == 0, stop=n == N - 1)
                mm.then_inc(S("nope_done"), 1)
                for g in range(2):
                    mm = pe.matmul(bank[2 + half][0:32, :], qrblk[:, g, :],
                                   krT[:, g, 4 * half:4 * half + 4, :].rearrange("p a b -> p (a b)"),
                                   start=g == 0, stop=g == 1)
                mm.then_inc(S("rope_done"), 1)
                if half == 0:
                    pe.wait_ge(S("rinv_ready"), 1)
                    for p in range(PAGES):
                        mm = pe.transpose(bank[4 + p // 4][0:32, P * (p % 4):P * (p % 4) + P], ssq[:, p, :], ident)
                    mm.then_inc(S("rT_done"), 1)
                    pe.matmul(bank[6][0:32, 0:RANK], C("sel832")[0:N, :], ckvn[0:N, 2, :], start=True, stop=True)\
                        .then_inc(S("rep_done"), 1)
            pe.wait_ge(S("exp_done"), 1)
            for p in range(PAGES):
                mm = pe.transpose(bank[7][:, 32 * p:32 * p + 32], sc[:, P * p:P * p + P], ident[0:32, 0:32])
            mm.then_inc(S("pT_done"), 1)
            for p in range(PAGES):
                pe.wait_ge(S("pblk_ready"), p + 1)
                for n in range(N):
                    i = N * p + n
                    mm = pe.matmul(bank[5][0:32, 0:RANK], pblk[:, p, n, :], ck[:, n, RANK * p:RANK * p + RANK], start=i == 0,
                                   stop=i == NPG - 1)
            mm.then_inc(S("lat_done"), 1)
            pe.wait_ge(S("lat_ready"), 1)
            pe.transpose(bank[4][:, 0:32], lat[:], ident[0:32, 0:32]).then_inc(S("latT_done"), 1)
            pe.wait_ge(S("latT_ready"), 1)
            pe.wait_ge(S("wuv_loaded"), 16)
            for h in range(H):
                o = HD * (h % 2)
                mm = pe.matmul(bank[h // 2][o:o + HD, 0:T], wuv[:, HD * h:HD * h + HD], latT[:, h, :], start=True,
                               stop=True)
            mm.then_inc(S("out_done"), 1)

        @ph.b.scalar
        def _(act):
            for b in range(0, NPG // 4 + 4, 2):
                act.wait_ge(S("ckT_done"), b + 1)
                dst = ckT[:, 4 * b:4 * b + 4, :] if b < NPG // 4 else krT[:, (b - NPG // 4) // 2, 0:4, :]
                nc.scalar.copy(dst.rearrange("p a b -> p (a b)"), bank[4 + b % 4][:]).then_inc(S("ckT_even"), 1)
            for b in range(NPG // 2):
                act.wait_ge(S("raw_done"), b + 1)
                if b >= RAW:
                    act.wait_ge(S("summed"), b - RAW + 1)
                nc.scalar.activation(sqr[:, b % RAW, :], bank[4 + b % RAW][:], ACT.Square)\
                    .then_inc(S("squared"), 1)
            act.wait_ge(S("summed"), NPG // 2)
            nc.scalar.activation(ssq[:], ssq[:], ACT.Sqrt, bias=E["epsc"][:], scale=1.0 / HD)\
                .then_inc(S("root_ready"), 1)
            act.wait_ge(S("shift"), 1)
            nc.scalar.activation(sc[:], sc[:], ACT.Exp, bias=mx[:, 2:3], scale=MLA_SCALE).then_inc(S("exp_done"), 1)
            act.wait_ge(S("out_done"), 1)
            for t in range(2):
                nc.scalar.copy(brT[:, 2 + t, :], bank[t][:, 0:T])

        @ph.b.vector
        def _(dve):
            step = E["stepper"](ph, dve, "dve_step")
            tt, red = nc.vector.tensor_tensor, nc.vector.tensor_reduce
            q3 = q[0:N, 2, :].rearrange("p (h e) -> p h e", h=H)
            step(nc.vector.tensor_copy(qrep[:], q3[:, :, HD:QK].unsqueeze(2).to_broadcast([N, H, 4, ROPE])),
                 "qrep_ready", wait=False)
            step(tt(prod[:], q[0:N, 2, :], kc[0:N, 2, :], ALU.mult))
            step(red(so[:], prod[:].rearrange("p (h e) -> p h e", h=H), AX.X, ALU.add))
            step(tt(sox[:], C("sel832")[0:N].rearrange("p (n h) -> p n h", n=N),
                    so[:].unsqueeze(1).to_broadcast([N, N, H]), ALU.mult), "sox_ready", wait=False)
            dve.wait_ge(S("qsT_done"), 1)
            step(nc.vector.tensor_scalar(qsT[0:HD].rearrange("p h n -> p (h n)"), bank[0][0:HD, 0:H * N],
                                         V("kn_g")[0:HD], None, ALU.mult), "qsT_ready", wait=False)
            dve.wait_ge(S("qr_done"), 1)
            step(nc.vector.tensor_copy(qr[:], bank[2][:, 0:H * N].rearrange("p (h n) -> p n h", h=H)))
            step(tt(qrblk[:], C("qr", 2, 32), qr[:].rearrange("p n h -> p (n h)").unsqueeze(1)
                    .to_broadcast([P, 2, 32]), ALU.mult), "qblk_ready", wait=False)
            dve.wait_ge(S("qa_done"), 1)
            step(nc.vector.tensor_copy(qa[:], bank[1][:, 0:H * N].rearrange("p (h n) -> p n h", h=H)))
            step(tt(qblk[:], C("m832", N, 32), qa[:].rearrange("p n h -> p (n h)").unsqueeze(1)
                    .to_broadcast([P, N, 32]), ALU.mult), "qblk_ready", wait=False)
            dve.wait_ge(S("own_done"), 1)
            step(nc.vector.tensor_copy(sc[:, PAGES * P:], bank[3][0:32, 0:1]), "qblk_ready")
            for b in range(1, NPG // 4 + 4, 2):
                dve.wait_ge(S("ckT_done"), b + 1)
                dst = ckT[:, 4 * b:4 * b + 4, :] if b < NPG // 4 else krT[:, (b - NPG // 4) // 2, 4:8, :]
                step(nc.vector.tensor_copy(dst.rearrange("p a b -> p (a b)"), bank[4 + b % 4][:]), "ckT_odd",
                     wait=False)
            for b in range(NPG // 2):
                n, p = b // 4, 2 * (b % 4)
                dve.wait_ge(S("squared"), b + 1)
                step(red(ssq[:, p:p + 2, H * n:H * n + H],
                         sqr[:, b % RAW, :].rearrange("p (j h e) -> p j h e", j=2, h=H), AX.X, ALU.add), "summed",
                     wait=False)
            dve.wait_ge(S("root_ready"), 1)
            step(nc.vector.reciprocal(ssq[:], ssq[:]), "rinv_ready", wait=False)
            dve.wait_ge(S("rT_done"), 1)
            for half in range(2):
                step(nc.vector.tensor_copy(rT[:, 512 * half:512 * half + 512], bank[4 + half][0:32, :]))
            for half in range(2):
                at = slice(512 * half, 512 * half + 512)
                dve.wait_ge(S("nope_done"), half + 1)
                step(tt(sc[:, at], rT[:, at], bank[half][0:32, :], ALU.mult))
                dve.wait_ge(S("rope_done"), half + 1)
                step(tt(sc[:, at], sc[:, at], bank[2 + half][0:32, :], ALU.add))
                step(red(mx[:, half:half + 1], sc[:, 512 * half:512 * half + 512 + half], AX.X, ALU.max))
            step(tt(mx[:, 2:3], mx[:, 0:1], mx[:, 1:2], ALU.max))
            step(nc.vector.tensor_scalar(mx[:, 2:3], mx[:, 2:3], -MLA_SCALE, None, ALU.mult), "shift", wait=False)
            dve.wait_ge(S("rep_done"), 1)
            step(nc.vector.tensor_copy(own[:], bank[6][0:32, 0:RANK]))
            dve.wait_ge(S("pT_done"), 1)
            step(nc.vector.tensor_copy(pT[:].rearrange("p a b -> p (a b)"), bank[7][:, 0:PAGES * 32]))
            for p in range(PAGES):
                step(tt(pblk[:, p], C("m832", N, 32), pT[:, p].unsqueeze(1).to_broadcast([P, N, 32]), ALU.mult),
                     "pblk_ready", wait=False)
            dve.wait_ge(S("exp_done"), 1)
            step(red(mx[:, 0:1], sc[:], AX.X, ALU.add))
            step(nc.vector.reciprocal(mx[:, 0:1], mx[:, 0:1]))
            dve.wait_ge(S("lat_done"), 1)
            step(nc.vector.scalar_tensor_tensor(lat[:], own[:], sc[:, PAGES * P:], bank[5][0:32, 0:RANK], ALU.mult,
                                                ALU.add))
            step(nc.vector.tensor_scalar(lat[:], lat[:], mx[:, 0:1], None, ALU.mult), "lat_ready", wait=False)
            dve.wait_ge(S("latT_done"), 1)
            step(nc.vector.tensor_copy(latT[:, :, NP_TOK:T], bank[4][:, 0:32].rearrange("p (n h) -> p h n", h=H)),
                 "latT_ready", wait=False)


def gdn(nc, A, E, l, F):
    zT, tm, brT, bank, C, V, R, ones = (E[k] for k in ("zT", "tm", "brT", "bank", "C", "V", "R", "ones"))
    N = NS_TOK
    GS = 3 * HD + 2
    with E["Phase"]("gdn") as ph:
        S = ph.sem
        y = ph.sb("y", [P, 6, T])
        sq = ph.sb("sq", [P, 4, T])
        buf = ph.sb("buf", [P, 6, 3, N])
        gb = ph.sb("gb", [P, 2, 3, H])
        e1 = ph.sb("e1", [P, 2, 3, H])
        sp1 = ph.sb("sp1", [P, 3, 3, H])
        alog = ph.sb("alog", [P, H])
        G = ph.sb("G", [P, 2, H])
        wG = ph.sb("wG", [P, 3, 2, H])
        rep = ph.sb("rep", [P, 2, 2, H, P])
        D = ph.sb("D", [P, 2, H, P])
        EG = ph.sb("EG", [P, 2, H, P])
        bB = ph.sb("bB", [P, 2, H, P])
        AT = ph.sb("AT", [P, 2, H, P])
        PT = ph.sb("PT", [P, 2, H, P])
        MT = ph.sb("MT", [P, 2, H, P])
        P1 = ph.sb("P1", [P, 2, H, P])
        X = ph.sb("X", [P, 2, H, P])
        XT = ph.sb("XT", [P, 2, H, P])
        qg = ph.sb("qg", [P, 2, NP_TOK])
        kv = ph.sb("kv", [P, 2, 512])
        ST = ph.sb("ST", [P, 2, HD])
        Rr = ph.sb("Rr", [P, 2, H, HD])
        u = ph.sb("u", [P, 2, H, HD])
        oT = ph.sb("oT", [P, 2, T])
        osq = ph.sb("osq", [P, 2, T])
        zg = ph.sb("zg", [P, 2, T])
        gs = ph.sb("gs", [N, H, GS])
        rs = ph.sb("rs", [P, GS])
        st = ph.sb("st", [P, 16, HD])
        pr = ph.sb("pr", [P, 16, HD])
        v16 = ph.sb("v16", [P, 4, 16])
        sc1 = ph.sb("sc1", [P, 2])
        oX = ph.sb("oX", [P, 16, 16])
        raw = zT[:, FM_QKV:FM_QKV + 6, :]
        ident = C("ident")

        def by_parity(a, par):
            return a.rearrange("p (a b) t -> p b a t", b=2)[:, par]

        @ph.b.sync
        def _(sp):
            sp.dma_start(buf[:], A["sconv"][l]).then_inc(S("buf_loaded"), 16)
            sp.dma_start(A["o_conv"][l], raw[:, :, NP_TOK - 3:NP_TOK]).then_inc(S("stored"), 16)
            sp.dma_start(A["o_convs"][l, :, :, 2, :], raw[:, :, NP_TOK:T]).then_inc(S("stored"), 16)
            sp.dma_start(st[:], A["sgdn"][l]).then_inc(S("state_loaded"), 16)
            sp.wait_ge(S("buf_loaded"), 16)
            for i in range(2):
                sp.dma_start(A["o_convs"][l, :, :, i, :], buf[:, :, i + 1, :]).then_inc(S("stored"), 16)
            for r in range(2, 9):
                gate_load(sp, S, A, l, F, r % 2, MLA_TILES + r, used=r - 1)
            with sp.Fori(1, 7) as k:
                gate_load(sp, S, A, l, F, 1, MLA_TILES + 8 + k, used=k + 8)
            gate_load(sp, S, A, l, F, 0, MLA_TILES + 15, used=9)
            sp.dma_start(F["memT"][:], A["memT"]).then_inc(S("mem_loaded"), 16)
            gate_load(sp, S, A, l, F, 1, MLA_TILES + GDN_TILES + 1, used=15)
            gate_load(sp, S, A, l, F, 0, MLA_TILES + GDN_TILES, used=16)
            sp.wait_ge(S("state_s_ready"), 1)
            sp.dma_start(A["o_gdns"][l], st[:]).then_inc(S("stored"), 16)
            sp.wait_ge(S("state_ready"), 8)
            sp.dma_start(A["o_gdn"][l], ST[:]).then_inc(S("stored"), 16)
            sp.wait_ge(S("mem_loaded"), 16)
            sp.wait_ge(S("gw0_loaded"), 16 * 6)
            sp.wait_ge(S("gw1_loaded"), 16 * 10)
            sp.wait_ge(S("stored"), 96)

        @ph.b.tensor
        def _(pe):
            def gates(*tiles):
                for r in tiles:
                    gate_multiply(pe, S, E, F, r % 2, r // 2, 6 + r % 2, r - 1 if r >= 2 else None)

            gates(0, 1, 2, 3)
            pe.wait_ge(S("sq_ready"), 1)
            for t in range(4):
                mm = pe.matmul(bank[t][:, 0:T], C("blk"), sq[:, t, :], start=True, stop=True)
            mm.then_inc(S("ss_done"), 1)
            gates(4, 5, 6, 7)
            pe.wait_ge(S("gb_ready"), 3)
            for j in range(2):
                mm = pe.matmul(bank[4 + j][:, 0:H], C("tri"), gb[:, 1, j, :], start=True, stop=True)
            mm.then_inc(S("G_done"), 1)
            pe.wait_ge(S("rep_ready"), 4)
            pe.wait_ge(S("G_ready"), 2)
            pe.wait_ge(S("roots_taken"), 4)
            pe.wait_ge(S("qk_ready"), 2)
            for j in range(2):
                if j:
                    pe.wait_ge(S("gate_copied"), 8)
                for h in range(H):
                    pe.matmul(bank[4 * j][:, P * h:P * h + P], rep[:, 1, j, h, :], C("tri"), start=True, stop=True)
                for h in range(H):
                    mm = pe.matmul(bank[4 * j + 1][:, P * h:P * h + P], rep[:, 0, j, h, :], ident, start=True,
                                   stop=True)
                mm.then_inc(S("rows_done"), 1)
                for h in range(H):
                    o, a, c = HD * (h % 2), h // 2, slice(P * j, P * j + P)
                    for i in range(2):
                        mm = pe.matmul(bank[4 * j + 2 + h % 2][:, P * (2 * i + a):P * (2 * i + a) + P],
                                       y[o:o + HD, 2 + a, c], y[o:o + HD, 2 * (1 - i) + a, c], start=True, stop=True)
                    mm.then_inc(S("kq_done"), 1)
            pe.wait_ge(S("kq_read"), 4)
            gate_multiply(pe, S, E, F, 0, 4, 3)
            for j in range(2):
                pe.wait_ge(S(f"mt{j}_ready"), 1)
                pe.wait_ge(S("kq_read"), 8)
                for h in range(H):
                    mm = pe.matmul(bank[4 * j][:, P * h:P * h + P], MT[:, j, h, :], ident, start=True, stop=True)
                mm.then_inc(S(f"p1{j}_done"), 1)
            with pe.Fori(1, 7) as k:
                for j in range(2):
                    pe.wait_ge(S(f"mt{j}_ready"), k + 1)
                    pe.wait_ge(S(f"x{j}_ready"), 2 * k)
                    for h in range(H):
                        mm = pe.matmul(bank[4 * j][:, P * h:P * h + P], MT[:, j, h, :], X[:, j, h, :], start=True,
                                       stop=True)
                    mm.then_inc(S(f"p1{j}_done"), 1)
                for j in range(2):
                    pe.wait_ge(S(f"p1{j}_copied"), k)
                    for h in range(H):
                        mm = pe.matmul(bank[4 * j + 1][:, P * h:P * h + P], XT[:, j, h, :], P1[:, j, h, :],
                                       start=True, stop=True)
                    for h in range(H):
                        mm = pe.matmul(bank[4 * j + 2][:, P * h:P * h + P], P1[:, j, h, :], XT[:, j, h, :],
                                       start=True, stop=True)
                    mm.then_inc(S(f"xp{j}_done"), 1)
                gate_multiply(pe, S, E, F, 1, k + 3, 7, k + 8)
            pe.wait_ge(S("x0_ready"), 14)
            pe.wait_ge(S("x1_ready"), 14)
            for j in range(2):
                for i in range(4):
                    mm = pe.transpose(bank[j][:, P * i:P * i + P], y[:, 2 + i, P * j:P * j + P], ident)
                mm.then_inc(S("kvT_done"), 1)
            pe.wait_ge(S("gate_copied"), 15)
            for i in range(6):
                mm = pe.transpose(bank[2 + i // 4][0:N, P * (i % 4):P * (i % 4) + P], y[:, i, NP_TOK:T], ident)
            mm.then_inc(S("sT_done"), 1)
            gate_multiply(pe, S, E, F, 0, 5, 6)
            pe.wait_ge(S("gs_ready"), 4)
            for h in range(H):
                mm = pe.matmul(bank[7][:, 0:GS], C("selg", H, P)[0:N, h, :], gs[:, h, :], start=h == 0,
                               stop=h == H - 1)
            mm.then_inc(S("rs_done"), 1)
            pe.wait_ge(S("kv_ready"), 2)
            pe.wait_ge(S("gate_copied"), GDN_TILES)
            pe.wait_ge(S("qg_ready"), 8)
            for j in range(2):
                c = slice(P * j, P * j + P)
                pe.wait_ge(S("state_ready"), 4 * j) if j else pe.wait_ge(S("state_zeroed"), 1)
                for h in range(H):
                    o, a = HD * (h % 2), h // 2
                    mm = pe.matmul(bank[h % 2][:, HD * a:HD * a + HD], y[o:o + HD, 2 + a, c], ST[o:o + HD, a, :],
                                   start=True, stop=True)
                mm.then_inc(S("kS_done"), 1)
                if j:
                    pe.wait_ge(S("o_read"), 2)
                for h in range(H):
                    o, a = HD * (h % 2), h // 2
                    mm = pe.matmul(bank[3 + h % 2][o:o + HD, P * a:P * a + P], ST[o:o + HD, a, :], qg[o:o + HD, a, c],
                                   start=True, stop=True)
                pe.wait_ge(S("R_ready"), j + 1)
                for h in range(H):
                    mm = pe.matmul(bank[2][:, HD * h:HD * h + HD], XT[:, j, h, :], Rr[:, j, h, :], start=True,
                                   stop=True)
                mm.then_inc(S("u_done"), 1)
                pe.wait_ge(S("u_ready"), 2 * j + 1)
                for h in range(H):
                    o, a = HD * (h % 2), h // 2
                    mm = pe.matmul(bank[5][o:o + HD, P * a:P * a + P], u[:, 0, h, :], PT[:, j, h, :], start=True,
                                   stop=True)
                mm.then_inc(S("o_done"), 1)
                pe.wait_ge(S("u_ready"), 2 * j + 2)
                for h in range(H):
                    o, a = HD * (h % 2), h // 2
                    mm = pe.matmul(bank[6][o:o + HD, HD * a:HD * a + HD], kv[:, j, HD * h:HD * h + HD],
                                   u[:, 1, h, :], start=True, stop=True)
                mm.then_inc(S("ku_done"), 1)
            pe.wait_ge(S("oX_ready"), 1)
            for t in range(2):
                mm = pe.matmul(bank[7][:, N * t:N * t + N], oX[:, 8 * t:8 * t + 8, :].rearrange("p a b -> p (a b)"),
                               C("seln"), start=True, stop=True)
            mm.then_inc(S("os_done"), 1)
            pe.wait_ge(S("osq_ready"), 1)
            pe.wait_ge(S("R_ready"), 2)
            for t in range(2):
                mm = pe.matmul(bank[t][:, 0:T], C("blk"), osq[:, t, :], start=True, stop=True)
            mm.then_inc(S("oss_done"), 1)

        @ph.b.scalar
        def _(act):
            eps = E["epsc"][:]
            def gates(*tiles):
                for r in tiles:
                    gate_copy(nc, act, S, E, F, r, 6 + r % 2)

            gates(0, 1, 2)
            act.wait_ge(S("conv_ready"), 1)
            nc.scalar.activation(y[:], y[:], ACT.Silu).then_inc(S("silu_done"), 1)
            nc.scalar.activation(zg[:], zT[:, FM_ZG:FM_ZG + 2, :], ACT.Silu)
            gates(3)
            act.wait_ge(S("ss_done"), 1)
            for t in range(4):
                nc.scalar.activation(sq[:, t, :], bank[t][:, 0:T], ACT.Sqrt, bias=eps).then_inc(S("roots_taken"), 1)
            gates(4)
            act.wait_ge(S("neg_ready"), 2)
            nc.scalar.activation(e1[:], e1[:], ACT.Exp, scale=-1.0).then_inc(S("e1_done"), 1)
            nc.scalar.activation(alog[:], R("a_log"), ACT.Exp).then_inc(S("e1_done"), 1)
            act.wait_ge(S("one_plus_ready"), 2)
            nc.scalar.activation(sp1[:, 1], sp1[:, 0], ACT.Ln).then_inc(S("ln_done"), 1)
            gates(5, 6, 7)
            for j in range(2):
                act.wait_ge(S("rows_done"), j + 1)
                nc.scalar.activation(EG[:, j].rearrange("p h t -> p (h t)"), bank[4 * j][:], ACT.Exp)\
                    .then_inc(S("EG_done"), 1)
                nc.scalar.copy(bB[:, j].rearrange("p h t -> p (h t)"), bank[4 * j + 1][:]).then_inc(S("bB_done"), 1)
                act.wait_ge(S("D_shifted"), j + 1)
                nc.scalar.activation(D[:, j], D[:, j], ACT.Exp).then_inc(S("D_done"), 1)
            gate_copy(nc, act, S, E, F, 8, 3)
            act.wait_ge(S("wG_shifted"), 2)
            nc.scalar.activation(wG[:, 2], wG[:, 2], ACT.Exp).then_inc(S("wG_done"), 1)
            nc.scalar.activation(wG[:, 0], G[:], ACT.Exp).then_inc(S("wG_done"), 1)
            nc.scalar.activation(e1[:, 1], gb[:, 1], ACT.Exp).then_inc(S("wG_done"), 1)
            with act.Fori(1, 7) as k:
                for j in range(2):
                    act.wait_ge(S(f"p1{j}_done"), k + 1)
                    nc.scalar.copy(P1[:, j].rearrange("p h t -> p (h t)"), bank[4 * j][:])\
                        .then_inc(S(f"p1{j}_copied"), 1)
                gate_copy(nc, act, S, E, F, k + 8, 7)
            for j in range(2):
                act.wait_ge(S("kvT_done"), j + 1)
                nc.scalar.copy(kv[:, j], bank[j][:]).then_inc(S("kv_ready"), 1)
            gate_copy(nc, act, S, E, F, 15, 6)
            act.wait_ge(S("oss_done"), 1)
            for t in range(2):
                nc.scalar.activation(osq[:, t, :], bank[t][:, 0:T], ACT.Sqrt, bias=eps, scale=1.0 / HD)\
                    .then_inc(S("oroot_ready"), 1)

        @ph.b.vector
        def _(dve):
            step = E["stepper"](ph, dve, "dve_step")
            v = nc.vector
            tt, ts, stt, red = v.tensor_tensor, v.tensor_scalar, v.scalar_tensor_tensor, v.tensor_reduce
            for t in range(6):
                step(ts(y[:, t, :], raw[:, t, :], V("conv", 18 + t), None, ALU.mult), wait=t == 5)
            for i in range(1, 4):
                for t in range(6):
                    step(stt(y[:, t, i:NP_TOK], raw[:, t, 0:NP_TOK - i], V("conv", 6 * (3 - i) + t),
                             y[:, t, i:NP_TOK], ALU.mult, ALU.add), wait=t == 5)
            dve.wait_ge(S("buf_loaded"), 16)
            for i in range(3):
                for t in range(6):
                    last = stt(y[:, t, NP_TOK:T], buf[:, t, i, :], V("conv", 6 * i + t), y[:, t, NP_TOK:T], ALU.mult,
                               ALU.add)
                    if i == 2 and t == 5:
                        step(last, "conv_ready", wait=False)
                    else:
                        step(last, wait=t == 5)
            dve.wait_ge(S("silu_done"), 1)
            step(tt(sq[:], y[:, 0:4, :], y[:, 0:4, :], ALU.mult), "sq_ready", wait=False)
            step(v.tensor_copy(e1[:, 0], tm[:, :, TM_BETA:TM_BETA + H]), "neg_ready")
            step(tt(gb[:, 1], tm[:, :, TM_ALPHA:TM_ALPHA + H], R("dt").unsqueeze(1).to_broadcast([P, 3, H]), ALU.add))
            step(ts(sp1[:, 0], gb[:, 1], -1.0, None, ALU.mult))
            step(tt(e1[:, 1], gb[:, 1], sp1[:, 0], ALU.max), "neg_ready")
            dve.wait_ge(S("roots_taken"), 4)
            step(v.reciprocal(sq[:], sq[:]))
            step(stt(y[:, 0:2, :], y[:, 0:2, :], HD ** -0.5, sq[:, 0:2, :], ALU.mult, ALU.mult), "qk_ready",
                 wait=False)
            step(tt(y[:, 2:4, :], y[:, 2:4, :], sq[:, 2:4, :], ALU.mult), "qk_ready")
            dve.wait_ge(S("e1_done"), 2)
            step(ts(sp1[:, 0], e1[:, 1], 1.0, None, ALU.add), "one_plus_ready")
            step(ts(gb[:, 0], e1[:, 0], 1.0, None, ALU.add), "one_plus_ready")
            step(v.reciprocal(gb[:, 0], gb[:, 0]), "gb_ready")
            step(ts(sp1[:, 2], sp1[:, 0], -1.0, None, ALU.add))
            dve.wait_ge(S("ln_done"), 1)
            step(ts(sp1[:, 0], sp1[:, 2], 1e-30, None, ALU.max))
            step(v.reciprocal(sp1[:, 0], sp1[:, 0]))
            step(tt(sp1[:, 1], sp1[:, 1], sp1[:, 0], ALU.mult))
            step(ts(sp1[:, 2], sp1[:, 2], 0.0, None, ALU.is_equal))
            step(tt(sp1[:, 1], sp1[:, 1], sp1[:, 2], ALU.add))
            step(tt(sp1[:, 1], sp1[:, 1], e1[:, 1], ALU.mult))
            step(stt(gb[:, 1], gb[:, 1], 0.0, sp1[:, 1], ALU.max, ALU.add), "gb_ready")
            step(stt(gb[:, 1], gb[:, 1], -1.0, alog[:].unsqueeze(1).to_broadcast([P, 3, H]), ALU.mult, ALU.mult),
                 "gb_ready")
            for i in range(2):
                for j in range(2):
                    step(v.tensor_copy(rep[:, i, j], gb[:, i, j].unsqueeze(2).to_broadcast([P, H, P])), "rep_ready",
                         wait=False)
            dve.wait_ge(S("G_done"), 1)
            for j in range(2):
                step(v.tensor_copy(G[:, j], bank[4 + j][:, 0:H]), "G_ready")
            for j in range(2):
                dve.wait_ge(S("rows_done"), j + 1)
                g4 = bank[4 * j][:].rearrange("p (h t) -> p h t", h=H)
                dve.wait_ge(S("EG_done"), j + 1)
                step(tt(D[:, j], g4, G[:, j].unsqueeze(2).to_broadcast([P, H, P]), ALU.subtract))
                step(tt(wG[:, 2, j], g4[:, :, P - 1], G[:, j], ALU.subtract), "wG_shifted")
                step(ts(D[:, j], D[:, j], 0.0, None, ALU.min), "D_shifted", wait=False)
                dve.wait_ge(S("D_done"), j + 1)
                step(tt(D[:, j], D[:, j], C("tri").unsqueeze(1).to_broadcast([P, H, P]), ALU.mult))
                dve.wait_ge(S("bB_done"), j + 1)
                dve.wait_ge(S("kq_done"), 4 * j + 4)
                for par in range(2):
                    kq = bank[4 * j + 2 + par][:].rearrange("p (i a t) -> p i a t", i=2, a=2)
                    step(tt(by_parity(AT[:, j], par), kq[:, 0], by_parity(D[:, j], par), ALU.mult), "kq_read")
                    step(tt(by_parity(PT[:, j], par), kq[:, 1], by_parity(D[:, j], par), ALU.mult), "kq_read")
                step(tt(AT[:, j], AT[:, j], bB[:, j], ALU.mult))
                step(tt(MT[:, j], AT[:, j], C("lev", 7, P)[:, 0:1].to_broadcast([P, H, P]), ALU.mult),
                     f"mt{j}_ready")
            eye = ident.unsqueeze(1).to_broadcast([P, H, P])
            for j in range(2):
                step(tt(XT[:, j], eye, MT[:, j], ALU.subtract), f"x{j}_ready", wait=False)
                dve.wait_ge(S(f"p1{j}_done"), 1)
                step(tt(X[:, j], eye, bank[4 * j][:].rearrange("p (h t) -> p h t", h=H), ALU.subtract),
                     f"x{j}_ready", wait=False)
            with dve.Fori(1, 7) as k:
                for j in range(2):
                    dve.wait_ge(S(f"p1{j}_done"), k)
                    dve.wait_ge(S(f"x{j}_ready"), 2 * k)
                    tt(MT[:, j], AT[:, j], C("lev", 7, P)[:, bass.ds(k, 1)].to_broadcast([P, H, P]), ALU.mult)\
                        .then_inc(S(f"mt{j}_ready"), 1)
                for j in range(2):
                    dve.wait_ge(S(f"xp{j}_done"), k)
                    tt(X[:, j].rearrange("p h t -> p (h t)"), X[:, j].rearrange("p h t -> p (h t)"),
                       bank[4 * j + 1][:], ALU.subtract).then_inc(S(f"x{j}_ready"), 1)
                    tt(XT[:, j].rearrange("p h t -> p (h t)"), XT[:, j].rearrange("p h t -> p (h t)"),
                       bank[4 * j + 2][:], ALU.subtract).then_inc(S(f"x{j}_ready"), 1)
            dve.wait_ge(S("wG_done"), 3)
            step(tt(wG[:, 1], wG[:, 0], gb[:, 0, 0:2], ALU.mult))
            for j in range(2):
                for h in range(H):
                    o, a = HD * (h % 2), h // 2
                    c = slice(P * j, P * j + P)
                    step(tt(qg[o:o + HD, a, c], y[o:o + HD, a, c], EG[o:o + HD, j, h, :], ALU.mult), "qg_ready",
                         wait=False)
            step(v.memset(ST[:], 0.0), "state_zeroed")
            dve.wait_ge(S("sT_done"), 1)
            step(v.tensor_copy(gs[:, :, 0:2 * HD].rearrange("p h (s e) -> p h s e", s=2),
                               bank[2][0:N, :].rearrange("p (s h e) -> p h s e", s=2, h=H)), "gs_ready")
            step(v.tensor_copy(gs[:, :, 2 * HD:3 * HD], bank[3][0:N, 0:256].rearrange("p (h e) -> p h e", h=H)),
                 "gs_ready")
            step(v.tensor_copy(gs[:, :, 3 * HD], gb[0:N, 0, 2, :]), "gs_ready")
            step(v.tensor_copy(gs[:, :, 3 * HD + 1], e1[0:N, 1, 2, :]), "gs_ready")
            qv, kvec, beta, eg = rs[:, 0:HD], rs[:, HD:2 * HD], rs[:, 3 * HD:3 * HD + 1], rs[:, 3 * HD + 1:GS]
            wide = [P, 16, HD]

            def decode_values():
                dve.wait_ge(S("rs_done"), 1)
                step(v.tensor_copy(rs[:], bank[7][:, 0:GS]))
                step(tt(v16[:], rs[:, 2 * HD:3 * HD].rearrange("p (a b) -> p a b", a=4),
                        C("mv").unsqueeze(2).to_broadcast([P, 4, 16]), ALU.mult))
                step(red(oX[:, 0, :], v16[:].rearrange("p a b -> p b a"), AX.X, ALU.add))
                dve.wait_ge(S("state_loaded"), 16)
                step(tt(pr[:], st[:], kvec.unsqueeze(1).to_broadcast(wide), ALU.mult))

            def decode_new_value():
                step(red(v16[:, 1, :], pr[:], AX.X, ALU.add))
                step(ts(v16[:, 0, :], v16[:, 0, :], eg, beta, ALU.mult, ALU.mult))
                step(stt(v16[:, 2, :], oX[:, 0, :], beta, v16[:, 0, :], ALU.mult, ALU.subtract))

            def decode_output():
                step(tt(pr[:, 0, :], qv, kvec, ALU.mult))
                step(red(sc1[:, 0:1], pr[:, 0, :], AX.X, ALU.add))
                step(ts(v16[:, 1, :], v16[:, 1, :], eg, None, ALU.mult))
                step(stt(v16[:, 3, :], v16[:, 2, :], sc1[:, 0:1], v16[:, 1, :], ALU.mult, ALU.add))
                step(tt(oX[:], C("m16").unsqueeze(2).to_broadcast([P, 16, 16]),
                        v16[:, 3, :].unsqueeze(1).to_broadcast([P, 16, 16]), ALU.mult), "oX_ready")

            for j in range(2):
                dve.wait_ge(S("kv_ready"), j + 1)
                step(tt(Rr[:, j], kv[:, j, 256:512].rearrange("p (h e) -> p h e", h=H),
                        gb[:, 0, j].unsqueeze(2).to_broadcast([P, H, HD]), ALU.mult))
                if j:
                    step(tt(pr[:], st[:], qv.unsqueeze(1).to_broadcast(wide), ALU.mult))
                dve.wait_ge(S("kS_done"), j + 1)
                for par in range(2):
                    w = wG[:, 1, j].rearrange("p (a b) -> p b a", b=2)[:, par].unsqueeze(2).to_broadcast([P, 2, HD])
                    step(tt(by_parity(u[:, 1], par), bank[par][:, 0:P].rearrange("p (a e) -> p a e", a=2), w,
                            ALU.mult))
                step(tt(Rr[:, j], Rr[:, j], u[:, 1], ALU.subtract), "R_ready", wait=False)
                decode_new_value() if j else decode_values()
                dve.wait_ge(S("u_done"), j + 1)
                u4 = bank[2][:, 0:H * HD].rearrange("p (h e) -> p h e", h=H)
                step(v.tensor_copy(u[:, 0], u4), "u_ready", wait=False)
                step(tt(u[:, 1], u4, wG[:, 2, j].unsqueeze(2).to_broadcast([P, H, HD]), ALU.mult), "u_ready",
                     wait=False)
                if j:
                    decode_output()
                else:
                    step(red(v16[:, 0, :], pr[:], AX.X, ALU.add))
                dve.wait_ge(S("o_done"), j + 1)
                for par in range(2):
                    o = HD * par
                    p4 = bank[3 + par][o:o + HD, 0:256].rearrange("p (a t) -> p a t", a=2)
                    step(v.tensor_copy(oT[o:o + HD, :, P * j:P * j + P], p4))
                    step(tt(oT[o:o + HD, :, P * j:P * j + P], oT[o:o + HD, :, P * j:P * j + P],
                            bank[5][o:o + HD, 0:256].rearrange("p (a t) -> p a t", a=2), ALU.add), "o_read")
                dve.wait_ge(S("ku_done"), j + 1)
                for h in range(H):
                    o, a = HD * (h % 2), h // 2
                    step(stt(ST[o:o + HD, a, :], ST[o:o + HD, a, :], EG[o:o + HD, j, h, P - 1:P],
                             bank[6][o:o + HD, HD * a:HD * a + HD], ALU.mult, ALU.add), "state_ready")
            dve.wait_ge(S("os_done"), 1)
            step(v.tensor_copy(oT[:, :, NP_TOK:T], bank[7][:, 0:2 * N].rearrange("p (t n) -> p t n", t=2)))
            step(tt(osq[:], oT[:], oT[:], ALU.mult), "osq_ready")
            step(stt(oT[:], oT[:], V("gdn_g"), zg[:], ALU.mult, ALU.mult))
            step(tt(pr[:], v16[:, 2, :].unsqueeze(2).to_broadcast(wide), kvec.unsqueeze(1).to_broadcast(wide),
                    ALU.mult))
            step(stt(st[:].rearrange("p a b -> p (a b)"), st[:].rearrange("p a b -> p (a b)"), eg,
                     pr[:].rearrange("p a b -> p (a b)"), ALU.mult, ALU.add), "state_s_ready", wait=False)
            dve.wait_ge(S("oroot_ready"), 2)
            step(v.reciprocal(osq[:], osq[:]))
            step(tt(brT[:, 4:6, :], oT[:], osq[:], ALU.mult))


def mix(nc, A, E, l, F):
    xT, brT, bank = (E[k] for k in ("xT", "brT", "bank"))
    g0, gT = F["g0"], F["gT"]
    with E["Phase"]("mix") as ph:
        S = ph.sem
        w = F["wbr"]
        wo = [ph.sb(f"wo{i}", [P, KT, P]) for i in range(4)]
        mixT = ph.sb("mixT", [P, KT, T])

        def gates(dt, b, n):
            first = 4 * dt + b
            if isinstance(dt, int):
                return (g0 if first < MLA_TILES else gT)[:, first % MLA_TILES:first % MLA_TILES + n, :]
            return gT[:, bass.ds(first - MLA_TILES, n), :]

        @ph.b.sync
        def _(sp):
            for i in range(4):
                sp.dma_start(wo[i][:], A["w_out"][l, i]).then_inc(S(f"wo{i}_loaded"), 16)
            with sp.Fori(1, KT // 2) as i:
                for s in range(2):
                    src = A["w_br"][l, 2 * i + s]
                    sp.wait_ge(S(f"p{s}_done"), 4 * i)
                    sp.dma_start(w[s][:], src).then_inc(S(f"w{s}_loaded"), 16)
            for i in range(4):
                sp.wait_ge(S("o_done"), i + 1)
                sp.dma_start(wo[i][:], A["w_out"][l, 4 + i]).then_inc(S(f"wo{i}_loaded"), 16)

        @ph.b.tensor
        def _(pe):
            def pair(i):
                for s in range(2):
                    if not isinstance(i, int):
                        pe.wait_ge(S(f"w{s}_loaded"), 16 * i)
                        pe.wait_ge(S(f"p{s}_read"), 4 * i)
                    for b in range(4):
                        for k in range(2):
                            mm = pe.matmul(bank[4 * s + b][:, 0:T], w[s][:, 2 * b + k, :], brT[:, 2 * b + k, :],
                                           start=k == 0, stop=k == 1)
                        mm.then_inc(S(f"p{s}_done"), 1)

            pair(0)
            with pe.Fori(1, KT // 2) as i:
                pair(i)
            pe.wait_ge(S("mix_ready"), KT)
            for dt in range(KT):
                i = dt % 4
                pe.wait_ge(S(f"wo{i}_loaded"), 16 * (dt // 4) + 16)
                if dt >= 4:
                    pe.wait_ge(S("x_ready"), dt - 3)
                for k in range(KT):
                    mm = pe.matmul(bank[i][:, 0:T], wo[i][:, k, :], mixT[:, k, :], start=k == 0, stop=k == KT - 1)
                mm.then_inc(S("o_done"), 1)

        @ph.b.scalar
        def _(act):
            def sigmoid(dt):
                nc.scalar.activation(gates(dt, 0, 4), gates(dt, 0, 4), ACT.Sigmoid).then_inc(S("gates_ready"), 1)

            sigmoid(0)
            sigmoid(1)
            with act.Fori(2, KT) as dt:
                sigmoid(dt)

        @ph.b.vector
        def _(dve):
            tt = nc.vector.tensor_tensor

            def pair(i):
                for s in range(2):
                    dt = 2 * i + s
                    dve.wait_ge(S("gates_ready"), dt + 1)
                    for b in range(4):
                        g = gates(dt, b, 1).squeeze(1)
                        dve.wait_ge(S(f"p{s}_done"), 4 * i + b + 1)
                        tt(g, g, bank[4 * s + b][:, 0:T], ALU.mult).then_inc(S(f"p{s}_read"), 1)
                    dve.wait_ge(S(f"p{s}_read"), 4 * i + 4)
                    lo, hi = gates(dt, 0, 2), gates(dt, 2, 2)
                    tt(lo, lo, hi, ALU.add).then_inc(S("halved"), 1)
                    dve.wait_ge(S("halved"), dt + 1)
                    a, b = (gates(dt, x, 1).squeeze(1) for x in range(2))
                    out = mixT[:, dt, :] if isinstance(dt, int) else mixT[:, bass.ds(dt, 1), :].squeeze(1)
                    tt(out, a, b, ALU.add).then_inc(S("mix_ready"), 1)

            pair(0)
            with dve.Fori(1, KT // 2) as i:
                pair(i)
            for dt in range(KT):
                dve.wait_ge(S("o_done"), dt + 1)
                tt(xT[:, dt, :], xT[:, dt, :], bank[dt % 4][:, 0:T], ALU.add).then_inc(S("x_ready"), 1)


def branches(nc, A, E, l):
    with ExitStack() as shared:
        sb = lambda name, shape: E["alloc"](shared, name, shape, F32)
        g0 = sb("g0", [P, MLA_TILES, T])
        F = dict(g0=g0, wf=[sb(f"wf{i}", [P, KT, P]) for i in range(2)])
        project(nc, A, E, l, F)
        mla(nc, A, E, l, dict(F, gT=g0, at=0))
        F.update(gT=sb("gT", [P, GATE_TILES - MLA_TILES, T]), memT=sb("memT", [P, KT, MEM]))
        gdn(nc, A, E, l, dict(F, at=0))
        F.update(wbr=[sb(f"wbr{i}", [P, 8, P]) for i in range(2)])
        memory(nc, A, E, l, dict(F, at=GDN_TILES))
        mix(nc, A, E, l, F)


def route(nc, A, E, l, M):
    xT, hT, ones, bank, C, V, R = (E[k] for k in ("xT", "hT", "ones", "bank", "C", "V", "R"))
    with E["Phase"]("route") as ph:
        S = ph.sem
        sq = ph.sb("sq", [P, KT, T])
        rstd = ph.sb("rstd", [P, T])
        wrt = ph.sb("wrt", [P, KT, 36])
        lg = ph.sb("lg", [P, 3, 36])
        m = ph.sb("m", [P, 8, 3])
        eg = ph.sb("eg", [P, 3, 4])
        ohg = ph.sb("ohg", [P, 3, 4])
        sel = ph.sb("sel", [P, 3, 4, 8])
        le = ph.sb("le", [P, 3, 8])
        oh = [ph.sb(f"oh{i}", [P, 3, 8]) for i in range(2)]
        OH = [ph.sb(f"OH{i}", [P, 3, NE]) for i in range(2)]
        both = ph.sb("both", [P, 3, NE])
        rank = ph.sb("rank", [P, 3, NE])
        tok = ph.sb("tok", [P, 3, 4])
        tokT = ph.sb("tokT", [4, T])
        selr = ph.sb("selr", [4, 4, P])
        ncnt = ph.sb("ncnt", [NE, 8])
        nrep = ph.sb("nrep", [NE, P])
        blk = ph.sb("blk", [NE, 1])
        jj = ph.sb("jj", [NE, ITEMS])
        table = ph.sb("table", [NE, 2, ITEMS])
        hTM = ph.sb("hTM", [P, 3, D_MODEL])
        G = ph.sb("G", [P, 3, SLOTS])
        HS, rows, items = M["HS"], M["rows"], M["items"]

        @ph.b.sync
        def _(sp):
            sp.dma_start(wrt[:], A["w_rt"][l]).then_inc(S("wrt_loaded"), 16)
            sp.wait_ge(S("wrt_loaded"), 16)
            sp.wait_ge(S("items_ready"), 1)
            for what in ("gu", "d"):
                for s in range(2):
                    load_expert(sp, M, s, load_sources(sp, A, l, M, s, what), S("first_loaded"))
            sp.wait_ge(S("first_loaded"), 2 * 3 * 16)

        @ph.b.tensor
        def _(pe):
            ident = C("ident")
            for k in range(KT):
                pe.wait_ge(S("sq_ready"), 1 + 2 * k // KT)
                mm = pe.matmul(bank[0][:, 0:T], ones[:], sq[:, k, :], start=k == 0, stop=k == KT - 1)
            mm.then_inc(S("ss_done"), 1)
            pe.wait_ge(S("wrt_loaded"), 16)
            for c, (t0, n) in enumerate(CHUNKS):
                for k in range(KT):
                    if c == 0:
                        pe.wait_ge(S("h_ready"), k + 1)
                    mm = pe.matmul(bank[1 + c][0:n, 0:36], hT[:, k, t0:t0 + n], wrt[:, k, :], start=k == 0,
                                   stop=k == KT - 1)
                mm.then_inc(S("lg_done"), 1)
            for c, (t0, n) in enumerate(CHUNKS):
                for i in range(2):
                    b = 2 * c + i
                    if b >= 4:
                        pe.wait_ge(S("hTM_ready"), b - 3)
                    for k in range(4):
                        mm = pe.transpose(bank[4 + b % 4][0:n, P * k:P * k + P], hT[:, 4 * i + k, t0:t0 + n], ident)
                    mm.then_inc(S("hTM_done"), 1)
            pe.wait_ge(S("both_ready"), 1)
            for c in range(3):
                for b in range(c + 1):
                    mm = pe.matmul(bank[0][:, NE * c:NE * c + NE], C("stri") if b == c else ones[:], both[:, b, :],
                                   start=b == 0, stop=b == c)
            mm.then_inc(S("rank_done"), 1)
            for c in range(3):
                mm = pe.matmul(bank[1][0:NE, 0:1], both[:, c, :], ones[:, 0:1], start=c == 0, stop=c == 2)
            mm.then_inc(S("count_done"), 1)
            pe.wait_ge(S("count_ready"), 2)
            pe.matmul(bank[2][:, 0:NE], nrep[:], C("stri")[0:NE, 0:NE], start=True, stop=True)\
                .then_inc(S("off_done"), 1)
            pe.matmul(bank[3][0:NE, 0:2], C("stri")[0:NE, 0:NE], ncnt[:, 0:2], start=True, stop=True)
            pe.matmul(bank[3][0:NE, 2:4], ones[0:NE, 0:NE], ncnt[:, 0:2], start=True, stop=True)\
                .then_inc(S("off_done"), 1)
            pe.wait_ge(S("table_ready"), 1)
            pe.matmul(bank[1][:, 0:2 * ITEMS], ones[0:NE, :], table[:].rearrange("p a b -> p (a b)"), start=True,
                      stop=True).then_inc(S("items_done"), 1)
            pe.wait_ge(S("tok_ready"), 4)
            for c, (t0, n) in enumerate(CHUNKS):
                mm = pe.transpose(bank[2][0:4, t0:t0 + n], tok[0:n, c, :], ident[0:n, 0:n])
            mm.then_inc(S("tokT_done"), 1)
            pe.wait_ge(S("G_ready"), 3)
            pe.wait_ge(S("hTM_ready"), 6)
            for b in range(2 * KT):
                k, half = b // 2, b % 2
                if b >= 4:
                    pe.wait_ge(S("HS_ready"), b - 3)
                for c, (t0, n) in enumerate(CHUNKS):
                    mm = pe.matmul(bank[4 + b % 4][:, 0:T], hTM[0:n, c, P * k:P * k + P],
                                   G[0:n, c, T * half:T * half + T], start=c == 0, stop=c == 2)
                mm.then_inc(S("HS_done"), 1)
            pe.wait_ge(S("tokT_ready"), 1)
            for r in range(4):
                mm = pe.matmul(bank[r][:, 0:T], selr[:, r, :], tokT[:], start=True, stop=True)
            mm.then_inc(S("rows_done"), 1)

        @ph.b.scalar
        def _(act):
            act.wait_ge(S("ss_done"), 1)
            nc.scalar.activation(rstd[:], bank[0][:, 0:T], ACT.Sqrt, bias=E["epsc"][:], scale=1.0 / D_MODEL)\
                .then_inc(S("root_ready"), 1)
            for c, (t0, n) in enumerate(CHUNKS):
                for i in range(2):
                    b = 2 * c + i
                    act.wait_ge(S("hTM_done"), b + 1)
                    nc.scalar.copy(hTM[0:n, c, 512 * i:512 * i + 512], bank[4 + b % 4][0:n, :])\
                        .then_inc(S("hTM_ready"), 1)
            act.wait_ge(S("eg_shifted"), 1)
            nc.scalar.activation(eg[:], eg[:], ACT.Exp).then_inc(S("exp_done"), 1)
            act.wait_ge(S("p2_shifted"), 1)
            nc.scalar.activation(m[:, 5], m[:, 5], ACT.Exp).then_inc(S("exp_done"), 1)
            for b in range(2 * KT):
                k, half = b // 2, b % 2
                act.wait_ge(S("HS_done"), b + 1)
                nc.scalar.copy(HS[:, k, T * half:T * half + T], bank[4 + b % 4][:, 0:T]).then_inc(S("HS_ready"), 1)
            act.wait_ge(S("rows_done"), 1)
            for r in range(4):
                nc.scalar.copy(rows[:, r, :], bank[r][:, 0:T]).then_inc(S("rows_ready"), 1)

        @ph.b.vector
        def _(dve):
            step = E["stepper"](ph, dve, "dve_step")
            v = nc.vector
            tt, ts, stt, red = v.tensor_tensor, v.tensor_scalar, v.scalar_tensor_tensor, v.tensor_reduce
            for i in range(2):
                ks = slice(KT // 2 * i, KT // 2 * i + KT // 2)
                step(tt(sq[:, ks], xT[:, ks], xT[:, ks], ALU.mult), "sq_ready", wait=False)
            step(v.memset(lg[:], 0.0))
            step(v.memset(HS[:, :, SLOTS:SLOTS + W], 0.0), wait=False)
            step(v.tensor_copy(selr[:], C("ident")[0:4, 0:4].unsqueeze(2).to_broadcast([4, 4, P])), wait=False)
            dve.wait_ge(S("root_ready"), 1)
            step(v.reciprocal(rstd[:], rstd[:]))
            for k in range(KT):
                step(stt(hT[:, k, :], xT[:, k, :], V("g2", k), rstd[:], ALU.mult, ALU.mult), "h_ready", wait=False)
            for c, (t0, n) in enumerate(CHUNKS):
                dve.wait_ge(S("lg_done"), c + 1)
                step(tt(lg[0:n, c, :], bank[1 + c][0:n, 0:36], R("moe_b")[0:n], ALU.add))

            def first_max(onehot, x, top, at, n):
                wide = [P, 3, n]
                step(red(top, x, AX.X, ALU.max))
                step(tt(onehot, x, top.unsqueeze(2).to_broadcast(wide), ALU.is_equal))
                step(tt(onehot, onehot, C("rev")[:, 0:n].unsqueeze(1).to_broadcast(wide), ALU.mult))
                step(red(at, onehot, AX.X, ALU.max))
                step(tt(onehot, onehot, at.unsqueeze(2).to_broadcast(wide), ALU.is_equal))

            lgg = lg[:, :, 0:4]
            first_max(ohg[:], lgg, m[:, 0], m[:, 1], 4)
            step(tt(eg[:], lgg, m[:, 0].unsqueeze(2).to_broadcast([P, 3, 4]), ALU.subtract), "eg_shifted",
                 wait=False)
            step(tt(sel[:], lg[:, :, 4:36].rearrange("p c (g e) -> p c g e", g=4),
                    ohg[:].unsqueeze(3).to_broadcast([P, 3, 4, 8]), ALU.mult))
            step(red(le[:], sel[:].rearrange("p c g e -> p c e g"), AX.X, ALU.add))
            first_max(oh[0][:], le[:], m[:, 2], m[:, 1], 8)
            step(stt(le[:], oh[0][:], NEG, le[:], ALU.mult, ALU.add))
            first_max(oh[1][:], le[:], m[:, 3], m[:, 1], 8)
            step(tt(m[:, 5], m[:, 3], m[:, 2], ALU.subtract), "p2_shifted", wait=False)
            step(tt(ohg[:], ohg[:], C("valid").unsqueeze(2).to_broadcast([P, 3, 4]), ALU.mult))
            for i in range(2):
                for c in range(3):
                    step(tt(OH[i][:, c].rearrange("p (g e) -> p g e", g=4),
                            ohg[:, c].unsqueeze(2).to_broadcast([P, 4, 8]),
                            oh[i][:, c].unsqueeze(1).to_broadcast([P, 4, 8]), ALU.mult), wait=c == 2)
            step(tt(both[:], OH[0][:], OH[1][:], ALU.add), "both_ready")
            dve.wait_ge(S("count_done"), 1)
            step(v.tensor_copy(ncnt[:, 0:1], bank[1][0:NE, 0:1]))
            step(ts(nrep[:], ones[0:NE, :], ncnt[:, 0:1], None, ALU.mult), "count_ready")
            step(ts(ncnt[:, 1:2], ncnt[:, 0:1], 0.0, None, ALU.is_gt))
            for b in range(1, -(-T // W)):
                step(stt(ncnt[:, 1:2], ncnt[:, 0:1], float(b * W), ncnt[:, 1:2], ALU.is_gt, ALU.add),
                     *(["count_ready"] if b == -(-T // W) - 1 else []))
            dve.wait_ge(S("rank_done"), 1)
            dve.wait_ge(S("off_done"), 2)
            step(v.tensor_copy(rank[:], bank[0][:, 0:3 * NE].rearrange("p (c e) -> p c e", c=3)))
            step(tt(rank[:], rank[:], bank[2][:, 0:NE].unsqueeze(1).to_broadcast([P, 3, NE]), ALU.add))
            step(v.tensor_copy(ncnt[:, 2:6], bank[3][0:NE, 0:4]))
            for i in range(2):
                step(tt(OH[i][:], OH[i][:], rank[:], ALU.mult))
                step(red(tok[:, :, i], OH[i][:], AX.X, ALU.add), "tok_ready")
            step(ts(blk[:], ncnt[:, 5:6], -1.0, None, ALU.add))
            step(ts(jj[:], C("iota")[0:NE, 0:ITEMS], blk[:], None, ALU.min))
            step(tt(ncnt[:, 6:7], ncnt[:, 3:4], ncnt[:, 1:2], ALU.add))
            step(ts(table[:, 0], jj[:], ncnt[:, 6:7], None, ALU.is_ge))
            step(ts(table[:, 1], jj[:], ncnt[:, 3:4], None, ALU.is_ge))
            step(tt(table[:, 1], table[:, 1], table[:, 0], ALU.subtract))
            step(ts(jj[:], jj[:], ncnt[:, 3:4], float(W), ALU.subtract, ALU.mult))
            step(stt(table[:, 1], jj[:], ncnt[:, 2:3], table[:, 1], ALU.add, ALU.mult), "table_ready", wait=False)
            dve.wait_ge(S("items_done"), 1)
            step(v.tensor_copy(items[:], bank[1][0:1, 0:2 * ITEMS]), "items_ready", wait=False)
            for c, (t0, n) in enumerate(CHUNKS):
                step(ts(G[:, c], C("iota"), tok[:, c, 0:1], None, ALU.is_equal))
                step(stt(G[:, c], C("iota"), tok[:, c, 1:2], G[:, c], ALU.is_equal, ALU.add), "G_ready")
            dve.wait_ge(S("exp_done"), 2)
            step(red(m[:, 4], eg[:], AX.X, ALU.add))
            step(ts(m[:, 6], m[:, 5], 1.0, None, ALU.add))
            step(tt(m[:, 6], m[:, 6], m[:, 4], ALU.mult))
            step(v.reciprocal(m[:, 6], m[:, 6]))
            step(v.tensor_copy(tok[:, :, 2], m[:, 6]), "tok_ready")
            step(tt(tok[:, :, 3], m[:, 6], m[:, 5], ALU.mult), "tok_ready")
            dve.wait_ge(S("tokT_done"), 1)
            step(v.tensor_copy(tokT[:], bank[2][0:4, 0:T]), "tokT_ready")


def load_sources(sp, A, l, M, j, what):
    e = sp.value_load(M["items"][0:1, bass.ds(j, 1)], min_val=0, max_val=NE - 1)
    return [("wg", A["w_g"][l, e]), ("wu", A["w_u"][l, e])] if what == "gu" else [("wd", A["w_d"][l, e])]


def load_expert(sp, M, s, sources, loaded):
    for name, src in sources:
        sp.dma_start(M[name][s][:], src).then_inc(loaded, 16)


def experts(nc, A, E, l, M):
    bank = E["bank"]
    HS, YS, items = M["HS"], M["YS"], M["items"]
    FT = 2
    PAIRS = ITEMS // 2
    with E["Phase"]("moe") as ph:
        S = ph.sem
        wg, wu, wd, rows, Q = (M[k] for k in ("wg", "wu", "wd", "rows", "Q"))
        tmp = ph.sb("tmp", [P, T])
        hb = [ph.sb(f"hb{s}", [P, KT, W]) for s in range(2)]
        sg = [ph.sb(f"sg{s}", [P, FT * W]) for s in range(2)]

        @ph.b.sync
        def _(sp):
            def load(i, s, what):
                j = 2 * i + s
                src = load_sources(sp, A, l, M, j, what)
                if what == "gu":
                    sp.wait_ge(S("gu_done"), j - 1)
                else:
                    sp.wait_ge(S("y_done"), 2 * j - 2)
                load_expert(sp, M, s, src, S(f"{what}{s}_loaded"))

            load(1, 0, "gu")
            with sp.Fori(1, PAIRS) as i:
                load(i, 1, "gu")
                load(i, 0, "d")
                load(i + 1, 0, "gu")
                load(i, 1, "d")
            load(PAIRS, 0, "d")

        @ph.b.tensor
        def _(pe):
            def gate_up(i, s, first=False):
                j = 2 * i + s
                if not first:
                    pe.wait_ge(S(f"gu{s}_loaded"), 32 * i)
                pe.wait_ge(S("hb_ready"), j + 1)
                if not first:
                    pe.wait_ge(S("act_ready"), j - 1)
                for w, b in ((wg[s], s), (wu[s], 2 + s)):
                    for f in range(FT):
                        for k in range(KT):
                            mm = pe.matmul(bank[b][:, W * f:W * f + W], w[:, k, P * f:P * f + P], hb[s][:, k, :],
                                           start=k == 0, stop=k == KT - 1)
                    mm.then_inc(S("g_done" if b < 2 else "gu_done"), 1)

            def down(i, s, first=False):
                j = 2 * i + s
                if not first:
                    pe.wait_ge(S(f"d{s}_loaded"), 16 * i)
                pe.wait_ge(S("act_ready"), j + 1)
                if not first:
                    pe.wait_ge(S("y_copied"), 2 * j - 2)
                for half in range(2):
                    for dt in range(4):
                        at = P * (4 * half + dt)
                        for f in range(FT):
                            mm = pe.matmul(bank[4 + 2 * s + half][:, W * dt:W * dt + W], wd[s][:, f, at:at + P],
                                           sg[s][:, W * f:W * f + W], start=f == 0, stop=f == FT - 1)
                    mm.then_inc(S("y_done"), 1)

            gate_up(0, 0, first=True)
            gate_up(0, 1, first=True)
            down(0, 0, first=True)
            gate_up(1, 0)
            down(0, 1, first=True)
            with pe.Fori(1, PAIRS) as i:
                gate_up(i, 1)
                down(i, 0)
                gate_up(i + 1, 0)
                down(i, 1)
            down(PAIRS, 0)

        @ph.b.scalar
        def _(act):
            def fetch(i, s, first=False):
                j = 2 * i + s
                at = act.value_load(items[0:1, bass.ds(j + ITEMS, 1)], min_val=0, max_val=SLOTS - 1)
                if not first:
                    act.wait_ge(S("gu_done"), j - 1)
                nc.scalar.copy(hb[s][:], HS[:, :, bass.ds(at, W)]).then_inc(S("hb_ready"), 1)

            def silu(i, s, first=False):
                j = 2 * i + s
                act.wait_ge(S("g_done"), j + 1)
                if not first:
                    act.wait_ge(S("y_done"), 2 * j - 2)
                nc.scalar.activation(sg[s][:], bank[s][:, 0:FT * W], ACT.Silu).then_inc(S("silu_done"), 1)

            fetch(0, 0, first=True)
            fetch(0, 1, first=True)
            silu(0, 0, first=True)
            fetch(1, 0)
            silu(0, 1, first=True)
            fetch(1, 1)
            with act.Fori(1, PAIRS - 1) as i:
                for s in range(2):
                    silu(i, s)
                    fetch(i + 1, s)
            silu(PAIRS - 1, 0)
            fetch(PAIRS, 0)
            silu(PAIRS - 1, 1)
            silu(PAIRS, 0)

        @ph.b.vector
        def _(dve):
            def scatter_weights():
                stt = nc.vector.scalar_tensor_tensor
                for c in range(SCH):
                    at = E["C"]("slot")[:, c:c + 1]
                    stt(Q[:, c], rows[:, 0], at, rows[:, 2], ALU.is_equal, ALU.mult).then_inc(S("q_step"), 1)
                    if c:
                        dve.wait_ge(S("q_step"), 3 * c)
                    stt(tmp[:], rows[:, 1], at, rows[:, 3], ALU.is_equal, ALU.mult).then_inc(S("q_step"), 1)
                    dve.wait_ge(S("q_step"), 3 * c + 2)
                    nc.vector.tensor_tensor(Q[:, c], Q[:, c], tmp[:], ALU.add).then_inc(S("q_step"), 1)

            def product(i, s):
                j = 2 * i + s
                dve.wait_ge(S("gu_done"), j + 1)
                dve.wait_ge(S("silu_done"), j + 1)
                nc.vector.tensor_tensor(sg[s][:], sg[s][:], bank[2 + s][:, 0:FT * W], ALU.mult)\
                    .then_inc(S("act_ready"), 1)

            def store(i, s, first=False):
                j = 2 * i + s
                at = dve.value_load(items[0:1, bass.ds(j + ITEMS, 1)], min_val=0, max_val=SLOTS - 1)
                if not first:
                    dve.wait_ge(S("y_copied"), 2 * j)
                for half in range(2):
                    dve.wait_ge(S("y_done"), 2 * j + half + 1)
                    nc.vector.tensor_copy(YS[:, 4 * half:4 * half + 4, bass.ds(at, W)],
                                          bank[4 + 2 * s + half][:].rearrange("p (a b) -> p a b", a=4))\
                        .then_inc(S("y_copied"), 1)

            product(0, 0)
            scatter_weights()
            product(0, 1)
            store(0, 0, first=True)
            product(1, 0)
            store(0, 1)
            with dve.Fori(1, PAIRS) as i:
                product(i, 1)
                store(i, 0)
                product(i + 1, 0)
                store(i, 1)
            store(PAIRS, 0)


def combine(nc, A, E, l, M):
    xT, bank, C = (E[k] for k in ("xT", "bank", "C"))
    YS, Q = M["YS"], M["Q"]
    slots = [min(P, SLOTS - P * c) for c in range(SCH)]
    with E["Phase"]("comb") as ph:
        S = ph.sem
        yTM = ph.sb("yTM", [P, SCH, D_MODEL])

        @ph.b.tensor
        def _(pe):
            for b in range(2 * SCH):
                c, i = b // 2, b % 2
                if b >= 4:
                    pe.wait_ge(S("y_ready"), b - 3)
                for k in range(4):
                    mm = pe.transpose(bank[b % 4][0:slots[c], P * k:P * k + P],
                                      YS[:, 4 * i + k, P * c:P * c + slots[c]], C("ident"))
                mm.then_inc(S("yT_done"), 1)
            pe.wait_ge(S("y_ready"), 2 * SCH)
            for dt in range(KT):
                if dt >= 4:
                    pe.wait_ge(S("x_ready"), dt - 3)
                for c, n in enumerate(slots):
                    mm = pe.matmul(bank[4 + dt % 4][:, 0:T], yTM[0:n, c, P * dt:P * dt + P], Q[0:n, c, :],
                                   start=c == 0, stop=c == SCH - 1)
                mm.then_inc(S("sum_done"), 1)

        @ph.b.scalar
        def _(act):
            for b in range(2 * SCH):
                c, i = b // 2, b % 2
                act.wait_ge(S("yT_done"), b + 1)
                nc.scalar.copy(yTM[0:slots[c], c, 512 * i:512 * i + 512], bank[b % 4][0:slots[c], :])\
                    .then_inc(S("y_ready"), 1)

        @ph.b.vector
        def _(dve):
            for dt in range(KT):
                dve.wait_ge(S("sum_done"), dt + 1)
                nc.vector.tensor_tensor(xT[:, dt, :], xT[:, dt, :], bank[4 + dt % 4][:, 0:T], ALU.add)\
                    .then_inc(S("x_ready"), 1)


def moe(nc, A, E, l):
    with ExitStack() as shared:
        sb = lambda name, shape, dt=F32: E["alloc"](shared, f"m_{name}", shape, dt)
        M = dict(HS=sb("HS", [P, KT, SLOTS + W]), YS=sb("YS", [P, KT, SLOTS + W]), Q=sb("Q", [P, SCH, T]),
                 items=sb("items", [1, 2 * ITEMS], I32),
                 rows=sb("rows", [P, 4, T]),
                 wg=[sb(f"wg{s}", [P, KT, 256]) for s in range(2)], wu=[sb(f"wu{s}", [P, KT, 256]) for s in range(2)],
                 wd=[sb(f"wd{s}", [P, 2, D_MODEL]) for s in range(2)])
        route(nc, A, E, l, M)
        experts(nc, A, E, l, M)
        combine(nc, A, E, l, M)


PHASES = [branches, moe]

OUTS = dict(
    o_x=(P, KT, T), o_ckv=(DEPTH, P, 3, RANK), o_kr=(DEPTH, P, 3, ROPE), o_gdn=(DEPTH, P, 2, HD),
    o_conv=(DEPTH, P, 6, 3), o_mem=(DEPTH, P, 2, 2, MEM), o_gdns=(DEPTH, P, 16, HD),
    o_convs=(DEPTH, P, 6, 3, NS_TOK), o_gv=(DEPTH, NS_TOK, 256))


def arrange(I):
    f = np.ascontiguousarray
    L = DEPTH
    w_in = I["w_in"].reshape(L, KT, P, -1).transpose(0, 2, 1, 3)
    off = dict(u=0, v=256, cq=512, ckv=768, kr=896, qkv=928, zg=1696, b=1952, alpha=1956, mq=1960, gate=2216)

    def cols(name, n):
        return w_in[..., off[name]:off[name] + n]

    fm = np.concatenate([cols("u", 256), cols("cq", 256), cols("qkv", 768), cols("zg", 256), cols("mq", 256)], -1)
    gate = cols("gate", 4096).reshape(L, P, KT, 4, KT, P)
    part = lambda a, n: a.reshape(L, n, P).transpose(0, 2, 1)
    twice = lambda a: np.concatenate([a, a], -1)[..., None]
    rep = lambda a: np.repeat(a.reshape(L, 2, 2), HD, 2).transpose(0, 2, 1)
    return {
        "xT": f(np.concatenate([I["x_prompt"][0], I["x_sample"][:, 0]]).reshape(T, KT, P).transpose(2, 1, 0)),
        "memT": f(I["mem_prompt"][0].reshape(MEM, KT, P).transpose(2, 1, 0)),
        "cst": constants(),
        "vec": f(np.concatenate([
            part(I["norm1_g"], 8), part(I["mla_cq_g"], 2),
            I["gdn_conv_w"].reshape(L, 4, 6, P).transpose(0, 3, 1, 2).reshape(L, P, 24),
            twice(I["gdn_out_g"]), twice(I["mem_qn_g"]), part(I["mem_norm_g"], 8), part(I["norm2_g"], 8),
            rep(I["gm_ws"][:, :, 0, 0]), rep(I["gm_b"][:, :, 0]), twice(I["mla_kn_g"])], -1)),
        "row": f(np.concatenate([
            I["gm_norm_g"], I["mla_ckv_g"], I["mla_kr_g"], I["mla_qn_g"], I["mla_qr_g"], I["mla_kn_g"],
            I["mem_kn_g"], I["gdn_a_log"], I["gdn_dt_bias"], I["moe_bg"], I["moe_be"]], -1)),
        "w_tm": f(np.concatenate([cols("v", 256), cols("ckv", 128), cols("kr", 32), cols("b", 4),
                                  cols("alpha", 4)], -1)),
        "w_fm": f(fm.reshape(L, P, KT, FM_N, P).transpose(0, 3, 1, 2, 4)),
        "w_gate": f(gate.transpose(0, 4, 3, 1, 2, 5).reshape(L, GATE_TILES, P, KT, P)),
        "w_br": f(I["w_branch"].reshape(L, 8, P, KT, P).transpose(0, 3, 2, 1, 4)),
        "gm_ws": f(I["gm_ws"].transpose(0, 3, 1, 2)),
        "gm_b": f(I["gm_b"].reshape(L, 2, 2, P).transpose(0, 2, 1, 3)),
        "w_uq": f(I["mla_w_uq"].reshape(L, 2, P, H * QK).transpose(0, 2, 1, 3)),
        "w_uk": f(I["mla_w_uk"].reshape(L, P, H * HD)),
        "w_ukT": f(I["mla_w_uk"].transpose(0, 3, 2, 1)),
        "w_uv": f(I["mla_w_uv"].reshape(L, P, H * HD)),
        "ckv": f(I["cache_mla_ckv"].reshape(L * POOL * SUB, -1)),
        "kr": f(I["cache_mla_kr"].reshape(L * POOL * SUB, -1)),
        "pages": f(np.repeat(I["page_table"].T, SUB, 0)),
        "sgdn": f(I["state_gdn"].reshape(L, P, 16, HD)),
        "sconv": f(I["state_conv"].reshape(L, NS_TOK, 3, 6, P).transpose(0, 4, 3, 2, 1)),
        "w_kv": f(I["mem_w_kv"].reshape(L, KT, P, 512).transpose(0, 2, 1, 3)),
        "memkT": f(I["cache_mem_k"].reshape(L, NS_TOK, MEM, 2, P).transpose(0, 4, 1, 3, 2)),
        "memv": f(I["cache_mem_v"].reshape(L, NS_TOK, 2, P, 256).transpose(0, 3, 1, 2, 4)),
        "w_out": f(I["w_out"].reshape(L, KT, P, KT, P).transpose(0, 3, 2, 1, 4)),
        "w_rt": f(np.concatenate([I["moe_wg"], I["moe_we"]], -1).reshape(L, KT, P, 36).transpose(0, 2, 1, 3)),
        "w_g": f(I["moe_w_gate"].reshape(L, 32, KT, P, 256).transpose(0, 1, 3, 2, 4)),
        "w_u": f(I["moe_w_up"].reshape(L, 32, KT, P, 256).transpose(0, 1, 3, 2, 4)),
        "w_d": f(I["moe_w_down"].reshape(L, 32, 2, P, D_MODEL).transpose(0, 1, 3, 2, 4)),
    }


def restore(r):
    L = DEPTH
    x = r["o_x"].transpose(2, 1, 0).reshape(T, D_MODEL)
    prompt = lambda a: a[:, :, 0:2].transpose(0, 2, 1, 3).reshape(L, 1, NP_TOK, -1)
    mem = r["o_mem"].transpose(2, 0, 3, 1, 4).reshape(2, L, 1, MEM, H, HD)
    gdn = r["o_gdn"].reshape(L, 2, HD, 2, HD).transpose(0, 3, 1, 4, 2).reshape(L, 1, H, HD, HD)
    out = (
        x[None, :NP_TOK], x[NP_TOK:, None], prompt(r["o_ckv"]), prompt(r["o_kr"]), gdn,
        r["o_conv"].transpose(0, 3, 2, 1).reshape(L, 1, 3, 768), mem[0], mem[1],
        r["o_ckv"][:, 0:NS_TOK, 2][:, :, None], r["o_kr"][:, 0:NS_TOK, 2][:, :, None],
        r["o_gdns"].reshape(L, NS_TOK, H, HD, HD),
        r["o_convs"].transpose(0, 4, 3, 2, 1).reshape(L, NS_TOK, 3, 768), r["o_gv"][:, :, None])
    return tuple(np.ascontiguousarray(a) for a in out)


def kernel(**inputs):
    import concourse.bacc as bacc
    from concourse.bass_utils import run_bass_kernel_spmd

    nc = bacc.Bacc("TRN2", target_bir_lowering=False, num_devices=1)
    arrays = arrange({k: np.asarray(v) for k, v in inputs.items()})
    A = {n: nc.dram_tensor("in_" + n, a.shape, mybir.dt.from_np(a.dtype), kind="ExternalInput").ap()
         for n, a in arrays.items()}
    for n, shape in OUTS.items():
        A[n] = nc.dram_tensor(n, shape, F32, kind="ExternalOutput").ap()
    build(nc, A)
    return restore(run_bass_kernel_spmd(nc, [{"in_" + n: a for n, a in arrays.items()}], core_ids=[0]).results[0])
```
